# Optimizing a Trainium2 kernel written in Bass

```python
import math
import jax, jax.numpy as jnp
from jax import lax
import numpy as np

D_MODEL = 1024
BATCH = 1
SEQ = 512
DEPTH = 1

D_MIX = D_MODEL
GLA_HEADS = 4
GLA_DV = D_MIX // 2 // GLA_HEADS
GLA_DK = GLA_DV // 2
GLA_LOWRANK = 16
GLA_TAU = 16.0
GLA_CHUNK = 64
SWA_HEADS = 8
SWA_KV_HEADS = 2
SWA_HD = (D_MIX - GLA_HEADS * GLA_DV) // SWA_HEADS
SWA_WINDOW = 128
D_FF = 2816
CONV_K = 3
EPS = 1e-6

GLA_Q = GLA_HEADS * GLA_DK
GLA_K = GLA_HEADS * GLA_DK
GLA_V = GLA_HEADS * GLA_DV
GLA_R = GLA_HEADS * GLA_DV
SWA_Q = SWA_HEADS * SWA_HD
SWA_K = SWA_KV_HEADS * SWA_HD
SWA_V = SWA_KV_HEADS * SWA_HD
SPLITS = (GLA_Q, GLA_K, GLA_V, GLA_R, GLA_LOWRANK, SWA_Q, SWA_K, SWA_V)
P_IN = sum(SPLITS)


def alibi_slopes(n_heads):
    return np.array([2.0 ** (-8.0 * (h + 1) / n_heads) for h in range(n_heads)], dtype=np.float32)

def rms_norm(x, g):
    xf = x.astype(jnp.float32)
    y = xf * lax.rsqrt(jnp.mean(xf * xf, axis=-1, keepdims=True) + EPS)
    return (y * g.astype(jnp.float32)).astype(x.dtype)

def split_cols(z, sizes):
    idx = np.cumsum(sizes)[:-1].tolist()
    return jnp.split(z, idx, axis=-1)

def gla_chunked(q, k, v, log_a):
    B, L, H, dk = q.shape
    dv = v.shape[-1]
    C = GLA_CHUNK
    n = L // C

    def chunk(t):
        return t.astype(jnp.float32).reshape(B, n, C, H, t.shape[-1]).transpose(0, 3, 1, 2, 4)

    q, k, v, log_a = chunk(q), chunk(k), chunk(v), chunk(log_a)
    b = jnp.cumsum(log_a, axis=-2)
    b_last = b[..., -1:, :]
    qe = q * jnp.exp(b)
    ke = k * jnp.exp(-b)
    causal = jnp.tril(jnp.ones((C, C), dtype=bool))
    A = jnp.einsum('bhncd,bhnsd->bhncs', qe, ke)
    A = jnp.where(causal, A, 0.0)
    o_intra = jnp.einsum('bhncs,bhnsv->bhncv', A, v)
    kd = k * jnp.exp(b_last - b)
    chunk_state = jnp.einsum('bhncd,bhncv->bhndv', kd, v)
    decay = jnp.exp(b_last[..., 0, :])

    def step(S, inp):
        dec, cs = inp
        return S * dec[..., None] + cs, S

    S0 = jnp.zeros((B, H, dk, dv), jnp.float32)
    _, S_prev = lax.scan(step, S0, (jnp.moveaxis(decay, 2, 0), jnp.moveaxis(chunk_state, 2, 0)))
    S_prev = jnp.moveaxis(S_prev, 0, 2)
    o_inter = jnp.einsum('bhncd,bhndv->bhncv', qe, S_prev)
    o = o_intra + o_inter
    return o.transpose(0, 2, 3, 1, 4).reshape(B, L, H, dv)

def swa_sink_attention(q, k, v, sinks):
    B, L, Hq, hd = q.shape
    Hkv = k.shape[2]
    G = Hq // Hkv
    W = SWA_WINDOW
    nb = L // W
    qb = q.reshape(B, nb, W, Hkv, G, hd)
    kb = k.reshape(B, nb, W, Hkv, hd)
    vb = v.reshape(B, nb, W, Hkv, hd)
    pad = ((0, 0), (1, 0), (0, 0), (0, 0), (0, 0))
    kk = jnp.concatenate([jnp.pad(kb, pad)[:, :-1], kb], axis=2)
    vv = jnp.concatenate([jnp.pad(vb, pad)[:, :-1], vb], axis=2)
    s = jnp.einsum('bnqkgd,bnskd->bnkgqs', qb, kk,
                   preferred_element_type=jnp.float32) * (1.0 / math.sqrt(hd))
    i = jnp.arange(W)[:, None]
    j = jnp.arange(2 * W)[None, :]
    dist = (W + i - j).astype(jnp.float32)
    key_abs = (jnp.arange(nb)[:, None, None] - 1) * W + j[None]
    mask = (dist >= 0) & (dist < W) & (key_abs >= 0)
    slopes = jnp.asarray(alibi_slopes(Hq)).reshape(Hkv, G)
    s = s - slopes[:, :, None, None] * dist
    s = jnp.where(mask[None, :, None, None], s, -jnp.inf)
    sink = sinks.astype(jnp.float32).reshape(Hkv, G)[None, None, :, :, None, None]
    m = jnp.maximum(jnp.max(s, axis=-1, keepdims=True), sink)
    p = jnp.exp(s - m)
    denom = jnp.sum(p, axis=-1, keepdims=True) + jnp.exp(sink - m)
    p = p / denom
    o = jnp.einsum('bnkgqs,bnskd->bnqkgd', p, vv.astype(jnp.float32))
    return o.reshape(B, L, Hq * hd)

def causal_dwconv(u, w, b):
    K = w.shape[0]
    L = u.shape[1]
    up = jnp.pad(u, ((0, 0), (K - 1, 0), (0, 0)))
    out = up[:, 0:L] * w[0]
    for j in range(1, K):
        out = out + up[:, j:j + L] * w[j]
    return out + b

def hybrid_layer(x, mix_norm, w_in, w_alpha2, b_alpha, gla_norm, q_norm, k_norm, sinks,
                 w_out, ffn_norm, w_up, conv_w, conv_b, w_down):
    B, L, _ = x.shape
    dt = x.dtype
    h = rms_norm(x, mix_norm)
    z = h @ w_in
    gq, gk, gv, gr, glr, sq, sk, sv = split_cols(z, SPLITS)

    log_a = jax.nn.log_sigmoid((glr @ w_alpha2 + b_alpha).astype(jnp.float32)) / GLA_TAU
    gq = gq.reshape(B, L, GLA_HEADS, GLA_DK) * (GLA_DK ** -0.5)
    gk = gk.reshape(B, L, GLA_HEADS, GLA_DK)
    gv = gv.reshape(B, L, GLA_HEADS, GLA_DV)
    o_gla = gla_chunked(gq, gk, gv, log_a.reshape(B, L, GLA_HEADS, GLA_DK))
    o_gla = rms_norm(o_gla, gla_norm).reshape(B, L, GLA_V)
    o_gla = (o_gla * jax.nn.silu(gr.astype(jnp.float32))).astype(dt)

    sq = rms_norm(sq.reshape(B, L, SWA_HEADS, SWA_HD), q_norm)
    sk = rms_norm(sk.reshape(B, L, SWA_KV_HEADS, SWA_HD), k_norm)
    sv = sv.reshape(B, L, SWA_KV_HEADS, SWA_HD)
    o_swa = swa_sink_attention(sq, sk, sv, sinks).astype(dt)

    x = x + jnp.concatenate([o_gla, o_swa], axis=-1) @ w_out

    h2 = rms_norm(x, ffn_norm)
    u = causal_dwconv(h2 @ w_up, conv_w, conv_b)
    a, bval = jnp.split(u, 2, axis=-1)
    return x + (jax.nn.silu(a) * bval) @ w_down

def first_inputs(seed: int = 0) -> dict:
    key = jax.random.key(seed)
    ks = jax.random.split(key, 16)
    f = jnp.float32

    def nrm(k, shape, scale):
        return jax.random.normal(k, shape, f) * scale

    return {
        "x": nrm(ks[0], (BATCH, SEQ, D_MODEL), 1.0),
        "mix_norm": 1.0 + nrm(ks[1], (DEPTH, D_MODEL), 0.02),
        "w_in": nrm(ks[2], (DEPTH, D_MODEL, P_IN), D_MODEL ** -0.5),
        "w_alpha2": nrm(ks[3], (DEPTH, GLA_LOWRANK, GLA_Q), GLA_LOWRANK ** -0.5),
        "b_alpha": nrm(ks[4], (DEPTH, GLA_Q), 0.1),
        "gla_norm": 1.0 + nrm(ks[5], (DEPTH, GLA_DV), 0.02),
        "q_norm": 1.0 + nrm(ks[6], (DEPTH, SWA_HD), 0.02),
        "k_norm": 1.0 + nrm(ks[7], (DEPTH, SWA_HD), 0.02),
        "sinks": nrm(ks[8], (DEPTH, SWA_HEADS), 0.5),
        "w_out": nrm(ks[9], (DEPTH, D_MIX, D_MODEL), (2.0 * D_MIX) ** -0.5),
        "ffn_norm": 1.0 + nrm(ks[10], (DEPTH, D_MODEL), 0.02),
        "w_up": nrm(ks[11], (DEPTH, D_MODEL, 2 * D_FF), D_MODEL ** -0.5),
        "conv_w": nrm(ks[12], (DEPTH, CONV_K, 2 * D_FF), CONV_K ** -0.5),
        "conv_b": nrm(ks[13], (DEPTH, 2 * D_FF), 0.02),
        "w_down": nrm(ks[14], (DEPTH, D_FF, D_MODEL), (2.0 * D_FF) ** -0.5),
    }

def first_block(x, mix_norm, w_in, w_alpha2, b_alpha, gla_norm, q_norm, k_norm, sinks,
              w_out, ffn_norm, w_up, conv_w, conv_b, w_down):
    for l in range(DEPTH):
        x = hybrid_layer(x, mix_norm[l], w_in[l], w_alpha2[l], b_alpha[l], gla_norm[l],
                         q_norm[l], k_norm[l], sinks[l], w_out[l], ffn_norm[l], w_up[l],
                         conv_w[l], conv_b[l], w_down[l])
    return x


DEPTH_2 = 2

CHUNK = 64
Q_BLOCK = 128
N_A_LAYERS = DEPTH_2 // 2
N_B_LAYERS = DEPTH_2 - N_A_LAYERS
CONV_WIDTH = 31
D_FF_2 = 4 * D_MODEL
N_HEADS = 8
QK_NOPE_DIM = 128
QK_ROPE_DIM = 64
QK_HEAD_DIM = QK_NOPE_DIM + QK_ROPE_DIM
V_HEAD_DIM = 128
Q_LORA_RANK = 384
KV_LORA_RANK = 256
ROPE_BASE = 10000.0
RMS_EPS = 1e-6
LN_EPS = 1e-5


def rms_norm_2(x, g):
    xf = x.astype(jnp.float32)
    y = xf * lax.rsqrt(jnp.mean(xf * xf, axis=-1, keepdims=True) + RMS_EPS)
    return (y * g.astype(jnp.float32)).astype(x.dtype)

def layer_norm(x, g, b):
    xf = x.astype(jnp.float32)
    mu = jnp.mean(xf, axis=-1, keepdims=True)
    xc = xf - mu
    var = jnp.mean(xc * xc, axis=-1, keepdims=True)
    y = xc * lax.rsqrt(var + LN_EPS) * g.astype(jnp.float32) + b.astype(jnp.float32)
    return y.astype(x.dtype)

def rope_tables(seq):
    inv = 1.0 / (ROPE_BASE ** (jnp.arange(0, QK_ROPE_DIM, 2, dtype=jnp.float32) / QK_ROPE_DIM))
    pos = jnp.arange(seq, dtype=jnp.float32)
    ang = pos[:, None] * inv[None, :]
    return jnp.cos(ang), jnp.sin(ang)

def apply_rope(x, cos, sin):
    xf = x.astype(jnp.float32)
    half = QK_ROPE_DIM // 2
    x1, x2 = xf[..., :half], xf[..., half:]
    out = jnp.concatenate([x1 * cos - x2 * sin, x1 * sin + x2 * cos], axis=-1)
    return out.astype(x.dtype)

def conformer_conv(h, w_pw1, b_pw1, w_dw, b_dw, ln_g, ln_b, w_pw2, b_pw2):
    u = h @ w_pw1 + b_pw1
    a, gate = jnp.split(u, 2, axis=-1)
    u = a * jax.nn.sigmoid(gate)
    u = jnp.pad(u, ((0, 0), (CONV_WIDTH - 1, 0), (0, 0)))
    u = lax.conv_general_dilated(u, w_dw[:, None, :], window_strides=(1,), padding='VALID',
                                 dimension_numbers=('NWC', 'WIO', 'NWC'),
                                 feature_group_count=D_MODEL) + b_dw
    u = jax.nn.silu(layer_norm(u, ln_g, ln_b))
    return u @ w_pw2 + b_pw2

def squared_relu_mlp(h, w1, w2):
    return jnp.square(jax.nn.relu(h @ w1)) @ w2

def mla_shared_kv(h, kv_in_g, w_dkv, kv_norm_g, w_kr, w_uk, w_uv, cos, sin):
    b, s, _ = h.shape
    hn = rms_norm_2(h, kv_in_g)
    c_kv = rms_norm_2(hn @ w_dkv, kv_norm_g)
    k_rope = apply_rope(hn @ w_kr, cos, sin)
    k_nope = (c_kv @ w_uk).reshape(b, s, N_HEADS, QK_NOPE_DIM)
    v = (c_kv @ w_uv).reshape(b, s, N_HEADS, V_HEAD_DIM)
    return k_nope, k_rope, v

def mla_attention(hn, w_dq, q_norm_g, w_uq, w_o, k_nope, k_rope, v, cos, sin):
    b, s, _ = hn.shape
    q = (rms_norm_2(hn @ w_dq, q_norm_g) @ w_uq).reshape(b, s, N_HEADS, QK_HEAD_DIM)
    q_nope = q[..., :QK_NOPE_DIM]
    q_rope = apply_rope(q[..., QK_NOPE_DIM:], cos[:, None, :], sin[:, None, :])
    scale = QK_HEAD_DIM ** -0.5
    key_chunk = jnp.arange(s) // CHUNK

    def block(i):
        start = i * Q_BLOCK
        qn = lax.dynamic_slice_in_dim(q_nope, start, Q_BLOCK, axis=1)
        qr = lax.dynamic_slice_in_dim(q_rope, start, Q_BLOCK, axis=1)
        sc = (jnp.einsum('bqhd,bkhd->bhqk', qn, k_nope, preferred_element_type=jnp.float32)
              + jnp.einsum('bqhr,bkr->bhqk', qr, k_rope, preferred_element_type=jnp.float32)) * scale
        q_chunk = (start + jnp.arange(Q_BLOCK)) // CHUNK
        mask = key_chunk[None, :] <= q_chunk[:, None]
        sc = jnp.where(mask[None, None], sc, -jnp.inf)
        p = jax.nn.softmax(sc, axis=-1).astype(v.dtype)
        return jnp.einsum('bhqk,bkhd->bqhd', p, v)

    o = lax.map(block, jnp.arange(s // Q_BLOCK))
    o = jnp.transpose(o, (1, 0, 2, 3, 4)).reshape(b, s, N_HEADS * V_HEAD_DIM)
    return o @ w_o

def second_inputs(seed: int = 0) -> dict:
    key = jax.random.key(seed)
    ks = jax.random.split(key, 40)
    f32 = jnp.float32

    def nrm(k, shape, fan_in):
        return jax.random.normal(k, shape, f32) * (fan_in ** -0.5)

    def gain(k, shape):
        return 1.0 + 0.1 * jax.random.normal(k, shape, f32)

    def bias(k, shape):
        return 0.02 * jax.random.normal(k, shape, f32)

    D = D_MODEL
    return {
        "x": jax.random.normal(ks[0], (BATCH, SEQ, D), f32),
        "mix_pre_g": gain(ks[1], (DEPTH_2, D)),
        "mix_post_g": gain(ks[2], (DEPTH_2, D)),
        "ffn_pre_g": gain(ks[3], (DEPTH_2, D)),
        "ffn_post_g": gain(ks[4], (DEPTH_2, D)),
        "w_ff1": nrm(ks[5], (DEPTH_2, D, D_FF_2), D),
        "w_ff2": nrm(ks[6], (DEPTH_2, D_FF_2, D), D_FF_2),
        "conv_w_pw1": nrm(ks[7], (N_A_LAYERS, D, 2 * D), D),
        "conv_b_pw1": bias(ks[8], (N_A_LAYERS, 2 * D)),
        "conv_w_dw": nrm(ks[9], (N_A_LAYERS, CONV_WIDTH, D), CONV_WIDTH),
        "conv_b_dw": bias(ks[10], (N_A_LAYERS, D)),
        "conv_ln_g": gain(ks[11], (N_A_LAYERS, D)),
        "conv_ln_b": bias(ks[12], (N_A_LAYERS, D)),
        "conv_w_pw2": nrm(ks[13], (N_A_LAYERS, D, D), D),
        "conv_b_pw2": bias(ks[14], (N_A_LAYERS, D)),
        "mla_w_dq": nrm(ks[15], (N_B_LAYERS, D, Q_LORA_RANK), D),
        "mla_q_norm_g": gain(ks[16], (N_B_LAYERS, Q_LORA_RANK)),
        "mla_w_uq": nrm(ks[17], (N_B_LAYERS, Q_LORA_RANK, N_HEADS * QK_HEAD_DIM), Q_LORA_RANK),
        "mla_w_o": nrm(ks[18], (N_B_LAYERS, N_HEADS * V_HEAD_DIM, D), N_HEADS * V_HEAD_DIM),
        "kv_in_g": gain(ks[19], (D,)),
        "kv_w_dkv": nrm(ks[20], (D, KV_LORA_RANK), D),
        "kv_norm_g": gain(ks[21], (KV_LORA_RANK,)),
        "kv_w_kr": nrm(ks[22], (D, QK_ROPE_DIM), D),
        "kv_w_uk": nrm(ks[23], (KV_LORA_RANK, N_HEADS * QK_NOPE_DIM), KV_LORA_RANK),
        "kv_w_uv": nrm(ks[24], (KV_LORA_RANK, N_HEADS * V_HEAD_DIM), KV_LORA_RANK),
    }

def second_block(x, mix_pre_g, mix_post_g, ffn_pre_g, ffn_post_g, w_ff1, w_ff2,
              conv_w_pw1, conv_b_pw1, conv_w_dw, conv_b_dw, conv_ln_g, conv_ln_b,
              conv_w_pw2, conv_b_pw2, mla_w_dq, mla_q_norm_g, mla_w_uq, mla_w_o,
              kv_in_g, kv_w_dkv, kv_norm_g, kv_w_kr, kv_w_uk, kv_w_uv):
    cos, sin = rope_tables(x.shape[1])
    h = x
    k_nope = k_rope = v = None
    for layer in range(DEPTH_2):
        if layer == N_A_LAYERS:
            k_nope, k_rope, v = mla_shared_kv(h, kv_in_g, kv_w_dkv, kv_norm_g, kv_w_kr,
                                              kv_w_uk, kv_w_uv, cos, sin)
        hn = rms_norm_2(h, mix_pre_g[layer])
        if layer < N_A_LAYERS:
            a = layer
            m = conformer_conv(hn, conv_w_pw1[a], conv_b_pw1[a], conv_w_dw[a], conv_b_dw[a],
                               conv_ln_g[a], conv_ln_b[a], conv_w_pw2[a], conv_b_pw2[a])
        else:
            bl = layer - N_A_LAYERS
            m = mla_attention(hn, mla_w_dq[bl], mla_q_norm_g[bl], mla_w_uq[bl], mla_w_o[bl],
                              k_nope, k_rope, v, cos, sin)
        h = h + rms_norm_2(m, mix_post_g[layer])
        f = squared_relu_mlp(rms_norm_2(h, ffn_pre_g[layer]), w_ff1[layer], w_ff2[layer])
        h = h + rms_norm_2(f, ffn_post_g[layer])
    return h


def setup_inputs(seed=0):
    out = dict(first_inputs(seed))
    for name, value in second_inputs(seed + 1).items():
        if name != "x":
            out[name + "_2"] = value
    return out


def reference(
    x, mix_norm, w_in, w_alpha2, b_alpha, gla_norm, q_norm, k_norm, sinks, w_out, ffn_norm,
    w_up, conv_w, conv_b, w_down, mix_pre_g_2, mix_post_g_2, ffn_pre_g_2, ffn_post_g_2, w_ff1_2,
    w_ff2_2, conv_w_pw1_2, conv_b_pw1_2, conv_w_dw_2, conv_b_dw_2, conv_ln_g_2, conv_ln_b_2,
    conv_w_pw2_2, conv_b_pw2_2, mla_w_dq_2, mla_q_norm_g_2, mla_w_uq_2, mla_w_o_2, kv_in_g_2,
    kv_w_dkv_2, kv_norm_g_2, kv_w_kr_2, kv_w_uk_2, kv_w_uv_2,
):
    x = first_block(
        x, mix_norm, w_in, w_alpha2, b_alpha, gla_norm, q_norm, k_norm, sinks, w_out, ffn_norm,
        w_up, conv_w, conv_b, w_down,
    )
    return second_block(
        x, mix_pre_g_2, mix_post_g_2, ffn_pre_g_2, ffn_post_g_2, w_ff1_2, w_ff2_2, conv_w_pw1_2,
        conv_b_pw1_2, conv_w_dw_2, conv_b_dw_2, conv_ln_g_2, conv_ln_b_2, conv_w_pw2_2,
        conv_b_pw2_2, mla_w_dq_2, mla_q_norm_g_2, mla_w_uq_2, mla_w_o_2, kv_in_g_2, kv_w_dkv_2,
        kv_norm_g_2, kv_w_kr_2, kv_w_uk_2, kv_w_uv_2,
    )


_drawn_inputs = setup_inputs


def setup_inputs(seed=0):
    import zlib

    import numpy as np

    out = dict(_drawn_inputs(seed))
    spreads = {}
    factors = {'mix_norm': 3.714,
     'b_alpha': 4.248,
     'gla_norm': 7.533,
     'q_norm': 8.0,
     'k_norm': 8.0,
     'sinks': 46.592,
     'ffn_norm': 5.154,
     'conv_b': 4.861,
     'conv_b_pw1_2': 22.92,
     'mla_q_norm_g_2': 14.218,
     'mix_pre_g_2': 4.415,
     'mix_post_g_2': 6.663,
     'ffn_pre_g_2': 5.66,
     'ffn_post_g_2': 6.447,
     'conv_b_dw_2': 8.0,
     'conv_ln_g_2': 7.412,
     'conv_ln_b_2': 8.0,
     'conv_b_pw2_2': 8.0,
     'kv_in_g_2': 4.255,
     'kv_norm_g_2': 5.19}
    for name, (base, spread) in spreads.items():
        noise = np.random.default_rng([zlib.crc32(name.encode()), seed]).standard_normal(out[name].shape)
        drawn = base * np.exp(spread * noise) if base else spread * noise
        out[name] = __import__('jax').numpy.asarray(drawn.astype(out[name].dtype))
    for name, factor in factors.items():
        out[name] = (out[name] * factor).astype(out[name].dtype)
    return out
```

```python
from contextlib import ExitStack

import numpy as np

import concourse.bass as bass
from concourse import mybir

F32 = mybir.dt.float32
F32R = mybir.dt.float32r
I32 = mybir.dt.int32
ALU = mybir.AluOpType
ACT = mybir.ActivationFunctionType
AX_X = mybir.AxisListType.X

P = 128
SEQ = 512
D = 1024
KD = D // P
UNIT = 1024
RING = 4
AHEAD = 3
EPS = 1e-6
LN_EPS = 1e-5
NEG = -1e30

GLA_H, GLA_DK, GLA_DV, GLA_RANK, CHUNK = 4, 64, 128, 16, 64
SWA_H, SWA_KV, SWA_HD, WINDOW = 8, 2, 64, 128
D_FF = 2816
UP_PAIRS = D_FF // P
PAIRS_A = 12
PAIRS_B = UP_PAIRS - PAIRS_A
D_FF_2 = 4096
CONV_W = 31
MLA_H, NOPE, ROPE, V_DIM, Q_RANK, KV_RANK = 8, 128, 64, 128, 384, 256
MLA_SCALE = float(NOPE + ROPE) ** -0.5
NB = SEQ // P
NCH = SEQ // CHUNK
USE_LOOPS = True

PRODUCTS = [
    ("z", 19, 22), ("wout", 8, 8),
    ("upA", 2 * PAIRS_A, 2 * PAIRS_A), ("downA", PAIRS_A, 8),
    ("upB", 2 * PAIRS_B, 2 * PAIRS_B), ("downB", PAIRS_B, 8),
    ("pw1", 16, 16), ("pw2", 8, 8),
    ("ff1a0", 16, 16), ("ff2a0", 16, 8), ("ff1b0", 16, 16), ("ff2b0", 16, 8),
    ("dkv", 3, 3), ("dq", 3, 3), ("uk", 2, 8), ("uv", 2, 8), ("uq", 6, 12), ("wo", 8, 8),
    ("ff1a1", 16, 16), ("ff2a1", 16, 8), ("ff1b1", 16, 16), ("ff2b1", 16, 8),
]
UNIT0, TILE0 = {}, {}
_u = _t = 0
for _name, _units, _tiles in PRODUCTS:
    UNIT0[_name], TILE0[_name] = _u, _t
    _u, _t = _u + _units, _t + _tiles
N_UNITS = _u

SPLITS = [
    ("mix", 8), ("attn", 8), ("ffn", 8), ("prodA", PAIRS_A), ("prodB", PAIRS_B), ("pre0", 8), ("conv", 8),
    ("ffpre0", 8), ("hid0a", 16), ("hid0b", 16), ("kvpre", 8), ("pre1", 8), ("ckv", 2), ("cq", 3), ("mla", 8),
    ("ffpre1", 8), ("hid1a", 16), ("hid1b", 16),
]
SPLIT0 = {}
_x = 0
for _name, _n in SPLITS:
    SPLIT0[_name] = _x
    _x += _n

STATS = [("mix", 8)] + [(f"sq{t}", 1) for t in range(4)] + [("sk", 1)] + [(f"gla{h}", 1) for h in range(4)] + [
    ("ffn", 8), ("pre0", 8), ("ln_mean", 0), ("ln_var", 8), ("post0", 8), ("ffpre0", 8), ("ffpost0", 8),
    ("pre1", 8), ("ckv", 2), ("cq", 3), ("post1", 8), ("ffpre1", 8), ("ffpost1", 8),
]
STAT_NO, SQ0, ADD0, STAT_TILES = {}, {}, {}, {}
_s = _a = 0
for _i, (_name, _n) in enumerate(STATS):
    STAT_NO[_name], SQ0[_name], ADD0[_name], STAT_TILES[_name] = _i, _s, _a, _n
    _s, _a = _s + _n, _a + max(_n - 1, 0)

VECTORS = [
    ("mix_norm", 8), ("b_alpha", 2), ("gla_norm", 1), ("q_norm", 1), ("k_norm", 1), ("sinks", 8), ("ffn_norm", 8),
    ("conv", 4 * 2 * UP_PAIRS), ("pre", 16), ("post", 16), ("ffpre", 16), ("ffpost", 16), ("b_pw1", 16),
    ("w_dw", 8 * CONV_W), ("b_dw", 8), ("ln_g", 8), ("ln_b", 8), ("b_pw2", 8), ("kv_in", 8), ("ckv_norm", 2),
    ("cq_norm", 3),
]
COL0 = {}
_c = 0
for _name, _n in VECTORS:
    COL0[_name] = _c
    _c += _n
N_COLS = _c

IDENT, ONES, HALVES, SWAP = 0, P, 2 * P, 3 * P
CAUSAL, RESET, DIST = 0, SEQ, 2 * SEQ
COS, SIN, MASK_Q, MASK_K = 0, SEQ, 2 * SEQ, 2 * SEQ + P
N_CONST = 2 * SEQ + 3 * 256


def program(nc, xT, stream, vectors, w_alpha, consts, consts1, consts2, outT, stage=99):
    ctx = ExitStack()
    with ctx:
        def sb(name, shape, dtype=F32, where=ctx):
            return where.enter_context(nc.sbuf_tensor(name, shape, dtype))

        def sem(name):
            return ctx.enter_context(nc.semaphore(name))

        h = sb("h", [P, KD * SEQ])
        m = sb("m", [P, KD * SEQ])
        w_raw = [sb(f"w_raw{i}", [P, UNIT]) for i in range(RING)]
        w_hi = [sb(f"w_hi{i}", [P, UNIT], F32R) for i in range(RING)]
        w_lo = [sb(f"w_lo{i}", [P, UNIT], F32R) for i in range(RING)]
        cst = sb("cst", [P, 4 * P])
        cst_b = sb("cst_b", [P, N_CONST])
        cols = sb("cols", [P, N_COLS])
        TW = SEQ + 8
        tmp = [sb(f"tmp{i}", [P, TW]) for i in range(6)]
        ssum = sb("ssum", [P, SEQ])
        r_pre = sb("r_pre", [P, SEQ])
        r_post = sb("r_post", [P, SEQ])
        small = sb("small", [P, 64])
        sq_buf = [tmp[4][:, 0:SEQ], tmp[5][:, 0:SEQ]]
        root = tmp[4][:, 0:SEQ]

        at_a = ExitStack()
        a_hi = sb("a_hi", [P, KD * SEQ], F32R, at_a)
        a_lo = sb("a_lo", [P, KD * SEQ], F32R, at_a)
        at_a.close()
        at_a = ExitStack()
        gla_b = sb("gla_b", [P, 2 * SEQ], where=at_a)
        gla_e = sb("gla_e", [P, 2 * SEQ], where=at_a)
        gla_ke = sb("gla_ke", [P, 2 * SEQ], where=at_a)
        gla_kd = sb("gla_kd", [P, 2 * SEQ], where=at_a)
        gla_kdt = sb("gla_kdt", [P, 2 * SEQ], where=at_a)
        gla_s = sb("gla_s", [P, 2 * NCH * GLA_DV], where=at_a)
        gla_a = sb("gla_a", [P, 2 * SEQ], where=at_a)
        at_a.close()
        at_a = ExitStack()
        swa_p = [sb(f"swa_p{i}", [P, NB * 256], where=at_a) for i in range(2)]
        swa_pt = [sb(f"swa_pt{i}", [P, NB * 256], where=at_a) for i in range(2)]
        at_a.close()
        sb("a_region", [P, 2 * KD * SEQ])

        big = ExitStack()
        o_hi = sb("o_hi", [P, KD * SEQ], F32R, big)
        o_lo = sb("o_lo", [P, KD * SEQ], F32R, big)
        z_q = sb("z_q", [P, 2 * SEQ], where=big)
        z_k = sb("z_k", [P, 2 * SEQ], where=big)
        z_sq = sb("z_sq", [P, 4 * SEQ], where=big)
        z_v = sb("z_v", [P, NB * SEQ], where=big)
        z_sk = sb("z_sk", [P, P + SEQ], where=big)
        z_vs = sb("z_vs", [P, NB * P], where=big)
        z_lr = sb("z_lr", [P, SEQ], where=big)
        w_al = sb("w_al", [P, 256], where=big)
        big.close()
        z_r = m[:, 0:4 * SEQ]
        gla_a23 = m[:, 4 * SEQ:6 * SEQ]
        big = ExitStack()
        g_hi = sb("g_hi", [P, 16 * SEQ], F32R, big)
        g_lo = sb("g_lo", [P, 16 * SEQ], F32R, big)
        big.close()
        big = ExitStack()
        UW = SEQ + CONV_W - 1
        u_pad = sb("u_pad", [P, KD * UW], where=big)
        cv = sb("cv", [P, KD * SEQ], where=big)
        big.close()
        big = ExitStack()
        k_nope = sb("k_nope", [P, MLA_H * SEQ], where=big)
        v_tok = sb("v_tok", [P, NB * MLA_H * V_DIM], where=big)
        small_mla = ExitStack()
        b_hi = sb("b_hi", [P, KD * SEQ], F32R, small_mla)
        b_lo = sb("b_lo", [P, KD * SEQ], F32R, small_mla)
        small_mla.close()
        small_mla = ExitStack()
        q_nope = sb("q_nope", [P, MLA_H * SEQ], where=small_mla)
        q_rope = sb("q_rope", [P, 4 * SEQ], where=small_mla)
        small_mla.close()
        big.close()
        sb("big_region", [P, 32 * SEQ])
        c_kv, c_q = m[:, 0:2 * SEQ], m[:, 2 * SEQ:5 * SEQ]
        k_rope = m[:, 7 * SEQ:8 * SEQ]
        NP_ = P * NB * (NB + 1) // 2
        prob = m[:, 0:NP_]
        probT = m[:, NP_:2 * NP_]

        bank = [ctx.enter_context(nc.psum_tensor(f"bank{i}", [P, SEQ], F32)) for i in range(8)]

        h_landed = [sem(f"h_landed{k}") for k in range(KD)]
        cst_landed = sem("cst_landed")
        cst2_landed = sem("cst2_landed")
        w_landed = [sem(f"w_landed{i}") for i in range(RING)]
        whi_ready = sem("whi_ready")
        wlo_ready = sem("wlo_ready")
        unit_used = sem("unit_used")
        out_read = sem("out_read")
        xhi_ready = sem("xhi_ready")
        x_ready = sem("x_ready")
        sq_ready = sem("sq_ready")
        sum_added = sem("sum_added")
        stat_done = sem("stat_done")
        root_ready = sem("root_ready")
        r_ready = sem("r_ready")
        out_stored = sem("out_stored")

        def T(t, k, w=SEQ):
            return t[:, k * w:(k + 1) * w]

        def col(name, k=0):
            c = COL0[name] + k
            return cols[:, c:c + 1]

        def col_at(name, k):
            return cols[:, bass.ds(COL0[name] + k, 1)]

        def f(x):
            return x.bitcast(F32)

        def at(t, i, w=SEQ):
            return t[:, bass.ds(i * w, w)] if not isinstance(i, int) else t[:, i * w:(i + 1) * w]

        def swa_head(i):
            return i // 2 + 4 * (i % 2)

        def looped(eng, n, body):
            if USE_LOOPS:
                with eng.Fori(0, n) as i:
                    body(i)
            else:
                for i in range(n):
                    body(i)

        out_ready = sem("out_ready")
        rtok_sum = sem("rtok_sum")
        rtok_root = sem("rtok_root")
        rtok_ready = sem("rtok_ready")
        v_chain = sem("v_chain")
        a_chain = sem("a_chain")
        p_zero = sem("p_zero")
        gla_y = sem("gla_y")
        gla_l = sem("gla_l")
        gla_ls = sem("gla_ls")
        gla_cum = sem("gla_cum")
        gla_exp = sem("gla_exp")
        gla_ops = sem("gla_ops")
        gla_pe = sem("gla_pe")
        gla_ev = sem("gla_ev")
        silu_r = sem("silu_r")
        o_done = sem("o_done")
        q_normed = sem("q_normed")
        swa_sc = sem("swa_sc")
        swa_bias = sem("swa_bias")
        swa_mx = sem("swa_mx")
        swa_exp = sem("swa_exp")
        swa_se = sem("swa_se")
        swa_pn = sem("swa_pn")
        swa_tr = sem("swa_tr")
        swa_ev = sem("swa_ev")
        swa_ea = sem("swa_ea")
        swa_pv = sem("swa_pv")
        taps_a = sem("taps_a")
        taps_b = sem("taps_b")
        tap_mid = sem("tap_mid")
        tap_one = sem("tap_one")
        gated = sem("gated")
        prod = sem("prod")
        ug_sig = sem("ug_sig")
        u_ready = sem("u_ready")
        dw_chain = sem("dw_chain")
        mean_add = sem("mean_add")
        cen_ready = sem("cen_ready")
        ln_ready = sem("ln_ready")
        ln_silu = sem("ln_silu")
        h_ready = sem("h_ready")
        hid_sq = sem("hid_sq")
        rope_sw = sem("rope_sw")
        rope_t = sem("rope_t")
        rope_done = sem("rope_done")
        mla_sc = sem("mla_sc")
        mla_mx = sem("mla_mx")
        mla_exp = sem("mla_exp")
        mla_pn = sem("mla_pn")
        mla_tr = sem("mla_tr")
        mla_ev = sem("mla_ev")
        mla_ea = sem("mla_ea")
        mla_pv = sem("mla_pv")
        c_normed = sem("c_normed")

        H0 = {"post0": 0, "ffpost0": 8, "post1": 16}
        last_unit = {1: UNIT0["wout"], 2: UNIT0["upA"], 3: UNIT0["pw1"], 4: UNIT0["ff1a0"] + 1, 5: UNIT0["dkv"]}

        block = ctx.enter_context(nc.Block())

        @block.sync
        def _(sp):
            def load(n, slot):
                if not isinstance(n, int) or n >= RING:
                    sp.wait_ge(wlo_ready, n - RING + 1)
                src = stream[bass.ds(n * P, P), :] if not isinstance(n, int) else stream[n * P:(n + 1) * P, :]
                sp.dma_start(w_raw[slot][:, :], src).then_inc(w_landed[slot], 16)

            sp.dma_start(h[:, 0:SEQ], xT[0:P, :]).then_inc(h_landed[0], 16)
            sp.dma_start(cols[:, :], vectors).then_inc(cst_landed, 16)
            load(0, 0)
            for k in range(1, KD):
                sp.dma_start(T(h, k), xT[k * P:(k + 1) * P, :]).then_inc(h_landed[k], 16)
                if k in (2, 4, 6):
                    load(k // 2, k // 2)
            sp.dma_start(cst[:, :], consts).then_inc(cst_landed, 16)
            sp.dma_start(cst_b[:, :], consts1).then_inc(cst_landed, 16)
            sp.dma_start(w_al[:, :], w_alpha).then_inc(cst_landed, 16)

            def four(i):
                for j in range(RING):
                    load(4 * i + (RING + j), j)
            total = min(N_UNITS, last_unit[stage] + AHEAD) if stage in last_unit else N_UNITS
            rounds = (total - RING) // RING
            looped(sp, rounds, four)
            for n in range(RING + RING * rounds, total):
                load(n, n % RING)
            for k in range(KD):
                sp.wait_ge(out_ready, k + 1)
                sp.dma_start(outT[k * P:(k + 1) * P, :], T(h, k)).then_inc(out_stored, 16)
            sp.wait_ge(out_stored, 16 * KD)
            if stage > 2:
                sp.wait_ge(cst2_landed, 16)

        @block.gpsimd
        def _(pool):
            def add_squares(name):
                for k in range(1, STAT_TILES[name]):
                    a = ADD0[name] + k - 1
                    pool.wait_ge(sq_ready, SQ0[name] + k + 1)
                    if k >= 2:
                        pool.wait_ge(sum_added, a)
                    pool.tensor_tensor(ssum[:, :], ssum[:, :], sq_buf[a % 2], ALU.add).then_inc(sum_added, 1)

            def gate_products(name, pairs):
                base = 0 if name == "prodA" else PAIRS_A

                def body(i):
                    for j in range(2):
                        pool.wait_ge(gated, 2 * i + (base + j + 1))
                        pool.wait_ge(taps_b, 2 * i + (base + j + 1))
                        pool.tensor_tensor(tmp[4][:, 0:SEQ], tmp[4][:, 0:SEQ], tmp[3][:, 0:SEQ], ALU.mult)\
                            .then_inc(prod, 1)
                looped(pool, pairs // 2, body)

            def hidden_squares(half):
                def body(i):
                    for j in range(4):
                        pool.wait_ge(out_read, 4 * i + (TILE0[f"ff1{half[1]}{half[0]}"] + j + 1))
                        pool.wait_ge(x_ready, 4 * i + (SPLIT0[f"hid{half}"] + j - 1))
                        pool.tensor_tensor(tmp[2 + j % 2][:, 0:SEQ], tmp[j % 2][:, 0:SEQ], tmp[j % 2][:, 0:SEQ],
                                           ALU.mult).then_inc(hid_sq, 1)
                looped(pool, 4, body)

            pool.memset(z_sk[:, 0:P], 0.0).then_inc(p_zero, 1)
            add_squares("mix")
            if stage < 2:
                return
            pool.wait_ge(unit_used, UNIT0["wout"])
            pool.memset(gla_a[:, :], 0.0).then_inc(p_zero, 1)
            pool.memset(gla_a23, 0.0).then_inc(p_zero, 1)
            add_squares("ffn")
            if stage < 3:
                return
            for i in range(2):
                pool.memset(tmp[i][:, 0:2], 0.0).then_inc(p_zero, 1)
            gate_products("prodA", PAIRS_A)
            gate_products("prodB", PAIRS_B)
            add_squares("pre0")
            if stage < 4:
                return
            pool.wait_ge(unit_used, UNIT0["pw1"])
            for k in range(KD):
                pool.memset(u_pad[:, k * UW:k * UW + CONV_W - 1], 0.0).then_inc(p_zero, 1)
            for k in range(KD):
                pool.wait_ge(dw_chain, 2 * CONV_W * (k // 2 + 1))
                if k == 0:
                    pool.wait_ge(stat_done, STAT_NO["ln_mean"])
                    pool.tensor_copy(ssum[:, :], T(cv, 0)).then_inc(mean_add, 1)
                else:
                    pool.wait_ge(mean_add, k)
                    pool.tensor_tensor(ssum[:, :], ssum[:, :], T(cv, k), ALU.add).then_inc(mean_add, 1)
            add_squares("ln_var")
            add_squares("post0")
            add_squares("ffpre0")
            if stage < 5:
                return
            for layer in range(2):
                if layer == 1:
                    add_squares("pre1")
                    add_squares("ckv")
                    add_squares("cq")
                    add_squares("post1")
                    add_squares("ffpre1")
                hidden_squares(f"{layer}a")
                hidden_squares(f"{layer}b")
                add_squares(f"ffpost{layer}")
                if stage < 6:
                    return

        @block.scalar
        def _(act):
            def w_hi_of(n, slot):
                if isinstance(n, int) and n >= N_UNITS:
                    return
                rounds = (n - slot) // RING + 1 if isinstance(n, int) else None
                assert rounds is not None
                act.wait_ge(w_landed[slot], 16 * rounds)
                if n >= RING:
                    act.wait_ge(unit_used, n - RING + 1)
                act.activation(w_hi[slot][:, :], w_raw[slot][:, :], ACT.Copy).then_inc(whi_ready, 1)

            def w_hi_loop(n0, i, j):
                n = n0 + j + AHEAD
                slot = n % RING
                if isinstance(i, int):
                    return w_hi_of(n + 4 * i, slot)
                act.wait_ge(w_landed[slot], 16 * i + 16 * (n // RING + 1))
                act.wait_ge(unit_used, 4 * i + (n - RING + 1))
                act.activation(w_hi[slot][:, :], w_raw[slot][:, :], ACT.Copy).then_inc(whi_ready, 1)

            def square(name, k, src):
                s = STAT_NO[name]
                if k == 0:
                    if s:
                        act.wait_ge(stat_done, s)
                        act.wait_ge(r_ready, s)
                    dst = ssum[:, :]
                else:
                    a = ADD0[name] + k - 1
                    if a >= 2:
                        act.wait_ge(sum_added, a - 1)
                    dst = sq_buf[a % 2]
                act.activation(dst, src, ACT.Square).then_inc(sq_ready, 1)

            def take_root(name, n, eps=EPS):
                s = STAT_NO[name]
                act.wait_ge(stat_done, s + 1)
                act.activation(root, bank[4][:, :], ACT.Sqrt, scale=1.0 / n, bias=eps_col(eps)).then_inc(root_ready, 1)

            def x_hi(dst, k, src, gain):
                act.activation(T(dst, k), src, ACT.Identity, scale=gain).then_inc(xhi_ready, 1)

            def eps_col(eps):
                return small[:, 60:61] if eps == EPS else small[:, 61:62]

            act.wait_ge(cst_landed, 64)
            for k in range(KD):
                act.wait_ge(h_landed[k], 16)
                x_hi(a_hi, k, T(h, k), col("mix_norm", k))
                if k in (0, 2, 4):
                    w_hi_of(k // 2, k // 2)
                square("mix", k, T(h, k))
            act.wait_ge(v_chain, 2)
            take_root("mix", D)
            act.wait_ge(rtok_sum, 1)
            act.activation(small[:, 0:NB], bank[5][:, 0:NB], ACT.Sqrt, scale=1.0 / D, bias=eps_col(EPS))\
                .then_inc(rtok_root, 1)
            for n in range(19):
                w_hi_of(n + AHEAD, (n + AHEAD) % RING)
            if stage < 2:
                return
            t0 = TILE0["z"]
            for t in range(4):
                act.wait_ge(out_read, t0 + 9 + t + 1)
                square(f"sq{t}", 0, T(z_sq, t))
                take_root(f"sq{t}", SWA_HD)
            act.wait_ge(out_read, t0 + 13 + 1)
            square("sk", 0, z_sk[:, P:])
            take_root("sk", SWA_HD)
            act.wait_ge(unit_used, UNIT0["wout"])
            for t in range(2):
                act.wait_ge(gla_pe, t + 1)
                act.activation(T(gla_b, t), bank[t][:, :], ACT.Identity, bias=col("b_alpha", t)).then_inc(gla_y, 1)
            act.wait_ge(gla_y, 2)
            act.activation(gla_e[:, :], gla_b[:, :], ACT.Abs).then_inc(a_chain, 1)
            act.wait_ge(a_chain, 1)
            act.activation(gla_e[:, :], gla_e[:, :], ACT.Exp, scale=-1.0).then_inc(a_chain, 1)
            act.wait_ge(a_chain, 2)
            act.activation(gla_e[:, :], gla_e[:, :], ACT.Ln, bias=1.0).then_inc(gla_l, 1)
            act.wait_ge(gla_cum, 2)
            act.activation(gla_e[:, :], gla_b[:, :], ACT.Exp, scale=1.0 / 16).then_inc(gla_exp, 1)
            act.activation(gla_ke[:, :], gla_b[:, :], ACT.Exp, scale=-1.0 / 16).then_inc(gla_exp, 1)
            act.wait_ge(gla_cum, 3)
            act.activation(gla_kd[:, :], gla_kd[:, :], ACT.Exp, scale=1.0 / 16).then_inc(gla_exp, 1)
            last = gla_b[:, :].rearrange("p (t n c) -> p t n c", t=2, c=CHUNK)[:, :, :, CHUNK - 1]
            act.activation(small[:, 8:8 + 2 * NCH].rearrange("p (t n) -> p t n", t=2), last, ACT.Exp,
                           scale=1.0 / 16).then_inc(gla_exp, 1)
            act.wait_ge(gla_pe, 8)
            act.activation(T(gla_kdt, 1), bank[6][:, :], ACT.Copy).then_inc(gla_exp, 1)
            for t in range(4):
                act.activation(T(z_r, t), T(z_r, t), ACT.Silu).then_inc(silu_r, 1)
            for hd in range(GLA_H):
                act.wait_ge(gla_pe, 13 + hd)
                square(f"gla{hd}", 0, bank[hd][:, :])
                take_root(f"gla{hd}", GLA_DV)
            for hd in range(GLA_H):
                act.wait_ge(o_done, hd + 1)
                act.activation(T(o_hi, hd), tmp[hd][:, 0:SEQ], ACT.Copy).then_inc(xhi_ready, 1)
            for i in range(SWA_H):
                p, t = swa_p[i % 2], swa_pt[i % 2]
                act.wait_ge(swa_mx, 2 * (i + 1))
                nm = small[:, 32:36] if i % 2 == 0 else small[:, 40:44]
                den = small[:, 36:40] if i % 2 == 0 else small[:, 44:48]
                se = small[:, 48:52] if i % 2 == 0 else small[:, 52:56]
                act.activation(se, nm, ACT.Exp, bias=col("sinks", swa_head(i))).then_inc(swa_se, 1)
                for b in range(NB):
                    act.activation(T(p, b, 256), T(p, b, 256), ACT.Exp, scale=SWA_HD ** -0.5, bias=nm[:, b:b + 1],
                                   accum_out=den[:, b:b + 1]).then_inc(swa_exp, 1)
                act.wait_ge(swa_tr, 2 * (i + 1))
                if i >= 2:
                    act.wait_ge(swa_pv, i - 1)
                act.activation(t[:, SEQ:], bank[6][:, :], ACT.Copy).then_inc(swa_ea, 1)
                if i % 2:
                    act.wait_ge(swa_pv, i + 1)
                    act.activation(T(o_hi, 4 + i // 2), bank[7][:, :], ACT.Copy).then_inc(xhi_ready, 1)
            for k in range(8):
                w_hi_of(UNIT0["wout"] + k + AHEAD, (UNIT0["wout"] + k + AHEAD) % RING)
                act.wait_ge(out_read, TILE0["wout"] + k + 1)
                x_hi(a_hi, k, T(h, k), col("ffn_norm", k))
                square("ffn", k, T(h, k))
            take_root("ffn", D)
            if stage < 3:
                return
            act.dma_start(cst_b[:, :], consts2).then_inc(cst2_landed, 16)

            def up(name, split, first_pair, pairs):
                n0, x0 = UNIT0[name], SPLIT0[split]

                def body(i):
                    for j in range(2):
                        pr = first_pair + j + 1
                        w_hi_loop(n0, i, 2 * j)
                        act.wait_ge(out_read, 4 * i + (TILE0[name] + 2 * j + 1))
                        act.activation(tmp[2][:, 0:SEQ], tmp[0][:, 2:2 + SEQ], ACT.Identity,
                                       scale=conv_col(i, first_pair + j, 0, 2), bias=conv_col(i, first_pair + j, 0, 3))\
                            .then_inc(tap_mid, 1)
                        w_hi_loop(n0, i, 2 * j + 1)
                        act.wait_ge(out_read, 4 * i + (TILE0[name] + 2 * j + 2))
                        act.activation(tmp[3][:, 0:SEQ], tmp[1][:, 2:2 + SEQ], ACT.Identity,
                                       scale=conv_col(i, first_pair + j, 1, 2), bias=conv_col(i, first_pair + j, 1, 3))\
                            .then_inc(tap_mid, 1)
                        act.wait_ge(taps_a, 2 * i + pr)
                        act.wait_ge(x_ready, 2 * i + (x0 + j))
                        act.activation(tmp[4][:, 0:SEQ], tmp[2][:, 0:SEQ], ACT.Silu).then_inc(gated, 1)
                        act.wait_ge(prod, 2 * i + pr)
                        act.activation(at(g_hi, 2 * i + j), tmp[4][:, 0:SEQ], ACT.Copy).then_inc(xhi_ready, 1)
                looped(act, pairs // 2, body)

            def conv_col(i, j, half, tap):
                return col_at("conv", 16 * i + (8 * j + 4 * half + tap)) if not isinstance(i, int) else \
                    col("conv", 16 * i + 8 * j + 4 * half + tap)

            act.wait_ge(p_zero, 5)
            act.wait_ge(r_ready, STAT_NO["ffn"] + 1)
            up("upA", "prodA", 0, PAIRS_A)
            for n in range(UNIT0["downA"], UNIT0["upB"]):
                w_hi_of(n + AHEAD, (n + AHEAD) % RING)
            up("upB", "prodB", PAIRS_A, PAIRS_B)
            for k in range(KD):
                if k % 4 == 0:
                    first = UNIT0["downB"] + k // 4 * (PAIRS_B // 2)
                    for n in range(first, first + PAIRS_B // 2):
                        w_hi_of(n + AHEAD, (n + AHEAD) % RING)
                act.wait_ge(out_read, TILE0["downB"] + k + 1)
                x_hi(a_hi, k, T(h, k), col("pre", k))
                square("pre0", k, T(h, k))
            take_root("pre0", D)
            if stage < 4:
                return

            for k in range(KD):
                n = UNIT0["pw1"] + 2 * k
                w_hi_of(n + AHEAD, (n + AHEAD) % RING)
                w_hi_of(n + 1 + AHEAD, (n + 1 + AHEAD) % RING)
                act.wait_ge(out_read, TILE0["pw1"] + 2 * k + 2)
                act.activation(tmp[1][:, 0:SEQ], tmp[1][:, 0:SEQ], ACT.Sigmoid, bias=col("b_pw1", 8 + k))\
                    .then_inc(ug_sig, 1)
            act.wait_ge(stat_done, STAT_NO["ln_mean"] + 1)
            act.activation(root, bank[4][:, :], ACT.Copy, scale=1.0 / D).then_inc(root_ready, 1)
            for k in range(KD):
                act.wait_ge(cen_ready, k + 1)
                square("ln_var", k, T(cv, k))
            take_root("ln_var", D, LN_EPS)
            for k in range(KD):
                act.wait_ge(ln_ready, k + 1)
                act.activation(T(cv, k), T(cv, k), ACT.Silu, bias=col("ln_b", k)).then_inc(ln_silu, 1)
                act.wait_ge(ln_silu, k + 1)
                act.activation(T(a_hi, k), T(cv, k), ACT.Copy).then_inc(xhi_ready, 1)

            def after(product, stat, per_tile_units):
                for k in range(KD):
                    for u in range(per_tile_units):
                        n = UNIT0[product] + per_tile_units * k + u + AHEAD
                        w_hi_of(n, n % RING)
                    act.wait_ge(out_read, TILE0[product] + k + 1)
                    square(stat, k, T(m, k))
                take_root(stat, D)

            def next_operand(h0, gain, g0, stat):
                for k in range(KD):
                    act.wait_ge(h_ready, h0 + k + 1)
                    x_hi(a_hi, k, T(h, k), col(gain, g0 + k))
                    square(stat, k, T(h, k))
                take_root(stat, D)

            after("pw2", "post0", 1)
            next_operand(H0["post0"], "ffpre", 0, "ffpre0")
            if stage < 5:
                return

            def feed_forward(layer):
                for half in range(2):
                    c = "ab"[half]
                    n0 = UNIT0[f"ff1{c}{layer}"]
                    t0 = TILE0[f"ff1{c}{layer}"]

                    def body(i):
                        for j in range(4):
                            w_hi_loop(n0, i, j)
                            act.wait_ge(out_read, 4 * i + (t0 + j + 1))
                            act.activation(at(g_hi, 4 * i + j), tmp[j % 2][:, 0:SEQ], ACT.Square)\
                                .then_inc(xhi_ready, 1)
                    looped(act, 4, body)
                    if half == 0:
                        looped(act, 4, lambda i: [w_hi_loop(UNIT0[f"ff2a{layer}"], i, j) for j in range(4)])
                after(f"ff2b{layer}", f"ffpost{layer}", 2)

            feed_forward(0)
            if stage < 6:
                return
            for k in range(KD):
                act.wait_ge(h_ready, H0["ffpost0"] + k + 1)
                x_hi(a_hi, k, T(h, k), col("kv_in", k))
                square("pre1", k, T(h, k))
            take_root("pre1", D)
            for k in range(KD):
                x_hi(b_hi, k, T(h, k), col("pre", 8 + k))
            for n in range(UNIT0["dkv"], UNIT0["uk"]):
                w_hi_of(n + AHEAD, (n + AHEAD) % RING)
            for k in range(2):
                act.wait_ge(out_read, TILE0["dkv"] + k + 1)
                square("ckv", k, T(c_kv, k))
            take_root("ckv", KV_RANK)
            for k in range(3):
                act.wait_ge(out_read, TILE0["dq"] + k + 1)
                square("cq", k, T(c_q, k))
            take_root("cq", Q_RANK)
            for k in range(5):
                act.wait_ge(c_normed, k + 1)
                if k == 0:
                    act.wait_ge(unit_used, UNIT0["dq"])
                act.activation(T(a_hi, k), T(m, k), ACT.Copy).then_inc(xhi_ready, 1)
            for n in range(UNIT0["uk"], UNIT0["wo"]):
                w_hi_of(n + AHEAD, (n + AHEAD) % RING)
            for i in range(MLA_H):
                nm = small[:, 32:36] if i % 2 == 0 else small[:, 40:44]
                den = small[:, 36:40] if i % 2 == 0 else small[:, 44:48]
                act.wait_ge(mla_mx, 5 * (i + 1))
                if i:
                    act.wait_ge(mla_tr, 3 * i)
                for b in range(NB):
                    w = (b + 1) * P
                    o = P * b * (b + 1) // 2
                    act.activation(prob[:, o:o + w], bank[b][:, 0:w], ACT.Exp, scale=MLA_SCALE, bias=nm[:, b:b + 1],
                                   accum_out=den[:, b:b + 1]).then_inc(mla_exp, 1)
                act.wait_ge(mla_tr, 3 * i + 2)
                if i:
                    act.wait_ge(mla_pv, i)
                act.activation(probT[:, SEQ:2 * SEQ], bank[6][:, :], ACT.Copy).then_inc(mla_ea, 1)
                act.wait_ge(mla_pv, i + 1)
                act.activation(T(a_hi, i), bank[4][:, :], ACT.Copy).then_inc(xhi_ready, 1)
            after("wo", "post1", 1)
            next_operand(H0["post1"], "ffpre", 8, "ffpre1")
            feed_forward(1)

        @block.tensor
        def _(pe):
            def three(out, w0, w1, x0, x1, start, stop):
                pe.matmul(out, w0, x0, start=start, stop=False)
                pe.matmul(out, w0, x1, start=False, stop=False)
                return pe.matmul(out, w1, x0, start=False, stop=stop)

            def bank_free(name, j):
                pe.wait_ge(out_read, TILE0[name] + max(j - 3, 0))

            def k_ready(split, k):
                pe.wait_ge(x_ready, SPLIT0[split] + k + 1)

            def unit_ready(n, i=0):
                pe.wait_ge(wlo_ready, n + 1 + 4 * i if isinstance(i, int) else 4 * i + (n + 1))

            def tile_of_eight(n, slot, out, hi, lo, split=None, k0=0, start=True, stop=True, waits=()):
                for k in range(8):
                    if split is not None:
                        k_ready(split, k0 + k)
                    last = three(out, T(w_hi[slot], k, P), T(w_lo[slot], k, P), T(hi, k0 + k), T(lo, k0 + k),
                                 start and k == 0, stop and k == 7)
                last.then_inc(unit_used, 1)

            def stat(name, lhsT=None):
                s, n = STAT_NO[name], STAT_TILES[name]
                pe.wait_ge(sq_ready, SQ0[name] + n)
                if n > 1:
                    pe.wait_ge(sum_added, ADD0[name] + n - 1)
                if s:
                    pe.wait_ge(root_ready, s)
                pe.matmul(bank[4][:, :], cst[:, ONES:ONES + P] if lhsT is None else lhsT, ssum[:, :],
                          start=True, stop=True).then_inc(stat_done, 1)

            def tiles(name, count, hi, lo, split=None, stat_name=None, first=0):
                n0 = UNIT0[name]
                for j in range(first, count):
                    n = n0 + j
                    unit_ready(n)
                    bank_free(name, j)
                    tile_of_eight(n, n % RING, bank[j % 4][:, :], hi, lo, split if j == 0 else None)
                    if j == 0 and stat_name:
                        stat(stat_name)

            n0 = UNIT0["z"]
            for j in range(14):
                unit_ready(n0 + j)
                if j >= 4:
                    pe.wait_ge(out_read, j - 3)
                tile_of_eight(n0 + j, j % RING, bank[j % 4][:, :], a_hi, a_lo, "mix" if j == 0 else None)
                if j == 0:
                    pe.wait_ge(cst_landed, 64)
                    stat("mix")
                    for b in range(NB):
                        last = pe.matmul(bank[5][:, b:b + 1], T(ssum, b, P), cst[:, ONES:ONES + 1],
                                         start=True, stop=True)
                    last.then_inc(rtok_sum, 1)
            n = n0 + 14
            unit_ready(n)
            for b in range(NB):
                j = 14 + b
                pe.wait_ge(out_read, j - 3)
                for k in range(KD):
                    xh, xl = T(a_hi, k)[:, b * P:(b + 1) * P], T(a_lo, k)[:, b * P:(b + 1) * P]
                    last = three(bank[j % 4][:, 0:P], xh, xl, T(w_hi[n % RING], k, P), T(w_lo[n % RING], k, P),
                                 k == 0, k == KD - 1)
            last.then_inc(unit_used, 1)
            for u in range(4):
                n = n0 + 15 + u
                unit_ready(n)
                for kk in range(2):
                    k = 2 * u + kk
                    for b in range(NB):
                        j = 18 + b
                        if k == 0:
                            pe.wait_ge(out_read, j - 3)
                        xh, xl = T(a_hi, k)[:, b * P:(b + 1) * P], T(a_lo, k)[:, b * P:(b + 1) * P]
                        last = three(bank[j % 4][:, :], xh, xl, T(w_hi[n % RING], kk), T(w_lo[n % RING], kk),
                                     k == 0, k == KD - 1)
                last.then_inc(unit_used, 1)
            if stage < 2:
                return
            for name in ("sq0", "sq1", "sq2", "sq3", "sk"):
                stat(name, cst[:, HALVES:HALVES + P])
            pe.wait_ge(out_read, TILE0["wout"])
            for t in range(2):
                pe.matmul(bank[t][:, :], T(w_al, t, P), z_lr[:, :], start=True, stop=True).then_inc(gla_pe, 1)
            pe.wait_ge(gla_ops, 3)
            for hd in range(GLA_H):
                r = slice(64 * (hd % 2), 64 * (hd % 2) + 64)
                if hd == 0:
                    pe.wait_ge(gla_y, 2)
                for b in range(NB):
                    last = pe.matmul(T(bank[hd], b, P), T(gla_ke, hd // 2)[r, b * P:(b + 1) * P],
                                     T(z_q, hd // 2)[r, b * P:(b + 1) * P], start=True, stop=True)
                last.then_inc(gla_pe, 1)
            for t in range(2):
                for b in range(NB):
                    last = pe.transpose(T(bank[5 + t], b, P), T(gla_kd, t)[:, b * P:(b + 1) * P],
                                        cst[:, IDENT:IDENT + P])
                last.then_inc(gla_pe, 1)
            pe.wait_ge(gla_ev, 5)
            pe.wait_ge(gla_exp, 5)
            for t in range(2):
                for par in range(2):
                    for q in range(NB):
                        for e in range(2):
                            hd = 2 * t + e
                            last = pe.matmul(T(bank[2 * t + par], q, P)[64 * e:64 * e + 64, :],
                                             T(gla_kdt, t)[64 * par:64 * par + 64, q * P + 64 * e:q * P + 64 * e + 64],
                                             T(z_v, q)[64 * par:64 * par + 64, hd * P:(hd + 1) * P],
                                             start=True, stop=True, skip_group_check=True)
                    last.then_inc(gla_pe, 1)
            pe.wait_ge(gla_ev, 5 + 2 * (NCH - 1))
            for hd in range(GLA_H):
                r = slice(64 * (hd % 2), 64 * (hd % 2) + 64)
                a_t = gla_a[:, hd * SEQ:(hd + 1) * SEQ] if hd < 2 else gla_a23[:, (hd - 2) * SEQ:(hd - 1) * SEQ]
                for b in range(NB):
                    pe.matmul(T(bank[hd], b, P), T(z_v, b)[:, hd * P:(hd + 1) * P], a_t[:, b * P:(b + 1) * P],
                              start=True, stop=False)
                    for e in range(2):
                        c = 2 * b + e
                        if c == 0:
                            continue
                        s = gla_s[r, ((hd // 2) * NCH + c) * GLA_DV:((hd // 2) * NCH + c + 1) * GLA_DV]
                        last = pe.matmul(bank[hd][:, c * CHUNK:(c + 1) * CHUNK], s,
                                         T(z_q, hd // 2)[r, c * CHUNK:(c + 1) * CHUNK], start=False, stop=(e == 1))
                last.then_inc(gla_pe, 1)
            for hd in range(GLA_H):
                stat(f"gla{hd}")

            def swa_scores(i):
                hd = swa_head(i)
                r = slice(64 * (hd // 4), 64 * (hd // 4) + 64)
                t = hd % 4
                if i == 0:
                    pe.wait_ge(o_done, GLA_H)
                    pe.wait_ge(q_normed, 5)
                    pe.wait_ge(p_zero, 1)
                if i >= 2:
                    pe.wait_ge(swa_bias, 2 * (i - 1))
                for b in range(NB):
                    out = bank[2 * (i % 2) + b // 2][:, 256 * (b % 2):256 * (b % 2) + 256]
                    last = pe.matmul(out, T(z_sq, t)[r, b * P:(b + 1) * P], z_sk[r, b * P:b * P + 256],
                                     start=True, stop=True)
                last.then_inc(swa_sc, 1)

            swa_scores(0)
            for i in range(SWA_H):
                if i + 1 < SWA_H:
                    swa_scores(i + 1)
                p, t = swa_p[i % 2], swa_pt[i % 2]
                pe.wait_ge(swa_pn, NB * (i + 1))
                if i:
                    pe.wait_ge(swa_ev, i)
                    pe.wait_ge(swa_ea, i)
                for b in range(NB):
                    for e in range(2):
                        if b == 0 and e == 0:
                            continue
                        last = pe.transpose(bank[5 + b // 2][:, (2 * (b % 2) + e) * P:(2 * (b % 2) + e + 1) * P],
                                            p[:, b * 256 + e * P:b * 256 + (e + 1) * P], cst[:, IDENT:IDENT + P])
                    if b % 2:
                        last.then_inc(swa_tr, 1)
                pe.wait_ge(swa_ev, i + 1)
                pe.wait_ge(swa_ea, i + 1)
                g = i % 2
                if g == 0 and i:
                    pe.wait_ge(x_ready, SPLIT0["attn"] + 4 + i // 2)
                for b in range(NB):
                    es = [e for e in range(2) if b + e > 0]
                    for e in es:
                        last = pe.matmul(bank[7][64 * g:64 * g + 64, b * P:(b + 1) * P],
                                         z_vs[:, (b - 1 + e) * P + 64 * g:(b - 1 + e) * P + 64 * g + 64],
                                         t[:, (2 * b + e) * P:(2 * b + e + 1) * P], start=(e == es[0]), stop=(e == 1))
                last.then_inc(swa_pv, 1)
            tiles("wout", 8, o_hi, o_lo, "attn")
            if stage < 3:
                stat("ffn")
                return

            def up(name, split, pairs):
                n0 = UNIT0[name]

                def body(i):
                    for j in range(4):
                        unit_ready(n0 + j, i)
                        pe.wait_ge(out_read, 4 * i + (TILE0[name] + j - 3))
                        tile_of_eight(n0 + j, (n0 + j) % RING, bank[j % 4][:, :], a_hi, a_lo)
                if split:
                    for j in range(4):
                        unit_ready(n0 + j)
                        bank_free(name, j)
                        tile_of_eight(n0 + j, (n0 + j) % RING, bank[j % 4][:, :], a_hi, a_lo, split if j == 0 else None)
                        if j == 0:
                            stat(split)

                    def rest(i):
                        for j in range(4):
                            unit_ready(n0 + 4 + j, i)
                            pe.wait_ge(out_read, 4 * i + (TILE0[name] + j + 1))
                            tile_of_eight(n0 + j, (n0 + j) % RING, bank[j % 4][:, :], a_hi, a_lo)
                    looped(pe, pairs // 2 - 1, rest)
                else:
                    looped(pe, pairs // 2, body)

            def down(name, split, kts):
                n = UNIT0[name]
                for g in range(2):
                    for u in range(kts // 2):
                        unit_ready(n)
                        for kk in range(2):
                            k = 2 * u + kk
                            k_ready(split, k)
                            for j in range(4):
                                if k == 0:
                                    pe.wait_ge(out_read, TILE0[name])
                                w = slice((4 * kk + j) * P, (4 * kk + j + 1) * P)
                                last = three(bank[4 * g + j][:, :], w_hi[n % RING][:, w], w_lo[n % RING][:, w],
                                             T(g_hi, k), T(g_lo, k), k == 0, k == kts - 1)
                        last.then_inc(unit_used, 1)
                        n += 1

            up("upA", "ffn", PAIRS_A)
            down("downA", "prodA", PAIRS_A)
            pe.wait_ge(out_read, TILE0["upB"])
            up("upB", None, PAIRS_B)
            down("downB", "prodB", PAIRS_B)
            if stage < 4:
                stat("pre0")
                return
            pe.wait_ge(out_read, TILE0["pw1"])
            tiles("pw1", 16, a_hi, a_lo, "pre0", "pre0")
            pe.wait_ge(mean_add, KD)
            pe.wait_ge(root_ready, STAT_NO["ln_mean"])
            pe.matmul(bank[4][:, :], cst[:, ONES:ONES + P], ssum[:, :], start=True, stop=True).then_inc(stat_done, 1)
            stat("ln_var")
            tiles("pw2", 8, a_hi, a_lo, "conv")
            stat("post0")
            if stage < 5:
                tiles("ff1a0", 1, a_hi, a_lo, "ffpre0", "ffpre0")
                return

            def feed_forward(layer):
                up(f"ff1a{layer}", f"ffpre{layer}", 8)
                for half in range(2):
                    c = "ab"[half]
                    if half:
                        pe.wait_ge(out_read, TILE0[f"ff1b{layer}"])
                        up(f"ff1b{layer}", None, 8)
                    name = f"ff2{c}{layer}"
                    n0, t0 = UNIT0[name], TILE0[name]
                    pe.wait_ge(x_ready, SPLIT0[f"hid{layer}{c}"] + 16)

                    def body(i):
                        for j in range(2):
                            b = j
                            pe.wait_ge(out_read, 2 * i + (t0 + j - 1))
                            for u in range(2):
                                n = n0 + 2 * j + u
                                unit_ready(n, i)
                                tile_of_eight(n, n % RING, bank[b][:, :], g_hi, g_lo, None, 8 * u, u == 0, u == 1)
                    looped(pe, 4, body)
                stat(f"ffpost{layer}")

            feed_forward(0)
            if stage < 6:
                return
            tiles("dkv", 3, a_hi, a_lo, "kvpre", "pre1")
            tiles("dq", 3, b_hi, b_lo, "pre1")
            swap = cst[:, SWAP:SWAP + P]
            pe.wait_ge(out_read, TILE0["dkv"] + 3)
            pe.matmul(bank[5][:, :], swap, k_rope, start=True, stop=True).then_inc(rope_sw, 1)
            stat("ckv")
            stat("cq")
            for u in range(2):
                n = UNIT0["uk"] + u
                unit_ready(n)
                for j in range(4):
                    bank_free("uk", 4 * u + j)
                    for k in range(2):
                        if u == 0 and j == 0:
                            k_ready("ckv", k)
                        w = slice((4 * k + j) * P, (4 * k + j + 1) * P)
                        last = three(bank[j][:, :], w_hi[n % RING][:, w], w_lo[n % RING][:, w], T(a_hi, k), T(a_lo, k),
                                     k == 0, k == 1)
                last.then_inc(unit_used, 1)
            for u in range(2):
                n = UNIT0["uv"] + u
                unit_ready(n)
                for b in range(NB):
                    bank_free("uv", 4 * u + b)
                    for k in range(2):
                        last = three(bank[b][:, :], T(a_hi, k)[:, b * P:(b + 1) * P], T(a_lo, k)[:, b * P:(b + 1) * P],
                                     T(w_hi[n % RING], k), T(w_lo[n % RING], k), k == 0, k == 1)
                last.then_inc(unit_used, 1)
            for u in range(6):
                n = UNIT0["uq"] + u
                unit_ready(n)
                for e in range(2):
                    j = 2 * u + e
                    bank_free("uq", j)
                    for k in range(3):
                        if j == 0:
                            k_ready("cq", k)
                        w = slice(k * 256 + e * P, k * 256 + (e + 1) * P)
                        last = three(bank[j % 4][:, :], w_hi[n % RING][:, w], w_lo[n % RING][:, w],
                                     T(a_hi, 2 + k), T(a_lo, 2 + k), k == 0, k == 2)
                last.then_inc(unit_used, 1)
            for t in range(4):
                pe.wait_ge(out_read, TILE0["uq"] + 8 + t + 1)
                pe.wait_ge(rope_t, 2 * t + 2)
                pe.matmul(bank[5][:, :], swap, T(q_rope, t), start=True, stop=True).then_inc(rope_sw, 1)
            pe.wait_ge(rope_done, 5)
            pe.wait_ge(out_read, TILE0["wo"])
            pe.wait_ge(cst2_landed, 16)

            def mla_scores(i):
                r = slice(64 * (i % 2), 64 * (i % 2) + 64)
                for b in range(NB):
                    w = (b + 1) * P
                    if i:
                        pe.wait_ge(mla_exp, NB * (i - 1) + b + 1)
                    pe.matmul(bank[b][:, 0:w], T(q_nope, i)[:, b * P:(b + 1) * P], T(k_nope, i)[:, 0:w],
                              start=True, stop=False)
                    pe.matmul(bank[b][:, w - P:w], cst_b[0:1, MASK_Q:MASK_Q + P], cst_b[0:1, MASK_K:MASK_K + P],
                              start=False, stop=False)
                    pe.matmul(bank[b][:, 0:w], T(q_rope, i // 2)[r, b * P:(b + 1) * P], k_rope[r, 0:w],
                              start=False, stop=True).then_inc(mla_sc, 1)

            mla_scores(0)
            for i in range(MLA_H):
                if i + 1 < MLA_H:
                    mla_scores(i + 1)
                pe.wait_ge(mla_pn, NB * (i + 1))
                if i:
                    pe.wait_ge(mla_ev, 2 * i)
                    pe.wait_ge(mla_ea, i)
                for kt, bk, c0 in ((0, 5, 0), (1, 6, 0), (3, 6, 3 * P), (2, 7, 0)):
                    for b in range(kt, NB):
                        o = P * b * (b + 1) // 2 + kt * P
                        c = c0 + (b - kt) * P
                        last = pe.transpose(bank[bk][:, c:c + P], prob[:, o:o + P], cst[:, IDENT:IDENT + P])
                    if kt != 1:
                        last.then_inc(mla_tr, 1)
                pe.wait_ge(mla_ev, 2 * (i + 1))
                pe.wait_ge(mla_ea, i + 1)
                pe.wait_ge(x_ready, SPLIT0["mla"] + i)
                for b in range(NB):
                    for kt, c0 in enumerate((0, SEQ, 2 * SEQ, SEQ + 3 * P)[:b + 1]):
                        c = c0 + (b - kt) * P
                        last = pe.matmul(T(bank[4], b, P), T(v_tok, kt, MLA_H * V_DIM)[:, i * P:(i + 1) * P],
                                         probT[:, c:c + P], start=(kt == 0), stop=(kt == b))
                last.then_inc(mla_pv, 1)
            tiles("wo", 8, a_hi, a_lo, "mla")
            stat("post1")
            feed_forward(1)

        @block.vector
        def _(dve):
            def lo(n, slot, i=None):
                if i is None:
                    if n >= N_UNITS:
                        return
                    dve.wait_ge(whi_ready, n + 1)
                else:
                    dve.wait_ge(whi_ready, 4 * i + (n + 1))
                dve.tensor_tensor(w_lo[slot][:, :], w_raw[slot][:, :], f(w_hi[slot][:, :]), ALU.subtract)\
                    .then_inc(wlo_ready, 1)

            def lo_ahead(n, i=None):
                n += AHEAD
                if isinstance(i, int):
                    n, i = n + 4 * i, None
                lo(n, n % RING, i)

            def unit_done(n, i=None):
                dve.wait_ge(unit_used, n + 1 if i is None else 4 * i + (n + 1))

            def x_lo(no, dst_lo, dst_hi, k, src, gain=None):
                dve.wait_ge(xhi_ready, no + 1)
                if gain is None:
                    ins = dve.tensor_tensor(T(dst_lo, k), src, f(T(dst_hi, k)), ALU.subtract)
                else:
                    ins = dve.scalar_tensor_tensor(T(dst_lo, k), src, gain, f(T(dst_hi, k)), ALU.mult, ALU.subtract)
                ins.then_inc(x_ready, 1)

            def recip(name, dst):
                s = STAT_NO[name]
                dve.wait_ge(root_ready, s + 1)
                dve.reciprocal(dst, root).then_inc(r_ready, 1)

            def scaled(name):
                dve.wait_ge(r_ready, STAT_NO[name] + 1)

            links = [0]

            def link(ins):
                links[0] += 1
                ins.then_inc(v_chain, 1)
                dve.wait_ge(v_chain, links[0])

            link(dve.memset(small[:, 60:61], EPS))
            link(dve.memset(small[:, 61:62], LN_EPS))
            dve.wait_ge(cst_landed, 64)
            for k in range(KD):
                x_lo(SPLIT0["mix"] + k, a_lo, a_hi, k, T(h, k), col("mix_norm", k))
                if k in (0, 2, 4):
                    lo(k // 2, k // 2)
            recip("mix", r_pre[:, :])
            dve.wait_ge(rtok_root, 1)
            dve.reciprocal(small[:, 4:8], small[:, 0:4]).then_inc(rtok_ready, 1)
            scaled("mix")
            dests = [T(z_q, 0), T(z_q, 1), T(z_k, 0), T(z_k, 1), z_lr[:, :]] + [T(z_r, t) for t in range(4)] + \
                [T(z_sq, t) for t in range(4)] + [z_sk[:, P:]]
            for j in range(14):
                lo_ahead(j)
                unit_done(j)
                dve.tensor_tensor(dests[j], bank[j % 4][:, :], r_pre[:, :], ALU.mult).then_inc(out_read, 1)
            lo_ahead(14)
            dve.wait_ge(rtok_ready, 1)
            unit_done(14)
            for b in range(NB):
                dve.tensor_scalar(T(z_vs, b, P), bank[(14 + b) % 4][:, 0:P], small[:, 4 + b:5 + b], None, ALU.mult)\
                    .then_inc(out_read, 1)
            for u in range(4):
                lo_ahead(15 + u)
            unit_done(18)
            for b in range(NB):
                dve.tensor_scalar(T(z_v, b), bank[(18 + b) % 4][:, :], small[:, 4 + b:5 + b], None, ALU.mult)\
                    .then_inc(out_read, 1)
            if stage < 2:
                for k in range(KD):
                    dve.tensor_copy(T(h, k), z_q[:, 0:SEQ] if k == 0 else z_k[:, 0:SEQ] if k == 1 else T(z_v, k % 4))\
                        .then_inc(out_ready, 1)
                return
            for t in range(5):
                name = f"sq{t}" if t < 4 else "sk"
                if t:
                    dve.wait_ge(q_normed, t)
                recip(name, r_post[:, :])
                scaled(name)
                x = T(z_sq, t) if t < 4 else z_sk[:, P:]
                dve.scalar_tensor_tensor(x, x, col("q_norm" if t < 4 else "k_norm"), r_post[:, :], ALU.mult, ALU.mult)\
                    .then_inc(q_normed, 1)
            dve.wait_ge(gla_l, 1)
            dve.scalar_tensor_tensor(gla_b[:, :], gla_b[:, :], 0.0, gla_e[:, :], ALU.min, ALU.subtract)\
                .then_inc(gla_ls, 1)
            dve.wait_ge(gla_ls, 1)
            for t in range(2):
                dve.tensor_tensor_scan(T(gla_b, t), cst_b[:, RESET:RESET + SEQ], T(gla_b, t), 0.0, ALU.mult, ALU.add)\
                    .then_inc(gla_cum, 1)
            dve.wait_ge(gla_cum, 2)
            chunks = gla_b[:, :].rearrange("p (n c) -> p n c", c=CHUNK)
            dve.tensor_tensor(gla_kd[:, :].rearrange("p (n c) -> p n c", c=CHUNK),
                              chunks[:, :, CHUNK - 1:CHUNK].broadcast_to([P, 2 * NCH, CHUNK]), chunks, ALU.subtract)\
                .then_inc(gla_cum, 1)
            dve.wait_ge(gla_exp, 1)
            dve.scalar_tensor_tensor(z_q[:, :], z_q[:, :], GLA_DK ** -0.5, gla_e[:, :], ALU.mult, ALU.mult)\
                .then_inc(gla_ops, 1)
            dve.wait_ge(gla_exp, 2)
            dve.tensor_tensor(gla_ke[:, :], gla_ke[:, :], z_k[:, :], ALU.mult).then_inc(gla_ops, 1)
            dve.wait_ge(gla_exp, 3)
            dve.tensor_tensor(gla_kd[:, :], gla_kd[:, :], z_k[:, :], ALU.mult).then_inc(gla_ops, 1)
            dve.wait_ge(p_zero, 3)
            for hd in range(GLA_H):
                dve.wait_ge(gla_pe, 3 + hd)
                a_t = gla_a[:, hd * SEQ:(hd + 1) * SEQ] if hd < 2 else gla_a23[:, (hd - 2) * SEQ:(hd - 1) * SEQ]
                dve.copy_predicated(a_t, cst_b[:, CAUSAL:CAUSAL + SEQ].bitcast(I32), bank[hd][:, :]).then_inc(gla_ev, 1)
            dve.wait_ge(gla_pe, 7)
            dve.tensor_copy(T(gla_kdt, 0), bank[5][:, :]).then_inc(gla_ev, 1)
            dve.wait_ge(gla_exp, 4)
            for t in range(2):
                dve.wait_ge(gla_pe, 9 + 2 * t + 1)
            for c in range(NCH - 1):
                for t in range(2):
                    cs = T(bank[2 * t + c % 2], c // 2, P)
                    s_new = gla_s[:, (t * NCH + c + 1) * GLA_DV:(t * NCH + c + 2) * GLA_DV]
                    if c == 0:
                        dve.tensor_copy(s_new, cs).then_inc(gla_ev, 1)
                    else:
                        s_old = gla_s[:, (t * NCH + c) * GLA_DV:(t * NCH + c + 1) * GLA_DV]
                        dve.wait_ge(gla_ev, 5 + 2 * (c - 1) + t + 1)
                        dve.scalar_tensor_tensor(s_new, s_old, small[:, 8 + t * NCH + c:9 + t * NCH + c], cs,
                                                 ALU.mult, ALU.add).then_inc(gla_ev, 1)
            dve.wait_ge(q_normed, 5)
            for hd in range(GLA_H):
                recip(f"gla{hd}", r_post[:, :])
                scaled(f"gla{hd}")
                link(dve.scalar_tensor_tensor(tmp[hd][:, 0:SEQ], bank[hd][:, :], col("gla_norm"), r_post[:, :],
                                              ALU.mult, ALU.mult))
                dve.wait_ge(silu_r, hd + 1)
                dve.tensor_tensor(tmp[hd][:, 0:SEQ], tmp[hd][:, 0:SEQ], T(z_r, hd), ALU.mult).then_inc(o_done, 1)
            dve.wait_ge(o_done, GLA_H)
            for hd in range(GLA_H):
                x_lo(SPLIT0["attn"] + hd, o_lo, o_hi, hd, tmp[hd][:, 0:SEQ])

            def swa_softmax_in(i):
                p = swa_p[i % 2]
                hd = swa_head(i)
                slope = 2.0 ** (-8.0 * (hd + 1) / SWA_H) * SWA_HD ** 0.5
                nm = small[:, 32:36] if i % 2 == 0 else small[:, 40:44]
                dve.wait_ge(swa_sc, i + 1)
                for e in range(2):
                    dve.scalar_tensor_tensor(T(p, e), cst_b[:, DIST + 256 * e:DIST + 256 * e + SEQ], slope,
                                             bank[2 * (i % 2) + e][:, :], ALU.mult, ALU.add).then_inc(swa_bias, 1)
                dve.wait_ge(swa_bias, 2 * (i + 1))
                link(dve.tensor_reduce(nm, p[:, :].rearrange("p (b k) -> p b k", b=NB), AX_X, ALU.max))
                dve.tensor_scalar(nm, nm, SWA_HD ** -0.5, col("sinks", hd), ALU.mult, ALU.max).then_inc(swa_mx, 1)
                dve.wait_ge(swa_mx, 2 * i + 1)
                dve.tensor_scalar(nm, nm, -1.0, None, ALU.mult).then_inc(swa_mx, 1)

            swa_softmax_in(0)
            for i in range(SWA_H):
                if i + 1 < SWA_H:
                    if i:
                        dve.wait_ge(swa_tr, 2 * i)
                    swa_softmax_in(i + 1)
                p, t = swa_p[i % 2], swa_pt[i % 2]
                den = small[:, 36:40] if i % 2 == 0 else small[:, 44:48]
                se = small[:, 48:52] if i % 2 == 0 else small[:, 52:56]
                dve.wait_ge(swa_se, i + 1)
                dve.wait_ge(swa_exp, NB * (i + 1))
                link(dve.tensor_tensor(den, den, se, ALU.add))
                link(dve.reciprocal(den, den))
                for b in range(NB):
                    dve.tensor_scalar(T(p, b, 256), T(p, b, 256), den[:, b:b + 1], None, ALU.mult).then_inc(swa_pn, 1)
                dve.wait_ge(swa_tr, 2 * i + 1)
                if i >= 2:
                    dve.wait_ge(swa_pv, i - 1)
                dve.tensor_copy(t[:, P:SEQ], bank[5][:, P:SEQ]).then_inc(swa_ev, 1)
                if i % 2:
                    x_lo(SPLIT0["attn"] + 4 + i // 2, o_lo, o_hi, 4 + i // 2, bank[7][:, :])

            for k in range(8):
                n = UNIT0["wout"] + k
                lo_ahead(n)
                unit_done(n)
                dve.tensor_tensor(T(h, k), T(h, k), bank[k % 4][:, :], ALU.add).then_inc(out_read, 1)
                x_lo(SPLIT0["ffn"] + k, a_lo, a_hi, k, T(h, k), col("ffn_norm", k))
            recip("ffn", r_pre[:, :])
            if stage < 3:
                for k in range(KD):
                    dve.tensor_copy(small[:, 24 + k:25 + k], small[:, 60:61]).then_inc(out_ready, 1)
                return

            def conv_col(i, j, half, tap):
                return col_at("conv", 16 * i + (8 * j + 4 * half + tap)) if not isinstance(i, int) else \
                    col("conv", 16 * i + 8 * j + 4 * half + tap)

            def up(name, split, first_pair, pairs):
                n0, x0 = UNIT0[name], SPLIT0[split]

                def body(i):
                    for j in range(2):
                        pr = first_pair + j + 1
                        for half in range(2):
                            lo_ahead(n0 + 2 * j + half, i)
                            unit_done(n0 + 2 * j + half, i)
                            dve.tensor_tensor(tmp[half][:, 2:2 + SEQ], bank[2 * j + half][:, :], r_pre[:, :],
                                              ALU.mult).then_inc(out_read, 1)
                        for half in range(2):
                            dve.wait_ge(tap_mid, 4 * i + (2 * (pr - 1) + half + 1))
                            dve.scalar_tensor_tensor(tmp[2 + half][:, 0:SEQ], tmp[half][:, 1:1 + SEQ],
                                                     conv_col(i, first_pair + j, half, 1), tmp[2 + half][:, 0:SEQ],
                                                     ALU.mult, ALU.add).then_inc(tap_one, 1)
                        for half in range(2):
                            dve.wait_ge(tap_one, 4 * i + (2 * (pr - 1) + half + 1))
                            dve.scalar_tensor_tensor(tmp[2 + half][:, 0:SEQ], tmp[half][:, 0:SEQ],
                                                     conv_col(i, first_pair + j, half, 0), tmp[2 + half][:, 0:SEQ],
                                                     ALU.mult, ALU.add).then_inc(taps_a if half == 0 else taps_b, 1)
                        no = x0 + j
                        dve.wait_ge(xhi_ready, 2 * i + (no + 1))
                        dve.tensor_tensor(at(g_lo, 2 * i + j), tmp[4][:, 0:SEQ], f(at(g_hi, 2 * i + j)), ALU.subtract)\
                            .then_inc(x_ready, 1)
                looped(dve, pairs // 2, body)

            def down(name, units, final):
                n0, t0 = UNIT0[name], TILE0[name]
                for n in range(n0, n0 + units // 2):
                    lo_ahead(n)
                for g in range(2):
                    if g == 1:
                        for n in range(n0 + units // 2, n0 + units):
                            lo_ahead(n)
                    unit_done(n0 + (g + 1) * units // 2 - 1)
                    for j in range(4):
                        k = 4 * g + j
                        dve.tensor_tensor(T(h, k), T(h, k), bank[4 * g + j][:, :], ALU.add)\
                            .then_inc(out_read, 1)
                        if final:
                            x_lo(SPLIT0["pre0"] + k, a_lo, a_hi, k, T(h, k), col("pre", k))

            scaled("ffn")
            dve.wait_ge(p_zero, 5)
            up("upA", "prodA", 0, PAIRS_A)
            down("downA", PAIRS_A, False)
            up("upB", "prodB", PAIRS_A, PAIRS_B)
            down("downB", PAIRS_B, True)
            recip("pre0", r_pre[:, :])
            if stage < 4:
                for k in range(KD):
                    dve.tensor_copy(small[:, 24 + k:25 + k], small[:, 60:61]).then_inc(out_ready, 1)
                return
            scaled("pre0")
            dve.wait_ge(p_zero, 5 + KD)
            for k in range(KD):
                n = UNIT0["pw1"] + 2 * k
                for e in range(2):
                    lo_ahead(n + e)
                    unit_done(n + e)
                    if k:
                        dve.wait_ge(u_ready, k)
                    dve.tensor_tensor(tmp[e][:, 0:SEQ], bank[(2 * k + e) % 4][:, :], r_pre[:, :], ALU.mult)\
                        .then_inc(out_read, 1)
                dve.wait_ge(ug_sig, k + 1)
                u = u_pad[:, k * UW + CONV_W - 1:(k + 1) * UW]
                dve.scalar_tensor_tensor(u, tmp[0][:, 0:SEQ], col("b_pw1", k), tmp[1][:, 0:SEQ], ALU.add, ALU.mult)\
                    .then_inc(u_ready, 1)
                if k % 2:
                    dve.wait_ge(u_ready, k + 1)
                    base = (k // 2) * 2 * CONV_W
                    for tap in range(CONV_W):
                        for e in range(2):
                            c = k - 1 + e
                            src = u_pad[:, c * UW + tap:c * UW + tap + SEQ]
                            wc = col("w_dw", c * CONV_W + tap)
                            if tap:
                                dve.wait_ge(dw_chain, base + 2 * tap + e - 1)
                            if tap == 0:
                                dve.tensor_scalar(T(cv, c), src, wc, col("b_dw", c), ALU.mult, ALU.add)\
                                    .then_inc(dw_chain, 1)
                            else:
                                dve.scalar_tensor_tensor(T(cv, c), src, wc, T(cv, c), ALU.mult, ALU.add)\
                                    .then_inc(dw_chain, 1)
            dve.wait_ge(root_ready, STAT_NO["ln_mean"] + 1)
            dve.tensor_copy(r_pre[:, :], root).then_inc(r_ready, 1)
            scaled("ln_mean")
            for k in range(KD):
                dve.tensor_tensor(T(cv, k), T(cv, k), r_pre[:, :], ALU.subtract).then_inc(cen_ready, 1)
            recip("ln_var", r_post[:, :])
            scaled("ln_var")
            for k in range(KD):
                dve.scalar_tensor_tensor(T(cv, k), T(cv, k), col("ln_g", k), r_post[:, :], ALU.mult, ALU.mult)\
                    .then_inc(ln_ready, 1)
            for k in range(KD):
                x_lo(SPLIT0["conv"] + k, a_lo, a_hi, k, T(cv, k))
            for k in range(KD):
                n = UNIT0["pw2"] + k
                lo_ahead(n)
                unit_done(n)
                dve.tensor_scalar(T(m, k), bank[k % 4][:, :], col("b_pw2", k), None, ALU.add).then_inc(out_read, 1)

            def post_norm(stat, gain, g0, h0, split=None, next_gain=None, ng0=0):
                recip(stat, r_post[:, :])
                scaled(stat)
                for k in range(KD):
                    link(dve.scalar_tensor_tensor(T(m, k), T(m, k), col(gain, g0 + k), r_post[:, :],
                                                  ALU.mult, ALU.mult))
                    dve.tensor_tensor(T(h, k), T(h, k), T(m, k), ALU.add)\
                        .then_inc(h_ready if split else out_ready, 1)
                    if split and k:
                        x_lo(SPLIT0[split] + k - 1, a_lo, a_hi, k - 1, T(h, k - 1), col(next_gain, ng0 + k - 1))
                if split:
                    x_lo(SPLIT0[split] + KD - 1, a_lo, a_hi, KD - 1, T(h, KD - 1), col(next_gain, ng0 + KD - 1))

            post_norm("post0", "post", 0, H0["post0"], "ffpre0", "ffpre", 0)
            recip("ffpre0", r_pre[:, :])
            if stage < 5:
                for k in range(KD):
                    dve.tensor_copy(small[:, 24 + k:25 + k], small[:, 60:61]).then_inc(out_ready, 1)
                return

            def feed_forward(layer):
                scaled(f"ffpre{layer}")
                for half in range(2):
                    c = "ab"[half]
                    n0, t0, x0 = UNIT0[f"ff1{c}{layer}"], TILE0[f"ff1{c}{layer}"], SPLIT0[f"hid{layer}{c}"]

                    def body(i):
                        for j in range(4):
                            lo_ahead(n0 + j, i)
                            unit_done(n0 + j, i)
                            dve.scalar_tensor_tensor(tmp[j % 2][:, 0:SEQ], bank[j][:, :], 0.0, r_pre[:, :],
                                                     ALU.max, ALU.mult).then_inc(out_read, 1)
                            dve.wait_ge(hid_sq, 4 * i + (32 * layer + 16 * half + j + 1))
                            dve.wait_ge(xhi_ready, 4 * i + (x0 + j + 1))
                            dve.tensor_tensor(at(g_lo, 4 * i + j), tmp[2 + j % 2][:, 0:SEQ], f(at(g_hi, 4 * i + j)),
                                              ALU.subtract).then_inc(x_ready, 1)
                    looped(dve, 4, body)
                    name = f"ff2{c}{layer}"
                    n0 = UNIT0[name]

                    def first(i):
                        for j in range(2):
                            lo_ahead(n0 + 2 * j, i)
                            lo_ahead(n0 + 2 * j + 1, i)
                            unit_done(n0 + 2 * j + 1, i)
                            dve.tensor_copy(at(m, 2 * i + j), bank[j][:, :]).then_inc(out_read, 1)

                    if half == 0:
                        looped(dve, 4, first)
                        dve.wait_ge(out_read, TILE0[name] + 8)
                    else:
                        for k in range(KD):
                            lo_ahead(n0 + 2 * k)
                            lo_ahead(n0 + 2 * k + 1)
                            unit_done(n0 + 2 * k + 1)
                            dve.tensor_tensor(T(m, k), T(m, k), bank[k % 2][:, :], ALU.add).then_inc(out_read, 1)

            feed_forward(0)
            if stage < 6:
                post_norm("ffpost0", "ffpost", 0, H0["ffpost0"])
                return
            post_norm("ffpost0", "ffpost", 0, H0["ffpost0"], "kvpre", "kv_in", 0)
            for k in range(KD):
                x_lo(SPLIT0["pre1"] + k, b_lo, b_hi, k, T(h, k), col("pre", 8 + k))
            recip("pre1", r_pre[:, :])
            scaled("pre1")
            dests = [T(c_kv, 0), T(c_kv, 1), k_rope, T(c_q, 0), T(c_q, 1), T(c_q, 2)]
            for j in range(6):
                n = UNIT0["dkv"] + j
                lo_ahead(n)
                unit_done(n)
                dve.tensor_tensor(dests[j], bank[j % 3][:, :], r_pre[:, :], ALU.mult).then_inc(out_read, 1)

            def rotate(x, no):
                dve.wait_ge(rope_sw, no + 1)
                if no:
                    dve.wait_ge(rope_done, no)
                dve.tensor_tensor(tmp[0][:, 0:SEQ], bank[5][:, :], cst_b[:, SIN:SIN + SEQ], ALU.mult)\
                    .then_inc(rope_t, 1)
                dve.tensor_tensor(tmp[1][:, 0:SEQ], x, cst_b[:, COS:COS + SEQ], ALU.mult).then_inc(rope_t, 1)
                dve.wait_ge(rope_t, 2 * no + 2)
                dve.tensor_tensor(x, tmp[0][:, 0:SEQ], tmp[1][:, 0:SEQ], ALU.add).then_inc(rope_done, 1)

            dve.wait_ge(cst2_landed, 16)
            rotate(k_rope, 0)
            for stat, gain, tiles, first, base in (("ckv", "ckv_norm", 2, 0, 0), ("cq", "cq_norm", 3, 2, 2)):
                recip(stat, r_post[:, :])
                scaled(stat)
                for k in range(tiles):
                    dve.scalar_tensor_tensor(T(m, first + k), T(m, first + k), col(gain, k), r_post[:, :],
                                             ALU.mult, ALU.mult).then_inc(c_normed, 1)
                for k in range(tiles):
                    x_lo(SPLIT0["ckv"] + base + k, a_lo, a_hi, first + k, T(m, first + k))
            for u in range(2):
                n = UNIT0["uk"] + u
                lo_ahead(n)
                unit_done(n)
                for j in range(4):
                    dve.tensor_copy(T(k_nope, 4 * u + j), bank[j][:, :]).then_inc(out_read, 1)
            for u in range(2):
                n = UNIT0["uv"] + u
                lo_ahead(n)
                unit_done(n)
                for b in range(NB):
                    dve.tensor_copy(T(v_tok, b, MLA_H * V_DIM)[:, u * SEQ:(u + 1) * SEQ], bank[b][:, :])\
                        .then_inc(out_read, 1)
            for u in range(6):
                n = UNIT0["uq"] + u
                lo_ahead(n)
                unit_done(n)
                for e in range(2):
                    j = 2 * u + e
                    dst = T(q_nope, j) if j < 8 else T(q_rope, j - 8)
                    dve.tensor_copy(dst, bank[j % 4][:, :]).then_inc(out_read, 1)
            for t in range(4):
                rotate(T(q_rope, t), 1 + t)

            def mla_max(i):
                nm = small[:, 32:36] if i % 2 == 0 else small[:, 40:44]
                for b in range(NB):
                    dve.wait_ge(mla_sc, NB * i + b + 1)
                    dve.tensor_reduce(nm[:, b:b + 1], bank[b][:, 0:(b + 1) * P], AX_X, ALU.max).then_inc(mla_mx, 1)
                dve.wait_ge(mla_mx, 5 * i + 4)
                dve.tensor_scalar(nm, nm, -MLA_SCALE, None, ALU.mult).then_inc(mla_mx, 1)

            mla_max(0)
            for i in range(MLA_H):
                den = small[:, 36:40] if i % 2 == 0 else small[:, 44:48]
                dve.wait_ge(mla_exp, NB * (i + 1))
                link(dve.reciprocal(den, den))
                for b in range(NB):
                    o = P * b * (b + 1) // 2
                    x = prob[:, o:o + (b + 1) * P]
                    dve.tensor_scalar(x, x, den[:, b:b + 1], None, ALU.mult).then_inc(mla_pn, 1)
                if i + 1 < MLA_H:
                    mla_max(i + 1)
                dve.wait_ge(mla_tr, 3 * i + 1)
                if i:
                    dve.wait_ge(mla_pv, i)
                dve.tensor_copy(probT[:, 0:SEQ], bank[5][:, :]).then_inc(mla_ev, 1)
                dve.wait_ge(mla_tr, 3 * i + 3)
                dve.tensor_copy(probT[:, 2 * SEQ:2 * SEQ + 2 * P], bank[7][:, 0:2 * P]).then_inc(mla_ev, 1)
                x_lo(SPLIT0["mla"] + i, a_lo, a_hi, i, bank[4][:, :])
            for k in range(KD):
                n = UNIT0["wo"] + k
                lo_ahead(n)
                unit_done(n)
                dve.tensor_copy(T(m, k), bank[k % 4][:, :]).then_inc(out_read, 1)
            post_norm("post1", "post", 8, H0["post1"], "ffpre1", "ffpre", 8)
            recip("ffpre1", r_pre[:, :])
            feed_forward(1)
            post_norm("ffpost1", "ffpost", 8, None)


def _tiles(w):
    k, n = w.shape
    return w.reshape(k // P, P, n // P, P).transpose(2, 1, 0, 3).reshape(n // P, P, (k // P) * P)


def _pairs(w, kt, width):
    k, n = w.shape
    u = w.reshape(k // (kt * P), kt, P, n // width, width).transpose(3, 0, 2, 1, 4)
    return u.reshape(-1, P, kt * width)


def _stream(a):
    def pad(u):
        out = np.zeros((u.shape[0], P, UNIT), np.float32)
        out[:, :, :u.shape[2]] = u
        return out

    w_in = a["w_in"][0]
    qk = GLA_H * GLA_DK
    vw = GLA_H * GLA_DV
    o = np.cumsum([0, qk, qk, vw, vw, GLA_RANK, SWA_H * SWA_HD, SWA_KV * SWA_HD, SWA_KV * SWA_HD])
    gq, gk, gv, gr, glr, sq, sk, sv = (w_in[:, o[i]:o[i + 1]] for i in range(8))
    low = np.zeros((D, P), np.float32)
    low[:, :GLA_RANK] = glr
    sqp = sq.reshape(D, 2, 4, SWA_HD).transpose(0, 2, 1, 3).reshape(D, SWA_H * SWA_HD)
    units = [_tiles(gq), _tiles(gk), _tiles(low), _tiles(gr), _tiles(sqp), _tiles(sk), _tiles(sv), _pairs(gv, 2, 512)]
    w_out = a["w_out"][0]
    swa_rows = w_out[vw:].reshape(2, 4, SWA_HD, D).transpose(1, 0, 2, 3).reshape(SWA_H * SWA_HD, D)
    units.append(_tiles(np.concatenate([w_out[:vw], swa_rows])))
    up = _tiles(a["w_up"][0])
    down = a["w_down"][0]
    both = np.stack([up[:UP_PAIRS], up[UP_PAIRS:]], 1)
    units += [both[:PAIRS_A].reshape(-1, P, UNIT), _pairs(down[:PAIRS_A * P], 2, 512)]
    units += [both[PAIRS_A:].reshape(-1, P, UNIT), _pairs(down[PAIRS_A * P:], 2, 512)]
    pw1 = _tiles(a["conv_w_pw1_2"][0])
    units.append(np.stack([pw1[:KD], pw1[KD:]], 1).reshape(-1, P, UNIT))
    units.append(_tiles(a["conv_w_pw2_2"][0]))

    def ff(layer):
        w1 = _tiles(a["w_ff1_2"][layer])
        w2 = a["w_ff2_2"][layer]
        out = []
        for half in range(2):
            w = w2[half * 2048:(half + 1) * 2048].reshape(2, 1024, D)
            out += [w1[half * 16:(half + 1) * 16],
                    np.stack([_tiles(w[0]), _tiles(w[1])], 1).reshape(-1, P, UNIT)]
        return out
    units += ff(0)
    kr = a["kv_w_kr_2"]
    uq = a["mla_w_uq_2"][0].reshape(Q_RANK, MLA_H, NOPE + ROPE)
    units += [_tiles(a["kv_w_dkv_2"]), _tiles(np.concatenate([kr, kr], 1)), _tiles(a["mla_w_dq_2"][0])]
    units += [_pairs(a["kv_w_uk_2"], 2, 512), _pairs(a["kv_w_uv_2"], 2, 512)]
    uq2 = np.concatenate([uq[:, :, :NOPE].reshape(Q_RANK, -1), uq[:, :, NOPE:].reshape(Q_RANK, -1)], 1)
    units.append(pad(_pairs(uq2, 3, 256)))
    units.append(_tiles(a["mla_w_o_2"][0]))
    units += ff(1)
    out = np.concatenate(units)
    assert out.shape == (N_UNITS, P, UNIT)
    return out.reshape(N_UNITS * P, UNIT)


def _vectors(a):
    def c(v):
        return v.reshape(-1, P).T

    conv = np.concatenate([a["conv_w"][0], a["conv_b"]], 0)
    conv = conv.reshape(4, 2, UP_PAIRS, P).transpose(3, 2, 1, 0).reshape(P, -1)
    dw = a["conv_w_dw_2"][0].reshape(CONV_W, KD, P).transpose(2, 1, 0).reshape(P, -1)
    return np.concatenate([
        c(a["mix_norm"][0]), c(a["b_alpha"][0]), c(a["gla_norm"][0]), c(np.tile(a["q_norm"][0], 2)),
        c(np.tile(a["k_norm"][0], 2)), np.broadcast_to(a["sinks"], (P, SWA_H)), c(a["ffn_norm"][0]), conv,
        c(a["mix_pre_g_2"]), c(a["mix_post_g_2"]), c(a["ffn_pre_g_2"]), c(a["ffn_post_g_2"]), c(a["conv_b_pw1_2"][0]),
        dw, c(a["conv_b_dw_2"][0]), c(a["conv_ln_g_2"][0]), c(a["conv_ln_b_2"][0]), c(a["conv_b_pw2_2"][0]),
        c(a["kv_in_g_2"]), c(a["kv_norm_g_2"]), c(a["mla_q_norm_g_2"][0])], 1)


def _consts():
    i = np.arange(P)
    both = np.concatenate([np.eye(P), np.ones((P, P)), (i[:, None] // 64) == (i[None, :] // 64),
                           i[:, None] == (i[None, :] ^ 32)], 1).astype(np.float32)
    one = np.zeros((P, N_CONST), np.float32)
    causal = (i[:, None] <= i[None, :]) & (i[:, None] // CHUNK == i[None, :] // CHUNK)
    one[:, CAUSAL:CAUSAL + SEQ] = np.tile(causal, (1, NB))
    one[:, RESET:RESET + SEQ] = (np.arange(SEQ) % CHUNK != 0)
    dist = WINDOW + i[:, None] - np.arange(2 * WINDOW)[None, :]
    seen = (dist >= 0) & (dist < WINDOW)
    d = np.where(seen, -dist, NEG).astype(np.float32)
    first = np.where(np.arange(2 * WINDOW)[None, :] >= WINDOW, d, np.float32(NEG))
    one[:, DIST:DIST + 768] = np.concatenate([first, d, d], 1)
    two = np.zeros((P, N_CONST), np.float32)
    half = ROPE // 2
    inv = (1.0 / (np.float32(10000.0) ** (np.arange(0, ROPE, 2, dtype=np.float32) / np.float32(ROPE)))).astype(np.float32)
    ang = np.arange(SEQ, dtype=np.float32)[:, None] * inv[None, :]
    cos, sin = np.cos(ang).T, np.sin(ang).T
    two[:, COS:COS + SEQ] = np.tile(cos, (P // half, 1))
    two[:, SIN:SIN + SEQ] = np.tile(np.concatenate([-sin, sin]), (2, 1))
    two[:, MASK_Q:MASK_Q + P] = i[None, :] < CHUNK
    two[:, MASK_K:MASK_K + P] = np.where(i[None, :] >= CHUNK, NEG, 0.0)
    return both, one, two


def kernel(**inputs):
    import concourse.bacc as _bacc
    from concourse import mybir as _mybir
    from concourse.bass_utils import run_bass_kernel_spmd as _run

    a = {k: np.asarray(v) for k, v in inputs.items()}
    both, one, two = _consts()
    w_alpha = np.zeros((P, 256), np.float32)
    w_alpha[:GLA_RANK] = a["w_alpha2"][0]
    arrays = {
        "in_xT": np.ascontiguousarray(a["x"][0].T), "in_stream": _stream(a), "in_vectors": _vectors(a),
        "in_w_alpha": w_alpha, "in_consts": both, "in_consts1": one, "in_consts2": two,
    }
    arrays = {k: np.ascontiguousarray(v) for k, v in arrays.items()}
    nc = _bacc.Bacc("TRN2", target_bir_lowering=False, num_devices=1)
    args = [nc.dram_tensor(k, v.shape, _mybir.dt.float32, kind="ExternalInput").ap() for k, v in arrays.items()]
    out = nc.dram_tensor("out_0", (D, SEQ), _mybir.dt.float32, kind="ExternalOutput").ap()
    program(nc, *args, out)
    r = _run(nc, [arrays], core_ids=[0])
    got = r.results[0]["out_0"]
    return np.ascontiguousarray(got.T)[None]
```

```python
from contextlib import ExitStack

import numpy as np

import concourse.bass as bass
from concourse import mybir

F32 = mybir.dt.float32
F32R = mybir.dt.float32r
I32 = mybir.dt.int32
ALU = mybir.AluOpType
ACT = mybir.ActivationFunctionType
AX_X = mybir.AxisListType.X

P = 128
SEQ = 512
D = 1024
KD = D // P
UNIT = 1024
RING = 4
AHEAD = 3
EPS = 1e-6
LN_EPS = 1e-5
NEG = -1e30

GLA_H, GLA_DK, GLA_DV, GLA_RANK, CHUNK = 4, 64, 128, 16, 64
SWA_H, SWA_KV, SWA_HD, WINDOW = 8, 2, 64, 128
D_FF = 2816
UP_PAIRS = D_FF // P
PAIRS_A = 12
PAIRS_B = UP_PAIRS - PAIRS_A
D_FF_2 = 4096
CONV_W = 31
TAPS_PE = [12, 12, 12, 16]
TAPS_POOL = 2
MLA_H, NOPE, ROPE, V_DIM, Q_RANK, KV_RANK = 8, 128, 64, 128, 384, 256
MLA_SCALE = float(NOPE + ROPE) ** -0.5
NB = SEQ // P
NCH = SEQ // CHUNK
USE_LOOPS = True

PRODUCTS = [
    ("z", 19, 22), ("wout", 8, 8),
    ("upA", 2 * PAIRS_A, 2 * PAIRS_A), ("downA", PAIRS_A, 8),
    ("upB", 2 * PAIRS_B, 2 * PAIRS_B), ("downB", PAIRS_B, 8),
    ("pw1", 16 + sum(TAPS_PE) // 4, 16), ("pw2", 8, 8),
    ("ff1a0", 16, 16), ("ff2a0", 16, 8), ("ff1b0", 16, 16), ("ff2b0", 16, 8),
    ("dkv", 3, 3), ("dq", 3, 3), ("uk", 2, 8), ("uv", 2, 8), ("uq", 6, 12), ("wo", 8, 8),
    ("ff1a1", 16, 16), ("ff2a1", 16, 8), ("ff1b1", 16, 16), ("ff2b1", 16, 8),
]
UNIT0, TILE0 = {}, {}
_u = _t = 0
for _name, _units, _tiles in PRODUCTS:
    UNIT0[_name], TILE0[_name] = _u, _t
    _u, _t = _u + _units, _t + _tiles
N_UNITS = _u

SPLITS = [
    ("mix", 8), ("attn", 8), ("ffn", 8), ("prodA", PAIRS_A), ("prodB", PAIRS_B), ("pre0", 8), ("conv", 8),
    ("ffpre0", 8), ("hid0a", 16), ("hid0b", 16), ("kvpre", 8), ("pre1", 8), ("ckv", 2), ("cq", 3), ("mla", 8),
    ("ffpre1", 8), ("hid1a", 16), ("hid1b", 16),
]
SPLIT0 = {}
_x = 0
for _name, _n in SPLITS:
    SPLIT0[_name] = _x
    _x += _n

STATS = [
    ("mix", 8), ("ffn", 8), ("pre0", 8), ("ln_var", 8), ("post0", 8), ("ffpre0", 8), ("ffpost0", 8),
    ("pre1", 8), ("ckv", 2), ("cq", 3), ("post1", 8), ("ffpre1", 8), ("ffpost1", 8),
]
STAT_NO, SQ0, ADD0, STAT_TILES = {}, {}, {}, {}
_s = _a = 0
for _i, (_name, _n) in enumerate(STATS):
    STAT_NO[_name], SQ0[_name], ADD0[_name], STAT_TILES[_name] = _i, _s, _a, _n
    _s, _a = _s + _n, _a + max(_n - 2, 0)

R_NO = {name: i for i, name in enumerate(n for n, _ in STATS if "post" not in n and n != "ln_var")}

RC_SWA = 4 * len(STATS)
RC_GLA = RC_SWA + 40
N_RC = RC_GLA + 16

VECTORS = [
    ("mix_norm", 8), ("b_alpha", 2), ("gla_norm", 1), ("q_norm", 1), ("k_norm", 1), ("sinks", 8), ("ffn_norm", 8),
    ("conv", 4 * 2 * UP_PAIRS), ("pre", 16), ("post", 16), ("ffpre", 16), ("ffpost", 16), ("b_pw1", 16),
    ("w_dw", 8 * CONV_W), ("b_dw", 8), ("ln_g", 8), ("ln_b", 8), ("b_pw2", 8), ("kv_in", 8), ("ckv_norm", 2),
    ("cq_norm", 3),
]
COL0 = {}
_c = 0
for _name, _n in VECTORS:
    COL0[_name] = _c
    _c += _n
N_COLS = _c

IDENT, ONES, MEAN, SWAP, HALVES = 0, P, 2 * P, 3 * P, 4 * P
N_CST = 4 * P + 2
CAUSAL, RESET, DIST = 0, SEQ, 2 * SEQ
COS, SIN, MASK_Q, MASK_K = 0, SEQ, 2 * SEQ, 2 * SEQ + P
N_CONST = 2 * SEQ + 3 * 256


def program(nc, xT, stream, vectors, w_alpha, consts, consts1, consts2, outT, stage=99):
    ctx = ExitStack()
    with ctx:
        def sb(name, shape, dtype=F32, where=ctx):
            return where.enter_context(nc.sbuf_tensor(name, shape, dtype))

        def sem(name):
            return ctx.enter_context(nc.semaphore(name))

        h = sb("h", [P, KD * SEQ])
        m = sb("m", [P, KD * SEQ])
        w_raw = [sb(f"w_raw{i}", [P, UNIT]) for i in range(RING)]
        w_hi = [sb(f"w_hi{i}", [P, UNIT], F32R) for i in range(RING)]
        w_lo = [sb(f"w_lo{i}", [P, UNIT], F32R) for i in range(RING)]
        cst = sb("cst", [P, N_CST])
        cst_b = sb("cst_b", [P, N_CONST])
        cols = sb("cols", [P, N_COLS])
        TW = SEQ + 8
        tmp = [sb(f"tmp{i}", [P, TW]) for i in range(6)]
        ssum = sb("ssum", [P, SEQ])
        r_pre = sb("r_pre", [P, SEQ])
        r_post = sb("r_post", [P, SEQ])
        small = sb("small", [P, 64 + len(STATS) + 2])
        rms = sb("rms", [P, N_RC])
        r_tok = sb("r_tok", [P, N_RC])
        b_last = sb("b_last", [P, 2 * NCH])
        decay = sb("decay", [P, 2 * NCH])
        sq_buf = [tmp[4][:, 0:SEQ], tmp[5][:, 0:SEQ]]

        at_a = ExitStack()
        a_hi = sb("a_hi", [P, KD * SEQ], F32R, at_a)
        a_lo = sb("a_lo", [P, KD * SEQ], F32R, at_a)
        at_a.close()
        at_a = ExitStack()
        gla_kdt = sb("gla_kdt", [P, 2 * SEQ], where=at_a)
        gla_s = sb("gla_s", [P, 2 * NCH * GLA_DV], where=at_a)
        gla_a = sb("gla_a", [P, GLA_H * SEQ], where=at_a)
        at_a.close()
        sb("a_region", [P, 2 * KD * SEQ])

        big = ExitStack()
        os_hi = sb("os_hi", [P, 4 * SEQ], F32R, big)
        os_lo = sb("os_lo", [P, 4 * SEQ], F32R, big)
        at_o = ExitStack()
        og_hi = sb("og_hi", [P, 4 * SEQ], F32R, at_o)
        og_lo = sb("og_lo", [P, 4 * SEQ], F32R, at_o)
        at_o.close()
        swa_p = [sb(f"swa_p{i}", [P, NB * 256], where=big) for i in range(2)]
        swa_pt = [sb(f"swa_pt{i}", [P, NB * 256], where=big) for i in range(2)]
        z_q = sb("z_q", [P, 2 * SEQ], where=big)
        z_k = sb("z_k", [P, 2 * SEQ], where=big)
        z_sq = sb("z_sq", [P, 4 * SEQ], where=big)
        z_v = sb("z_v", [P, NB * SEQ], where=big)
        z_sk = sb("z_sk", [P, P + SEQ], where=big)
        z_vs = sb("z_vs", [P, NB * P], where=big)
        z_lr = sb("z_lr", [P, SEQ], where=big)
        w_al = sb("w_al", [P, 256], where=big)
        big.close()
        z_r = m[:, 0:4 * SEQ]
        gla_b, gla_e = m[:, 4 * SEQ:6 * SEQ], m[:, 6 * SEQ:8 * SEQ]
        big = ExitStack()
        g_hi = sb("g_hi", [P, 16 * SEQ], F32R, big)
        g_lo = sb("g_lo", [P, 16 * SEQ], F32R, big)
        big.close()
        big = ExitStack()
        UW = SEQ + CONV_W - 1
        u_pad = sb("u_pad", [P, KD * UW], where=big)
        cv = sb("cv", [P, KD * SEQ], where=big)
        u_hi = sb("u_hi", [P, 4 * UW], F32R, big)
        u_lo = sb("u_lo", [P, 4 * UW], F32R, big)
        big.close()
        big = ExitStack()
        k_nope = sb("k_nope", [P, MLA_H * SEQ], where=big)
        v_tok = sb("v_tok", [P, NB * MLA_H * V_DIM], where=big)
        small_mla = ExitStack()
        b_hi = sb("b_hi", [P, KD * SEQ], F32R, small_mla)
        b_lo = sb("b_lo", [P, KD * SEQ], F32R, small_mla)
        small_mla.close()
        small_mla = ExitStack()
        q_nope = sb("q_nope", [P, MLA_H * SEQ], where=small_mla)
        q_rope = sb("q_rope", [P, 4 * SEQ], where=small_mla)
        small_mla.close()
        big.close()
        sb("big_region", [P, 32 * SEQ])
        c_kv, c_q = m[:, 0:2 * SEQ], m[:, 2 * SEQ:5 * SEQ]
        k_rope = m[:, 7 * SEQ:8 * SEQ]
        NP_ = P * NB * (NB + 1) // 2
        prob = m[:, 0:NP_]
        probT = m[:, NP_:2 * NP_]

        bank = [ctx.enter_context(nc.psum_tensor(f"bank{i}", [P, SEQ], F32)) for i in range(8)]

        h_landed = [sem(f"h_landed{k}") for k in range(KD)]
        vec_landed = sem("vec_landed")
        cst_landed = sem("cst_landed")
        cst2_landed = sem("cst2_landed")
        w_landed = [sem(f"w_landed{i}") for i in range(RING)]
        whi_ready = sem("whi_ready")
        wlo_ready = sem("wlo_ready")
        unit_used = sem("unit_used")
        out_read = sem("out_read")
        xhi_ready = sem("xhi_ready")
        x_ready = sem("x_ready")
        sq_ready = sem("sq_ready")
        sum_added = sem("sum_added")
        stat_done = sem("stat_done")
        r_ready = sem("r_ready")
        out_stored = sem("out_stored")

        def T(t, k, w=SEQ):
            return t[:, k * w:(k + 1) * w]

        def col(name, k=0):
            c = COL0[name] + k
            return cols[:, c:c + 1]

        def col_at(name, k):
            return cols[:, bass.ds(COL0[name] + k, 1)]

        def f(x):
            return x.bitcast(F32)

        def at(t, i, w=SEQ):
            return t[:, bass.ds(i * w, w)] if not isinstance(i, int) else t[:, i * w:(i + 1) * w]

        def swa_head(i):
            return i // 2 + 4 * (i % 2)

        def swa_sq_buf(n):
            return ssum[:, :] if n % 3 == 0 else sq_buf[n % 3 - 1]

        def gla_sq_buf(hd):
            return (ssum[:, :], sq_buf[0], sq_buf[1], r_post[:, :])[hd]

        def r_cols(c, width=P):
            return r_tok[:, c:c + 1].broadcast_to([P, width])

        def swa_bias_t(i):
            return tmp[4 + i % 2][:, 0:SEQ]

        def looped(eng, n, body, first=0):
            if USE_LOOPS:
                with eng.Fori(first, n) as i:
                    body(i)
            else:
                for i in range(first, n):
                    body(i)

        out_ready = sem("out_ready")
        rms_ready = sem("rms_ready")
        r_tok_ready = sem("r_tok_ready")
        spread_done = sem("spread_done")
        mean_done = sem("mean_done")
        swa_sq = sem("swa_sq")
        swa_sums = sem("swa_sums")
        swa_rms = sem("swa_rms")
        swa_r = sem("swa_r")
        sk_spread = sem("sk_spread")
        swa_dist = sem("swa_dist")
        gla_sq = sem("gla_sq")
        gla_sums = sem("gla_sums")
        gla_r = sem("gla_r")
        v_chain = sem("v_chain")
        a_chain = sem("a_chain")
        p_zero = sem("p_zero")
        gla_y = sem("gla_y")
        gla_l = sem("gla_l")
        gla_ls = sem("gla_ls")
        gla_cum = sem("gla_cum")
        gla_exp = sem("gla_exp")
        gla_ops = sem("gla_ops")
        gla_blast = sem("gla_blast")
        gla_logit = sem("gla_logit")
        gla_scores = sem("gla_scores")
        gla_masked = sem("gla_masked")
        gla_tr = sem("gla_tr")
        gla_tr_read = sem("gla_tr_read")
        gla_cs = sem("gla_cs")
        gla_state = sem("gla_state")
        gla_o = sem("gla_o")
        gla_rms = sem("gla_rms")
        gla_gated = sem("gla_gated")
        silu_r = sem("silu_r")
        o_done = sem("o_done")
        k_normed = sem("k_normed")
        swa_sc = sem("swa_sc")
        swa_bias = sem("swa_bias")
        swa_mx = sem("swa_mx")
        swa_exp = sem("swa_exp")
        swa_se = sem("swa_se")
        swa_pn = sem("swa_pn")
        swa_tr = sem("swa_tr")
        swa_ev = sem("swa_ev")
        swa_ea = sem("swa_ea")
        swa_pv = sem("swa_pv")
        taps_a = sem("taps_a")
        taps_b = sem("taps_b")
        tap_mid = sem("tap_mid")
        tap_one = sem("tap_one")
        gated = sem("gated")
        prod = sem("prod")
        ug_sig = sem("ug_sig")
        u_ready = sem("u_ready")
        uhi_ready = sem("uhi_ready")
        ulo_ready = sem("ulo_ready")
        last_tap = sem("last_tap")
        tap_product = sem("tap_product")
        pool_tap = sem("pool_tap")
        dw_tap = sem("dw_tap")
        cv_ready = sem("cv_ready")
        mean_add = sem("mean_add")
        cen_ready = sem("cen_ready")
        ln_ready = sem("ln_ready")
        ln_silu = sem("ln_silu")
        h_ready = sem("h_ready")
        hid_sq = sem("hid_sq")
        rope_sw = sem("rope_sw")
        rope_t = sem("rope_t")
        rope_done = sem("rope_done")
        mla_sc = sem("mla_sc")
        mla_mx = sem("mla_mx")
        mla_exp = sem("mla_exp")
        mla_pn = sem("mla_pn")
        mla_tr = sem("mla_tr")
        mla_ev = sem("mla_ev")
        mla_ea = sem("mla_ea")
        mla_pv = sem("mla_pv")

        H0 = {"post0": 0, "ffpost0": 8, "post1": 16}
        last_unit = {1: UNIT0["wout"], 2: UNIT0["upA"], 3: UNIT0["pw1"], 4: UNIT0["ff1a0"] + 1, 5: UNIT0["dkv"]}

        def conv_step(s):
            n = UNIT0["pw1"] + 4 * s + sum(TAPS_PE[:max(s - 1, 0)]) // 4
            first = range(n, n + 4) if s < KD // 2 else range(n, n)
            taps = range(first.stop, first.stop + TAPS_PE[s - 1] // 4) if s else range(n, n)
            return first, taps

        def conv_bank(c):
            return bank[4 + c % 4]

        def o_tiles(k):
            return (T(os_hi, k), T(os_lo, k)) if k < 4 else (T(og_hi, k - 4), T(og_lo, k - 4))

        def z_out(j):
            return j if j < 6 else j + 3

        block = ctx.enter_context(nc.Block())

        @block.sync
        def _(sp):
            def load(n, slot):
                if not isinstance(n, int) or n >= RING:
                    sp.wait_ge(wlo_ready, n - RING + 1)
                src = stream[bass.ds(n * P, P), :] if not isinstance(n, int) else stream[n * P:(n + 1) * P, :]
                sp.dma_start(w_raw[slot][:, :], src).then_inc(w_landed[slot], 16)

            sp.dma_start(cols[:, :], vectors).then_inc(vec_landed, 16)
            sp.dma_start(h[:, 0:SEQ], xT[0:P, :]).then_inc(h_landed[0], 16)
            load(0, 0)
            for k in range(1, KD):
                sp.dma_start(T(h, k), xT[k * P:(k + 1) * P, :]).then_inc(h_landed[k], 16)
                if k in (2, 4):
                    load(k // 2, k // 2)
            load(3, 3)
            sp.dma_start(cst[:, :], consts).then_inc(cst_landed, 16)
            sp.dma_start(cst_b[:, :], consts1).then_inc(cst_landed, 16)
            sp.dma_start(w_al[:, :], w_alpha).then_inc(cst_landed, 16)

            def four(i):
                for j in range(RING):
                    load(4 * i + (RING + j), j)
            total = min(N_UNITS, last_unit[stage] + AHEAD) if stage in last_unit else N_UNITS
            rounds = (total - RING) // RING
            looped(sp, rounds, four)
            for n in range(RING + RING * rounds, total):
                load(n, n % RING)
            for k in range(KD):
                sp.wait_ge(out_ready, k + 1)
                sp.dma_start(outT[k * P:(k + 1) * P, :], T(h, k)).then_inc(out_stored, 16)
            sp.wait_ge(out_stored, 16 * KD)
            if stage > 2:
                sp.wait_ge(cst2_landed, 16)

        @block.gpsimd
        def _(pool):
            def add_squares(name):
                for k in range(1, STAT_TILES[name] - 1):
                    pool.wait_ge(sq_ready, SQ0[name] + k + 1)
                    if k >= 2:
                        pool.wait_ge(sum_added, ADD0[name] + k - 1)
                    pool.tensor_tensor(ssum[:, :], ssum[:, :], sq_buf[(k - 1) % 2], ALU.add).then_inc(sum_added, 1)

            def gate_products(name, pairs):
                base = 0 if name == "prodA" else PAIRS_A

                def body(i):
                    for j in range(2):
                        pool.wait_ge(gated, 2 * i + (base + j + 1))
                        pool.wait_ge(taps_b, 2 * i + (base + j + 1))
                        pool.tensor_tensor(tmp[4 + j][:, 0:SEQ], tmp[4 + j][:, 0:SEQ], tmp[3][:, 0:SEQ], ALU.mult)\
                            .then_inc(prod, 1)
                looped(pool, pairs // 2, body)

            def hidden_squares(half):
                def body(i):
                    for j in range(4):
                        pool.wait_ge(out_read, 4 * i + (TILE0[f"ff1{half[1]}{half[0]}"] + j + 1))
                        pool.wait_ge(x_ready, 4 * i + (SPLIT0[f"hid{half}"] + j - 1))
                        pool.tensor_tensor(tmp[2 + j % 2][:, 0:SEQ], tmp[j % 2][:, 0:SEQ], tmp[j % 2][:, 0:SEQ],
                                           ALU.mult).then_inc(hid_sq, 1)
                looped(pool, 4, body)

            pool.memset(z_sk[:, 0:P], 0.0).then_inc(p_zero, 1)
            add_squares("mix")
            if stage < 2:
                return
            pool.wait_ge(swa_sums, 5)
            for i in range(SWA_H):
                if i >= 2:
                    pool.wait_ge(swa_bias, NB * (i - 1))
                slope = 2.0 ** (-8.0 * (swa_head(i) + 1) / SWA_H) * SWA_HD ** 0.5
                pool.tensor_scalar(swa_bias_t(i), cst_b[:, DIST:DIST + SEQ], slope, None, ALU.mult)\
                    .then_inc(swa_dist, 1)
            pool.wait_ge(unit_used, UNIT0["wout"])
            for t in range(2):
                pool.memset(gla_a[:, 2 * t * SEQ:2 * (t + 1) * SEQ], 0.0).then_inc(p_zero, 1)
            add_squares("ffn")
            if stage < 3:
                return
            for i in range(2):
                pool.memset(tmp[i][:, 0:2], 0.0).then_inc(p_zero, 1)
            gate_products("prodA", PAIRS_A)
            gate_products("prodB", PAIRS_B)
            add_squares("pre0")
            if stage < 4:
                return
            pool.wait_ge(unit_used, UNIT0["pw1"])
            for k in range(KD):
                pool.memset(u_pad[:, k * UW:k * UW + CONV_W - 1], 0.0).then_inc(p_zero, 1)
            for t in (u_hi, u_lo):
                for k in range(4):
                    pool.memset(t[:, k * UW:k * UW + CONV_W - 1].bitcast(F32), 0.0).then_inc(p_zero, 1)

            def add_taps(k):
                pool.wait_ge(last_tap, k + 1)
                for j in range(TAPS_POOL):
                    pool.wait_ge(tap_product, TAPS_POOL * k + j + 1)
                    if j:
                        pool.wait_ge(pool_tap, TAPS_POOL * k + j)
                    pool.tensor_tensor(T(cv, k), T(cv, k), sq_buf[j], ALU.add).then_inc(pool_tap, 1)

            def add_tile(k):
                pool.wait_ge(cv_ready, k + 1)
                if k == 0:
                    pool.wait_ge(stat_done, STAT_NO["ln_var"])
                    pool.tensor_copy(ssum[:, :], T(cv, 0)).then_inc(mean_add, 1)
                else:
                    pool.wait_ge(mean_add, k)
                    pool.tensor_tensor(ssum[:, :], ssum[:, :], T(cv, k), ALU.add).then_inc(mean_add, 1)

            for p in range(KD // 2):
                if p >= 2:
                    add_tile(2 * p - 4)
                    add_tile(2 * p - 3)
                add_taps(2 * p)
                add_taps(2 * p + 1)
            add_tile(KD - 4)
            add_tile(KD - 3)
            add_squares("ln_var")
            add_squares("post0")
            add_squares("ffpre0")
            if stage < 5:
                return
            for layer in range(2):
                if layer == 1:
                    add_squares("pre1")
                    add_squares("ckv")
                    add_squares("cq")
                    add_squares("post1")
                    add_squares("ffpre1")
                hidden_squares(f"{layer}a")
                hidden_squares(f"{layer}b")
                add_squares(f"ffpost{layer}")
                if stage < 6:
                    return

        @block.scalar
        def _(act):
            def w_hi_of(n, slot):
                if isinstance(n, int) and n >= N_UNITS:
                    return
                rounds = (n - slot) // RING + 1 if isinstance(n, int) else None
                assert rounds is not None
                act.wait_ge(w_landed[slot], 16 * rounds)
                if n >= RING:
                    act.wait_ge(unit_used, n - RING + 1)
                act.activation(w_hi[slot][:, :], w_raw[slot][:, :], ACT.Copy).then_inc(whi_ready, 1)

            def w_hi_loop(n0, i, j):
                n = n0 + j + AHEAD
                slot = n % RING
                if isinstance(i, int):
                    return w_hi_of(n + 4 * i, slot)
                act.wait_ge(w_landed[slot], 16 * i + 16 * (n // RING + 1))
                act.wait_ge(unit_used, 4 * i + (n - RING + 1))
                act.activation(w_hi[slot][:, :], w_raw[slot][:, :], ACT.Copy).then_inc(whi_ready, 1)

            def square(name, k, src, n=D):
                if k == 0:
                    if STAT_NO[name]:
                        act.wait_ge(stat_done, STAT_NO[name])
                    dst = ssum[:, :]
                else:
                    if k >= 3:
                        act.wait_ge(sum_added, ADD0[name] + k - 2)
                    dst = sq_buf[(k - 1) % 2]
                act.activation(dst, src, ACT.Square, scale=float(n) ** -0.5).then_inc(sq_ready, 1)

            def load_sqrt(no):
                act.activation(small[:, 64 + no:65 + no], small[:, 60:61], ACT.Sqrt)

            def take_root(name, dst, eps=EPS):
                c = 4 * STAT_NO[name]
                act.wait_ge(stat_done, STAT_NO[name] + 1)
                act.activation(rms[:, c:c + NB], bank[4][:, 0:NB], ACT.Sqrt,
                               bias=small[:, 60:61] if eps == EPS else small[:, 61:62]).then_inc(rms_ready, 1)
                if dst is not None:
                    act.wait_ge(spread_done, STAT_NO[name] + 1)
                    act.activation(dst[:, :], bank[4][:, :], ACT.Copy).then_inc(r_ready, 1)

            def x_hi(dst, k, src, gain):
                act.activation(T(dst, k), src, ACT.Identity, scale=gain).then_inc(xhi_ready, 1)

            act.wait_ge(vec_landed, 16)
            for k in range(KD):
                act.wait_ge(h_landed[k], 16)
                x_hi(a_hi, k, T(h, k), col("mix_norm", k))
                if k in (0, 2, 4):
                    w_hi_of(k // 2, k // 2)
                square("mix", k, T(h, k))
            w_hi_of(AHEAD, AHEAD)
            act.wait_ge(v_chain, 2)
            take_root("mix", r_pre)
            z0 = UNIT0["z"]
            for n in range(z0, z0 + 6):
                if n > z0:
                    w_hi_of(n + AHEAD, (n + AHEAD) % RING)
                if n < z0 + 5:
                    src = T(z_sq, n) if n < 4 else z_sk[:, P:]
                    act.wait_ge(out_read, n + 1)
                    if n == z0:
                        act.wait_ge(stat_done, 1)
                    if n >= 3:
                        act.wait_ge(swa_sums, n - 2)
                    act.activation(swa_sq_buf(n), src, ACT.Square, scale=SWA_HD ** -0.5).then_inc(swa_sq, 1)
            load_sqrt(len(STATS))
            act.wait_ge(swa_sums, 5)
            act.activation(rms[:, RC_SWA:RC_SWA + 40], bank[4][:, 0:40], ACT.Sqrt, bias=small[:, 60:61])\
                .then_inc(swa_rms, 1)

            def swa_exp_of(i):
                p = swa_p[i % 2]
                act.wait_ge(swa_mx, 2 * (i + 1))
                nm = small[:, 32:36] if i % 2 == 0 else small[:, 40:44]
                den = small[:, 36:40] if i % 2 == 0 else small[:, 44:48]
                se = small[:, 48:52] if i % 2 == 0 else small[:, 52:56]
                act.activation(se, nm, ACT.Exp, bias=col("sinks", swa_head(i))).then_inc(swa_se, 1)
                for b in range(NB):
                    act.activation(T(p, b, 256), T(p, b, 256), ACT.Exp, scale=SWA_HD ** -0.5, bias=nm[:, b:b + 1],
                                   accum_out=den[:, b:b + 1]).then_inc(swa_exp, 1)

            def swa_out_of(i):
                if i % 2:
                    act.wait_ge(swa_pv, i + 1)
                    act.activation(T(os_hi, i // 2), bank[7][:, :], ACT.Copy).then_inc(xhi_ready, 1)

            for i in range(-1, SWA_H):
                n = z0 + 6 + i + 1
                w_hi_of(n + AHEAD, (n + AHEAD) % RING)
                if i + 1 < SWA_H:
                    swa_exp_of(i + 1)
                if i > 0:
                    swa_out_of(i - 1)
                if i >= 0:
                    act.wait_ge(swa_tr, 2 * (i + 1))
                    if i >= 2:
                        act.wait_ge(swa_pv, i - 1)
                    act.activation(swa_pt[i % 2][:, SEQ:], bank[6][:, :], ACT.Copy).then_inc(swa_ea, 1)
                if i in (4, 5):
                    act.wait_ge(gla_logit, i - 3)
                    act.activation(T(gla_b, i - 4), bank[4][:, :], ACT.Identity, bias=col("b_alpha", i - 4))\
                        .then_inc(gla_y, 1)
            w_hi_of(z0 + 15 + AHEAD, (z0 + 15 + AHEAD) % RING)
            swa_out_of(SWA_H - 1)
            act.wait_ge(gla_y, 2)
            act.activation(gla_e, gla_b, ACT.Abs).then_inc(a_chain, 1)
            act.wait_ge(a_chain, 1)
            act.activation(gla_e, gla_e, ACT.Exp, scale=-1.0).then_inc(a_chain, 1)
            act.wait_ge(a_chain, 2)
            act.activation(gla_e, gla_e, ACT.Ln, bias=1.0).then_inc(gla_l, 1)
            w_hi_of(z0 + 16 + AHEAD, (z0 + 16 + AHEAD) % RING)
            act.wait_ge(gla_cum, 2)
            act.activation(gla_e, gla_b, ACT.Exp, scale=1.0 / 16).then_inc(gla_exp, 1)
            w_hi_of(z0 + 17 + AHEAD, (z0 + 17 + AHEAD) % RING)
            act.wait_ge(gla_ops, 1)
            act.activation(gla_e, gla_b, ACT.Exp, scale=-1.0 / 16).then_inc(gla_exp, 1)
            act.wait_ge(gla_blast, 1)
            act.activation(decay[:, :], b_last[:, :], ACT.Exp, scale=1.0 / 16).then_inc(gla_exp, 1)
            act.wait_ge(gla_cum, 3)
            act.activation(gla_b, gla_b, ACT.Exp, scale=1.0 / 16).then_inc(gla_exp, 1)
            w_hi_of(z0 + 18 + AHEAD, (z0 + 18 + AHEAD) % RING)
            w_hi_of(z0 + 19 + AHEAD, (z0 + 19 + AHEAD) % RING)
            for t in range(4):
                act.activation(T(z_r, t), T(z_r, t), ACT.Silu).then_inc(silu_r, 1)
            if stage < 2:
                return
            act.wait_ge(gla_tr, 2)
            act.activation(T(gla_kdt, 1), bank[6][:, :], ACT.Copy).then_inc(gla_tr_read, 1)
            load_sqrt(len(STATS) + 1)
            for hd in range(GLA_H + 2):
                if hd < GLA_H:
                    act.wait_ge(gla_o, hd + 1)
                    act.activation(gla_sq_buf(hd), bank[hd][:, :], ACT.Square, scale=GLA_DV ** -0.5).then_inc(gla_sq, 1)
                if 0 < hd <= GLA_H:
                    act.wait_ge(gla_sums, hd)
                    act.activation(gla_sq_buf(hd - 1), bank[3 + hd][:, :], ACT.Sqrt, bias=small[:, 60:61])\
                        .then_inc(gla_rms, 1)
                if hd >= 2:
                    act.wait_ge(o_done, hd - 1)
                    act.activation(T(og_hi, hd - 2), tmp[hd - 2][:, 0:SEQ], ACT.Copy).then_inc(xhi_ready, 1)
            for k in range(8):
                if k:
                    w_hi_of(UNIT0["wout"] + k + AHEAD, (UNIT0["wout"] + k + AHEAD) % RING)
                act.wait_ge(out_read, TILE0["wout"] + k + 1)
                x_hi(a_hi, k, T(h, k), col("ffn_norm", k))
                if k == 7:
                    load_sqrt(STAT_NO["ffn"])
                square("ffn", k, T(h, k))
            w_hi_of(UNIT0["upA"] + AHEAD, (UNIT0["upA"] + AHEAD) % RING)
            take_root("ffn", r_pre)
            if stage < 3:
                return
            act.dma_start(cst_b[:, :], consts2).then_inc(cst2_landed, 16)

            def up(name, split, first_pair, pairs):
                n0, x0 = UNIT0[name], SPLIT0[split]

                def product_hi(i, j):
                    act.wait_ge(prod, 2 * i + (first_pair + j + 1))
                    act.activation(at(g_hi, 2 * i + j), tmp[4 + j % 2][:, 0:SEQ], ACT.Copy).then_inc(xhi_ready, 1)

                def body(i):
                    for j in range(2):
                        pr = first_pair + j
                        begun = not isinstance(i, int) or i or j
                        if begun or name == "upB":
                            w_hi_loop(n0, i, 2 * j)
                        act.wait_ge(out_read, 4 * i + (TILE0[name] + 2 * j + 1))
                        if begun:
                            act.wait_ge(gated, 2 * i + pr)
                        act.activation(tmp[2][:, 0:SEQ], tmp[0][:, 2:2 + SEQ], ACT.Identity,
                                       scale=conv_col(i, first_pair + j, 0, 2), bias=conv_col(i, first_pair + j, 0, 3))\
                            .then_inc(tap_mid, 1)
                        if begun:
                            product_hi(i, j - 1)
                        w_hi_loop(n0, i, 2 * j + 1)
                        act.wait_ge(out_read, 4 * i + (TILE0[name] + 2 * j + 2))
                        act.activation(tmp[3][:, 0:SEQ], tmp[1][:, 2:2 + SEQ], ACT.Identity,
                                       scale=conv_col(i, first_pair + j, 1, 2), bias=conv_col(i, first_pair + j, 1, 3))\
                            .then_inc(tap_mid, 1)
                        act.wait_ge(taps_a, 2 * i + (pr + 1))
                        act.wait_ge(x_ready, 2 * i + (x0 + j - 1))
                        act.activation(tmp[4 + j][:, 0:SEQ], tmp[2][:, 0:SEQ], ACT.Silu).then_inc(gated, 1)
                body(0)
                looped(act, pairs // 2, body, 1)
                product_hi(pairs // 2 - 1, 1)

            def conv_col(i, j, half, tap):
                return col_at("conv", 16 * i + (8 * j + 4 * half + tap)) if not isinstance(i, int) else \
                    col("conv", 16 * i + 8 * j + 4 * half + tap)

            act.wait_ge(p_zero, 5)
            act.wait_ge(r_ready, R_NO["ffn"] + 1)
            up("upA", "prodA", 0, PAIRS_A)
            for n in range(UNIT0["downA"], UNIT0["upB"]):
                w_hi_of(n + AHEAD, (n + AHEAD) % RING)
            up("upB", "prodB", PAIRS_A, PAIRS_B)
            for k in range(KD):
                if k % 4 == 0:
                    first = UNIT0["downB"] + k // 4 * (PAIRS_B // 2)
                    for n in range(first, first + PAIRS_B // 2):
                        w_hi_of(n + AHEAD, (n + AHEAD) % RING)
                act.wait_ge(out_read, TILE0["downB"] + k + 1)
                x_hi(a_hi, k, T(h, k), col("pre", k))
                if k == 7:
                    load_sqrt(STAT_NO["pre0"])
                square("pre0", k, T(h, k))
            w_hi_of(UNIT0["pw1"] + AHEAD, (UNIT0["pw1"] + AHEAD) % RING)
            take_root("pre0", r_pre)
            if stage < 4:
                return

            def conv_operand(k):
                act.wait_ge(u_ready, k + 1)
                if k >= 4:
                    act.wait_ge(unit_used, conv_step(k // 2 - 1)[1].stop)
                src = u_pad[:, k * UW + CONV_W - 1:(k + 1) * UW]
                act.activation(u_hi[:, (k % 4) * UW + CONV_W - 1:(k % 4 + 1) * UW], src, ACT.Copy)\
                    .then_inc(uhi_ready, 1)
                act.activation(T(cv, k), src, ACT.Identity, scale=col("w_dw", k * CONV_W + CONV_W - 1),
                               bias=col("b_dw", k)).then_inc(last_tap, 1)
                for j in range(TAPS_POOL):
                    tap = CONV_W - 2 - j
                    if k:
                        act.wait_ge(pool_tap, TAPS_POOL * (k - 1) + j + 1)
                    act.activation(sq_buf[j], u_pad[:, k * UW + tap:k * UW + tap + SEQ], ACT.Copy,
                                   scale=col("w_dw", k * CONV_W + tap)).then_inc(tap_product, 1)

            for s in range(KD // 2 + 1):
                first, taps = conv_step(s)
                for n in first:
                    if n > UNIT0["pw1"]:
                        w_hi_of(n + AHEAD, (n + AHEAD) % RING)
                    q = n - first.start
                    k = 2 * s + q // 2
                    if q % 2:
                        act.wait_ge(out_read, TILE0["pw1"] + 2 * k + 2)
                        gate = tmp[2 * (k % 2) + 1][:, 0:SEQ]
                        act.activation(gate, gate, ACT.Sigmoid, bias=col("b_pw1", 8 + k)).then_inc(ug_sig, 1)
                    elif q:
                        conv_operand(k - 1)
                for n in taps:
                    w_hi_of(n + AHEAD, (n + AHEAD) % RING)
                    if n == taps.start and s < KD // 2:
                        conv_operand(2 * s + 1)
                if s == 0:
                    conv_operand(1)
            load_sqrt(STAT_NO["ln_var"])
            act.wait_ge(mean_done, 1)
            for k in range(KD):
                act.wait_ge(cen_ready, k + 1)
                square("ln_var", k, T(cv, k))
            take_root("ln_var", None, LN_EPS)
            act.activation(small[:, 63:64], small[:, 60:61], ACT.Silu)
            w_hi_of(UNIT0["pw2"] + AHEAD, (UNIT0["pw2"] + AHEAD) % RING)
            for k in range(KD):
                act.wait_ge(ln_ready, k + 1)
                act.activation(T(a_hi, k), T(cv, k), ACT.Silu, bias=col("ln_b", k)).then_inc(xhi_ready, 1)
                act.activation(T(m, k), T(cv, k), ACT.Silu, bias=col("ln_b", k)).then_inc(ln_silu, 1)

            def after(product, stat, per_tile_units, done=0):
                for k in range(KD):
                    for u in range(done if k == 0 else 0, per_tile_units):
                        n = UNIT0[product] + per_tile_units * k + u + AHEAD
                        w_hi_of(n, n % RING)
                    act.wait_ge(out_read, TILE0[product] + k + 1)
                    if k == 7:
                        load_sqrt(STAT_NO[stat])
                    square(stat, k, T(m, k))
                take_root(stat, None)

            def next_operand(h0, gain, g0, stat, product):
                for k in range(KD):
                    act.wait_ge(h_ready, h0 + k + 1)
                    x_hi(a_hi, k, T(h, k), col(gain, g0 + k))
                    square(stat, k, T(h, k))
                w_hi_of(UNIT0[product] + AHEAD, (UNIT0[product] + AHEAD) % RING)
                take_root(stat, r_pre)

            after("pw2", "post0", 1, 1)
            next_operand(H0["post0"], "ffpre", 0, "ffpre0", "ff1a0")
            if stage < 5:
                return

            def feed_forward(layer):
                for half in range(2):
                    c = "ab"[half]
                    n0 = UNIT0[f"ff1{c}{layer}"]
                    t0 = TILE0[f"ff1{c}{layer}"]

                    def body(i):
                        for j in range(4):
                            if not isinstance(i, int) or j or half:
                                w_hi_loop(n0, i, j)
                            act.wait_ge(out_read, 4 * i + (t0 + j + 1))
                            act.activation(at(g_hi, 4 * i + j), tmp[j % 2][:, 0:SEQ], ACT.Square)\
                                .then_inc(xhi_ready, 1)
                    body(0)
                    looped(act, 4, body, 1)
                    if half == 0:
                        looped(act, 4, lambda i: [w_hi_loop(UNIT0[f"ff2a{layer}"], i, j) for j in range(4)])
                after(f"ff2b{layer}", f"ffpost{layer}", 2)

            feed_forward(0)
            if stage < 6:
                return
            for k in range(KD):
                act.wait_ge(h_ready, H0["ffpost0"] + k + 1)
                x_hi(a_hi, k, T(h, k), col("kv_in", k))
                square("pre1", k, T(h, k))
            w_hi_of(UNIT0["dkv"] + AHEAD, (UNIT0["dkv"] + AHEAD) % RING)
            for k in range(KD):
                x_hi(b_hi, k, T(h, k), col("pre", 8 + k))
            take_root("pre1", r_pre)
            for n in range(UNIT0["dkv"] + 1, UNIT0["uk"]):
                w_hi_of(n + AHEAD, (n + AHEAD) % RING)
            for k in range(2):
                act.wait_ge(out_read, TILE0["dkv"] + k + 1)
                square("ckv", k, T(c_kv, k), KV_RANK)
            act.wait_ge(unit_used, UNIT0["dq"])
            for k in range(2):
                x_hi(a_hi, k, T(c_kv, k), col("ckv_norm", k))
            for k in range(3):
                act.wait_ge(out_read, TILE0["dq"] + k + 1)
                square("cq", k, T(c_q, k), Q_RANK)
                x_hi(a_hi, 2 + k, T(c_q, k), col("cq_norm", k))
            take_root("ckv", r_post)
            take_root("cq", r_pre)
            for n in range(UNIT0["uk"], UNIT0["wo"] + 1):
                w_hi_of(n + AHEAD, (n + AHEAD) % RING)
            for i in range(MLA_H):
                nm = small[:, 32:36] if i % 2 == 0 else small[:, 40:44]
                den = small[:, 36:40] if i % 2 == 0 else small[:, 44:48]
                act.wait_ge(mla_mx, 5 * (i + 1))
                if i:
                    act.wait_ge(mla_tr, 3 * i)
                for b in range(NB):
                    w = (b + 1) * P
                    o = P * b * (b + 1) // 2
                    act.activation(prob[:, o:o + w], bank[b][:, 0:w], ACT.Exp, scale=MLA_SCALE, bias=nm[:, b:b + 1],
                                   accum_out=den[:, b:b + 1]).then_inc(mla_exp, 1)
                act.wait_ge(mla_tr, 3 * i + 2)
                if i:
                    act.wait_ge(mla_pv, i)
                act.activation(probT[:, SEQ:2 * SEQ], bank[6][:, :], ACT.Copy).then_inc(mla_ea, 1)
                act.wait_ge(mla_pv, i + 1)
                act.activation(T(a_hi, i), bank[4][:, :], ACT.Copy).then_inc(xhi_ready, 1)
            after("wo", "post1", 1, 1)
            next_operand(H0["post1"], "ffpre", 8, "ffpre1", "ff1a1")
            feed_forward(1)

        @block.tensor
        def _(pe):
            def three(out, w0, w1, x0, x1, start, stop):
                pe.matmul(out, w0, x0, start=start, stop=False)
                pe.matmul(out, w0, x1, start=False, stop=False)
                return pe.matmul(out, w1, x0, start=False, stop=stop)

            def x_tile(hi, lo, k):
                return hi(k) if lo is None else (T(hi, k), T(lo, k))

            def bank_free(name, j):
                if name == "pw1" and j < 4:
                    pe.wait_ge(out_read, TILE0["downB"] + 4)
                else:
                    pe.wait_ge(out_read, TILE0[name] + max(j - 3, 0))

            def k_ready(split, k):
                pe.wait_ge(x_ready, SPLIT0[split] + k + 1)

            def unit_ready(n, i=0):
                pe.wait_ge(wlo_ready, n + 1 + 4 * i if isinstance(i, int) else 4 * i + (n + 1))

            def tile_of_eight(n, slot, out, hi, lo, k0=0, start=True, stop=True, split=None):
                for k in range(8):
                    if split:
                        k_ready(split, k0 + k)
                    last = three(out, T(w_hi[slot], k, P), T(w_lo[slot], k, P), *x_tile(hi, lo, k0 + k),
                                 start and k == 0, stop and k == 7)
                last.then_inc(unit_used, 1)

            def token_sums(dst, sq, rhs=None, start=True, stop=True):
                rhs = cst[:, ONES:ONES + 1] if rhs is None else rhs
                w = rhs.shape[-1]
                for b in range(NB):
                    last = pe.matmul(dst[:, w * b:w * (b + 1)], T(sq, b, P), rhs, start=start, stop=stop)
                return last

            def stat(name):
                s, n = STAT_NO[name], STAT_TILES[name]
                if s == 0:
                    pe.wait_ge(cst_landed, 48)
                pe.wait_ge(sq_ready, SQ0[name] + n - 1)
                if n > 2:
                    pe.wait_ge(sum_added, ADD0[name] + n - 2)
                before = STATS[s - 1][0]
                if before in H0:
                    pe.wait_ge(h_ready, H0[before] + KD)
                elif before == "ln_var":
                    pe.wait_ge(ln_ready, KD)
                elif s:
                    pe.wait_ge(r_ready, R_NO[before] + 1)
                for b in range(NB):
                    pe.matmul(bank[4][:, b:b + 1], T(ssum, b, P), cst[:, ONES:ONES + 1], start=(b == 0), stop=False,
                              skip_group_check=True)
                pe.wait_ge(sq_ready, SQ0[name] + n)
                for b in range(NB):
                    last = pe.matmul(bank[4][:, b:b + 1], T(sq_buf[(n - 2) % 2], b, P), cst[:, ONES:ONES + 1],
                                     start=False, stop=(b == NB - 1), skip_group_check=True)
                last.then_inc(stat_done, 1)

            def spread(name):
                pe.wait_ge(r_tok_ready, STAT_NO[name] + 1)
                for b in range(NB):
                    last = pe.matmul(T(bank[4], b, P), r_cols(4 * STAT_NO[name] + b), cst[:, IDENT:IDENT + P],
                                     start=True, stop=True)
                last.then_inc(spread_done, 1)

            def three_tiles(name, hi, lo, split, stat_name=None):
                n0 = UNIT0[name]
                for k in range(8):
                    k_ready(split, k)
                    for j in range(3):
                        if k == 0:
                            unit_ready(n0 + j)
                            bank_free(name, j)
                        slot = (n0 + j) % RING
                        last = three(bank[j][:, :], T(w_hi[slot], k, P), T(w_lo[slot], k, P), *x_tile(hi, lo, k),
                                     k == 0, k == 7)
                        if k == 7:
                            last.then_inc(unit_used, 1)
                            if j == 0 and stat_name:
                                stat(stat_name)
                if stat_name:
                    spread(stat_name)

            def tiles(name, count, hi, lo, split=None, stat_name=None):
                n0 = UNIT0[name]
                if split:
                    three_tiles(name, hi, lo, split, stat_name)
                for j in range(3 if split else 0, count):
                    n = n0 + j
                    unit_ready(n)
                    bank_free(name, j)
                    tile_of_eight(n, n % RING, bank[j % 4][:, :], hi, lo)

            n0 = UNIT0["z"]
            three_tiles("z", a_hi, a_lo, "mix", "mix")

            def z_tile(j):
                unit_ready(n0 + j)
                if j < 6:
                    bk = j % 4
                    if j == 4:
                        pe.wait_ge(out_read, 1)
                else:
                    bk = j % 2
                    pe.wait_ge(out_read, z_out(j) - 1)
                tile_of_eight(n0 + j, (n0 + j) % RING, bank[bk][:, :], a_hi, a_lo)

            for j in range(3, 5):
                z_tile(j)
            halves = cst[:, HALVES:HALVES + 2]
            pe.wait_ge(r_ready, 1)
            for t in range(5):
                pe.wait_ge(swa_sq, t + 1)
                token_sums(bank[4][:, 8 * t:8 * t + 8], swa_sq_buf(t), halves).then_inc(swa_sums, 1)
            n = n0 + 5
            unit_ready(n)
            for b in range(NB):
                j = 5 + b
                pe.wait_ge(out_read, j - 3)
                for k in range(KD):
                    xh, xl = T(a_hi, k)[:, b * P:(b + 1) * P], T(a_lo, k)[:, b * P:(b + 1) * P]
                    last = three(bank[j % 4][:, 0:P], xh, xl, T(w_hi[n % RING], k, P), T(w_lo[n % RING], k, P),
                                 k == 0, k == KD - 1)
            last.then_inc(unit_used, 1)
            pe.wait_ge(swa_r, 1)
            for b in range(NB):
                for e in range(2):
                    last = pe.matmul(T(bank[5], b, P)[64 * e:64 * e + 64, :], r_cols(RC_SWA + 32 + 2 * b + e, 64),
                                     cst[:, IDENT:IDENT + P], start=True, stop=True)
            last.then_inc(sk_spread, 1)
            def swa_scores(i):
                hd = swa_head(i)
                r = slice(64 * (hd // 4), 64 * (hd // 4) + 64)
                t = hd % 4
                if i == 0:
                    pe.wait_ge(out_read, 9)
                    pe.wait_ge(k_normed, 1)
                    pe.wait_ge(p_zero, 1)
                else:
                    pe.wait_ge(swa_bias, NB * i)
                for b in range(NB):
                    pe.matmul(bank[2 + b // 2][:, 256 * (b % 2):256 * (b % 2) + 256], T(z_sq, t)[r, b * P:(b + 1) * P],
                              z_sk[r, b * P:b * P + 256], start=True, stop=True).then_inc(swa_sc, 1)

            def swa_transpose(i):
                p = swa_p[i % 2]
                pe.wait_ge(swa_pn, NB * (i + 1))
                if i:
                    pe.wait_ge(swa_ev, i)
                    pe.wait_ge(swa_ea, i)
                for b in range(NB):
                    for e in range(2):
                        if b == 0 and e == 0:
                            continue
                        last = pe.transpose(bank[5 + b // 2][:, (2 * (b % 2) + e) * P:(2 * (b % 2) + e + 1) * P],
                                            p[:, b * 256 + e * P:b * 256 + (e + 1) * P], cst[:, IDENT:IDENT + P])
                    if b % 2:
                        last.then_inc(swa_tr, 1)

            def swa_values(i):
                t, g = swa_pt[i % 2], i % 2
                pe.wait_ge(swa_ev, i + 1)
                pe.wait_ge(swa_ea, i + 1)
                if g == 0 and i:
                    pe.wait_ge(x_ready, SPLIT0["attn"] + i // 2)
                for b in range(NB):
                    es = [e for e in range(2) if b + e > 0]
                    for e in es:
                        last = pe.matmul(bank[7][64 * g:64 * g + 64, b * P:(b + 1) * P],
                                         z_vs[:, (b - 1 + e) * P + 64 * g:(b - 1 + e) * P + 64 * g + 64],
                                         t[:, (2 * b + e) * P:(2 * b + e + 1) * P], start=(e == es[0]), stop=(e == 1))
                last.then_inc(swa_pv, 1)

            for i in range(-1, SWA_H):
                if i + 1 < SWA_H:
                    swa_scores(i + 1)
                if i in (4, 5):
                    pe.wait_ge(out_read, z_out(10) + 1)
                    if i == 5:
                        pe.wait_ge(gla_y, 1)
                    pe.matmul(bank[4][:, :], T(w_al, i - 4, P), z_lr[:, :], start=True, stop=True).then_inc(gla_logit, 1)
                z_tile(6 + i + 1)
                if i > 0:
                    swa_values(i - 1)
                if i >= 0:
                    swa_transpose(i)
            for u in range(4):
                n = n0 + 15 + u
                unit_ready(n)
                for kk in range(2):
                    k = 2 * u + kk
                    for b in range(NB):
                        if k == 0:
                            pe.wait_ge(out_read, 18)
                            pe.wait_ge(swa_bias, NB * SWA_H)
                        xh, xl = T(a_hi, k)[:, b * P:(b + 1) * P], T(a_lo, k)[:, b * P:(b + 1) * P]
                        last = three(bank[b][:, :], xh, xl, T(w_hi[n % RING], kk), T(w_lo[n % RING], kk),
                                     k == 0, k == KD - 1)
                last.then_inc(unit_used, 1)
                if u == 0:
                    swa_values(SWA_H - 1)
            if stage < 2:
                return
            pe.wait_ge(out_read, TILE0["wout"])
            pe.wait_ge(gla_ops, 3)
            for hd in range(GLA_H):
                r = slice(64 * (hd % 2), 64 * (hd % 2) + 64)
                for b in range(NB):
                    last = pe.matmul(T(bank[hd], b, P), T(gla_e, hd // 2)[r, b * P:(b + 1) * P],
                                     T(z_q, hd // 2)[r, b * P:(b + 1) * P], start=True, stop=True)
                last.then_inc(gla_scores, 1)
            for t in range(2):
                for b in range(NB):
                    last = pe.transpose(T(bank[5 + t], b, P), T(gla_b, t)[:, b * P:(b + 1) * P],
                                        cst[:, IDENT:IDENT + P])
                last.then_inc(gla_tr, 1)
            pe.wait_ge(gla_tr_read, 2)
            for t in range(2):
                for par in range(2):
                    for q in range(NB):
                        for e in range(2):
                            hd = 2 * t + e
                            last = pe.matmul(T(bank[4 + 2 * t + par], q, P)[64 * e:64 * e + 64, :],
                                             T(gla_kdt, t)[64 * par:64 * par + 64, q * P + 64 * e:q * P + 64 * e + 64],
                                             T(z_v, q)[64 * par:64 * par + 64, hd * P:(hd + 1) * P],
                                             start=True, stop=True, skip_group_check=True)
                    last.then_inc(gla_cs, 1)
            for hd in range(GLA_H):
                pe.wait_ge(gla_masked, hd + 1)
                for b in range(NB):
                    pe.matmul(T(bank[hd], b, P), T(z_v, b)[:, hd * P:(hd + 1) * P],
                              T(gla_a, hd)[:, b * P:(b + 1) * P], start=(b == 0), stop=False, skip_group_check=True)

            def gla_mean_square(hd):
                pe.wait_ge(gla_sq, hd + 1)
                pe.matmul(bank[4 + hd][:, :], cst[:, ONES:ONES + P], gla_sq_buf(hd), start=True, stop=True)\
                    .then_inc(gla_sums, 1)

            pe.wait_ge(gla_state, 2 * (NCH - 1))
            for hd in range(GLA_H):
                r = slice(64 * (hd % 2), 64 * (hd % 2) + 64)
                for c in range(1, NCH):
                    s = gla_s[r, ((hd // 2) * NCH + c) * GLA_DV:((hd // 2) * NCH + c + 1) * GLA_DV]
                    last = pe.matmul(bank[hd][:, c * CHUNK:(c + 1) * CHUNK], s,
                                     T(z_q, hd // 2)[r, c * CHUNK:(c + 1) * CHUNK], start=False, stop=(c == NCH - 1),
                                     skip_group_check=True)
                last.then_inc(gla_o, 1)
                if hd:
                    gla_mean_square(hd - 1)
            gla_mean_square(GLA_H - 1)
            pe.wait_ge(o_done, GLA_H - 1)
            tiles("wout", 8, o_tiles, None, "attn")
            if stage < 3:
                stat("ffn")
                return

            def up(name, split, pairs):
                n0 = UNIT0[name]

                def body(i):
                    for j in range(4):
                        unit_ready(n0 + j, i)
                        pe.wait_ge(out_read, 4 * i + (TILE0[name] + j - 3))
                        tile_of_eight(n0 + j, (n0 + j) % RING, bank[j % 4][:, :], a_hi, a_lo)
                if split:
                    three_tiles(name, a_hi, a_lo, split, split)
                    unit_ready(n0 + 3)
                    bank_free(name, 3)
                    tile_of_eight(n0 + 3, (n0 + 3) % RING, bank[3][:, :], a_hi, a_lo)

                    def rest(i):
                        for j in range(4):
                            unit_ready(n0 + 4 + j, i)
                            pe.wait_ge(out_read, 4 * i + (TILE0[name] + j + 1))
                            tile_of_eight(n0 + j, (n0 + j) % RING, bank[j % 4][:, :], a_hi, a_lo)
                    looped(pe, pairs // 2 - 1, rest)
                else:
                    looped(pe, pairs // 2, body)

            def down(name, split, kts):
                n = UNIT0[name]
                for g in range(2):
                    for u in range(kts // 2):
                        unit_ready(n)
                        for kk in range(2):
                            k = 2 * u + kk
                            k_ready(split, k)
                            for j in range(4):
                                if k == 0:
                                    pe.wait_ge(out_read, TILE0[name])
                                w = slice((4 * kk + j) * P, (4 * kk + j + 1) * P)
                                last = three(bank[4 * g + j][:, :], w_hi[n % RING][:, w], w_lo[n % RING][:, w],
                                             T(g_hi, k), T(g_lo, k), k == 0, k == kts - 1)
                        last.then_inc(unit_used, 1)
                        n += 1

            up("upA", "ffn", PAIRS_A)
            down("downA", "prodA", PAIRS_A)
            up("upB", None, PAIRS_B)
            down("downB", "prodB", PAIRS_B)
            if stage < 4:
                stat("pre0")
                return
            for s in range(KD // 2 + 1):
                first, taps = conv_step(s)
                if s == 0:
                    three_tiles("pw1", a_hi, a_lo, "pre0", "pre0")
                for n in first:
                    q = n - first.start
                    if s or q == 3:
                        unit_ready(n)
                        bank_free("pw1", 4 * s + q)
                        tile_of_eight(n, n % RING, bank[q][:, :], a_hi, a_lo)
                for n in taps:
                    unit_ready(n)
                    for i in range(8):
                        e, tap = divmod(8 * (n - taps.start) + i, TAPS_PE[s - 1])
                        c = 2 * (s - 1) + e
                        if tap == 0:
                            pe.wait_ge(ulo_ready, c + 1)
                            if c >= 4:
                                pe.wait_ge(cv_ready, c - 3)
                        o = (c % 4) * UW + tap
                        last = three(conv_bank(c)[:, :], T(w_hi[n % RING], i, P), T(w_lo[n % RING], i, P),
                                     u_hi[:, o:o + SEQ], u_lo[:, o:o + SEQ], tap == 0, tap == TAPS_PE[s - 1] - 1)
                    last.then_inc(unit_used, 1)
            pe.wait_ge(mean_add, KD - 2)
            pe.matmul(bank[4][:, :], cst[:, MEAN:MEAN + P], ssum[:, :], start=True, stop=False)
            pe.wait_ge(cv_ready, KD)
            pe.matmul(bank[4][:, :], cst[:, MEAN:MEAN + P], T(cv, KD - 2), start=False, stop=False)
            pe.matmul(bank[4][:, :], cst[:, MEAN:MEAN + P], T(cv, KD - 1), start=False, stop=True).then_inc(mean_done, 1)
            pe.wait_ge(cen_ready, KD)
            stat("ln_var")
            spread("ln_var")
            tiles("pw2", 8, a_hi, a_lo, "conv")
            stat("post0")
            spread("post0")
            if stage < 5:
                tiles("ff1a0", 1, a_hi, a_lo, "ffpre0", "ffpre0")
                return

            def feed_forward(layer):
                up(f"ff1a{layer}", f"ffpre{layer}", 8)
                for half in range(2):
                    c = "ab"[half]
                    if half:
                        pe.wait_ge(out_read, TILE0[f"ff1b{layer}"])
                        up(f"ff1b{layer}", None, 8)
                    name = f"ff2{c}{layer}"
                    n0, t0 = UNIT0[name], TILE0[name]

                    def body(i):
                        for j in range(2):
                            b = j
                            pe.wait_ge(out_read, 2 * i + (t0 + j - 1))
                            if isinstance(i, int) and j == 0:
                                pe.wait_ge(out_read, t0)
                            for u in range(2):
                                n = n0 + 2 * j + u
                                unit_ready(n, i)
                                tile_of_eight(n, n % RING, bank[b][:, :], g_hi, g_lo, 8 * u, u == 0, u == 1,
                                              f"hid{layer}{c}" if isinstance(i, int) and j == 0 else None)
                    body(0)
                    looped(pe, 4, body, 1)
                stat(f"ffpost{layer}")
                spread(f"ffpost{layer}")

            feed_forward(0)
            if stage < 6:
                return
            tiles("dkv", 3, a_hi, a_lo, "kvpre", "pre1")
            tiles("dq", 3, b_hi, b_lo, "pre1")
            swap = cst[:, SWAP:SWAP + P]
            pe.wait_ge(out_read, TILE0["dkv"] + 3)
            pe.matmul(bank[5][:, :], swap, k_rope, start=True, stop=True).then_inc(rope_sw, 1)
            stat("ckv")
            spread("ckv")
            stat("cq")
            spread("cq")
            for u in range(2):
                n = UNIT0["uk"] + u
                unit_ready(n)
                for j in range(4):
                    bank_free("uk", 4 * u + j)
                    for k in range(2):
                        if u == 0 and j == 0:
                            k_ready("ckv", k)
                        w = slice((4 * k + j) * P, (4 * k + j + 1) * P)
                        last = three(bank[j][:, :], w_hi[n % RING][:, w], w_lo[n % RING][:, w], T(a_hi, k), T(a_lo, k),
                                     k == 0, k == 1)
                last.then_inc(unit_used, 1)
            for u in range(2):
                n = UNIT0["uv"] + u
                unit_ready(n)
                for b in range(NB):
                    bank_free("uv", 4 * u + b)
                    for k in range(2):
                        last = three(bank[b][:, :], T(a_hi, k)[:, b * P:(b + 1) * P], T(a_lo, k)[:, b * P:(b + 1) * P],
                                     T(w_hi[n % RING], k), T(w_lo[n % RING], k), k == 0, k == 1)
                last.then_inc(unit_used, 1)
            for u in range(6):
                n = UNIT0["uq"] + u
                unit_ready(n)
                for e in range(2):
                    j = 2 * u + e
                    bank_free("uq", j)
                    for k in range(3):
                        if j == 0:
                            k_ready("cq", k)
                        w = slice(k * 256 + e * P, k * 256 + (e + 1) * P)
                        last = three(bank[j % 4][:, :], w_hi[n % RING][:, w], w_lo[n % RING][:, w],
                                     T(a_hi, 2 + k), T(a_lo, 2 + k), k == 0, k == 2)
                last.then_inc(unit_used, 1)
            for t in range(4):
                pe.wait_ge(out_read, TILE0["uq"] + 8 + t + 1)
                pe.wait_ge(rope_t, 2 * t + 2)
                pe.matmul(bank[5][:, :], swap, T(q_rope, t), start=True, stop=True).then_inc(rope_sw, 1)
            pe.wait_ge(rope_done, 5)
            pe.wait_ge(out_read, TILE0["wo"])
            pe.wait_ge(cst2_landed, 16)

            def mla_scores(i):
                r = slice(64 * (i % 2), 64 * (i % 2) + 64)
                for b in range(NB):
                    w = (b + 1) * P
                    if i:
                        pe.wait_ge(mla_exp, NB * (i - 1) + b + 1)
                    pe.matmul(bank[b][:, 0:w], T(q_nope, i)[:, b * P:(b + 1) * P], T(k_nope, i)[:, 0:w],
                              start=True, stop=False)
                    pe.matmul(bank[b][:, w - P:w], cst_b[0:1, MASK_Q:MASK_Q + P], cst_b[0:1, MASK_K:MASK_K + P],
                              start=False, stop=False)
                    pe.matmul(bank[b][:, 0:w], T(q_rope, i // 2)[r, b * P:(b + 1) * P], k_rope[r, 0:w],
                              start=False, stop=True).then_inc(mla_sc, 1)

            mla_scores(0)
            for i in range(MLA_H):
                if i + 1 < MLA_H:
                    mla_scores(i + 1)
                pe.wait_ge(mla_pn, NB * (i + 1))
                if i:
                    pe.wait_ge(mla_ev, 2 * i)
                    pe.wait_ge(mla_ea, i)
                for kt, bk, c0 in ((0, 5, 0), (1, 6, 0), (3, 6, 3 * P), (2, 7, 0)):
                    for b in range(kt, NB):
                        o = P * b * (b + 1) // 2 + kt * P
                        c = c0 + (b - kt) * P
                        last = pe.transpose(bank[bk][:, c:c + P], prob[:, o:o + P], cst[:, IDENT:IDENT + P])
                    if kt != 1:
                        last.then_inc(mla_tr, 1)
                pe.wait_ge(mla_ev, 2 * (i + 1))
                pe.wait_ge(mla_ea, i + 1)
                pe.wait_ge(x_ready, SPLIT0["mla"] + i)
                for b in range(NB):
                    for kt, c0 in enumerate((0, SEQ, 2 * SEQ, SEQ + 3 * P)[:b + 1]):
                        c = c0 + (b - kt) * P
                        last = pe.matmul(T(bank[4], b, P), T(v_tok, kt, MLA_H * V_DIM)[:, i * P:(i + 1) * P],
                                         probT[:, c:c + P], start=(kt == 0), stop=(kt == b))
                last.then_inc(mla_pv, 1)
            tiles("wo", 8, a_hi, a_lo, "mla")
            stat("post1")
            spread("post1")
            feed_forward(1)

        @block.vector
        def _(dve):
            def lo(n, slot, i=None):
                if i is None:
                    if n >= N_UNITS:
                        return
                    dve.wait_ge(whi_ready, n + 1)
                else:
                    dve.wait_ge(whi_ready, 4 * i + (n + 1))
                dve.tensor_tensor(w_lo[slot][:, :], w_raw[slot][:, :], f(w_hi[slot][:, :]), ALU.subtract)\
                    .then_inc(wlo_ready, 1)

            def lo_ahead(n, i=None):
                n += AHEAD
                if isinstance(i, int):
                    n, i = n + 4 * i, None
                lo(n, n % RING, i)

            def unit_done(n, i=None):
                dve.wait_ge(unit_used, n + 1 if i is None else 4 * i + (n + 1))

            def x_lo(no, dst_lo, dst_hi, k, src, gain=None):
                dve.wait_ge(xhi_ready, no + 1)
                if gain is None:
                    ins = dve.tensor_tensor(T(dst_lo, k), src, f(T(dst_hi, k)), ALU.subtract)
                else:
                    ins = dve.scalar_tensor_tensor(T(dst_lo, k), src, gain, f(T(dst_hi, k)), ALU.mult, ALU.subtract)
                ins.then_inc(x_ready, 1)

            def take_r(name):
                c = 4 * STAT_NO[name]
                dve.wait_ge(rms_ready, STAT_NO[name] + 1)
                dve.reciprocal(r_tok[:, c:c + NB], rms[:, c:c + NB]).then_inc(r_tok_ready, 1)

            def scaled(name):
                dve.wait_ge(r_ready, R_NO[name] + 1)

            links = [0]

            def link(ins):
                links[0] += 1
                ins.then_inc(v_chain, 1)
                dve.wait_ge(v_chain, links[0])

            link(dve.memset(small[:, 60:61], EPS))
            link(dve.memset(small[:, 61:62], LN_EPS))
            dve.wait_ge(vec_landed, 16)
            for k in range(KD):
                x_lo(SPLIT0["mix"] + k, a_lo, a_hi, k, T(h, k), col("mix_norm", k))
                if k in (0, 2, 4):
                    lo(k // 2, k // 2)
            lo_ahead(0)
            take_r("mix")
            scaled("mix")
            for j in range(5):
                if j:
                    lo_ahead(j)
                unit_done(j)
                dst = T(z_sq, j) if j < 4 else z_sk[:, P:]
                dve.tensor_tensor(dst, bank[j % 4][:, :], r_pre[:, :], ALU.mult).then_inc(out_read, 1)
            lo_ahead(5)
            link(dve.tensor_tensor(small[:, 62:63], col("q_norm"), col("k_norm"), ALU.mult))
            dve.wait_ge(swa_rms, 1)
            dve.reciprocal(r_tok[:, RC_SWA:RC_SWA + 40], rms[:, RC_SWA:RC_SWA + 40]).then_inc(swa_r, 1)
            unit_done(5)
            for b in range(NB):
                dve.tensor_scalar(T(z_vs, b, P), bank[(5 + b) % 4][:, 0:P], r_tok[:, b:b + 1], None, ALU.mult)\
                    .then_inc(out_read, 1)
            dve.wait_ge(sk_spread, 1)
            dve.wait_ge(out_read, 5)
            dve.scalar_tensor_tensor(z_sk[:, P:], z_sk[:, P:], small[:, 62:63], bank[5][:, :], ALU.mult, ALU.mult)\
                .then_inc(k_normed, 1)

            def swa_softmax_in(i):
                p, t, e = swa_p[i % 2], swa_head(i) % 4, swa_head(i) // 4
                nm = small[:, 32:36] if i % 2 == 0 else small[:, 40:44]
                dve.wait_ge(swa_dist, i + 1)
                if i == 0:
                    dve.wait_ge(swa_r, 1)
                for b in range(NB):
                    dve.wait_ge(swa_sc, NB * i + b // 2 * 2 + 2)
                    c = RC_SWA + 8 * t + 2 * b + e
                    d0 = 0 if b == 0 else 256
                    dve.scalar_tensor_tensor(T(p, b, 256), bank[2 + b // 2][:, 256 * (b % 2):256 * (b % 2) + 256],
                                             r_tok[:, c:c + 1], swa_bias_t(i)[:, d0:d0 + 256], ALU.mult, ALU.add)\
                        .then_inc(swa_bias, 1)
                dve.wait_ge(swa_bias, NB * (i + 1))
                link(dve.tensor_reduce(nm, p[:, :].rearrange("p (b k) -> p b k", b=NB), AX_X, ALU.max))
                dve.tensor_scalar(nm, nm, SWA_HD ** -0.5, col("sinks", swa_head(i)), ALU.mult, ALU.max)\
                    .then_inc(swa_mx, 1)
                dve.wait_ge(swa_mx, 2 * i + 1)
                dve.tensor_scalar(nm, nm, -1.0, None, ALU.mult).then_inc(swa_mx, 1)

            def swa_normalise(i):
                p = swa_p[i % 2]
                den = small[:, 36:40] if i % 2 == 0 else small[:, 44:48]
                se = small[:, 48:52] if i % 2 == 0 else small[:, 52:56]
                dve.wait_ge(swa_se, i + 1)
                dve.wait_ge(swa_exp, NB * (i + 1))
                link(dve.tensor_tensor(den, den, se, ALU.add))
                link(dve.reciprocal(den, den))
                for b in range(NB):
                    dve.tensor_scalar(T(p, b, 256), T(p, b, 256), den[:, b:b + 1], None, ALU.mult).then_inc(swa_pn, 1)

            def swa_out_lo(i):
                if i % 2:
                    x_lo(SPLIT0["attn"] + i // 2, os_lo, os_hi, i // 2, bank[7][:, :])

            dests = [T(z_q, 0), T(z_q, 1), T(z_k, 0), T(z_k, 1), z_lr[:, :]] + [T(z_r, t) for t in range(4)]
            for i in range(-1, SWA_H):
                n = 6 + i + 1
                lo_ahead(n)
                if i + 1 < SWA_H:
                    if i >= 1:
                        dve.wait_ge(swa_tr, 2 * i)
                    swa_softmax_in(i + 1)
                if i >= 0:
                    swa_normalise(i)
                unit_done(n)
                dve.tensor_tensor(dests[i + 1], bank[n % 2][:, :], r_pre[:, :], ALU.mult).then_inc(out_read, 1)
                if i > 0:
                    swa_out_lo(i - 1)
                if i >= 0:
                    dve.wait_ge(swa_tr, 2 * i + 1)
                    if i >= 2:
                        dve.wait_ge(swa_pv, i - 1)
                    dve.tensor_copy(swa_pt[i % 2][:, P:SEQ], bank[5][:, P:SEQ]).then_inc(swa_ev, 1)
            lo_ahead(15)
            swa_out_lo(SWA_H - 1)
            dve.wait_ge(gla_l, 1)
            dve.scalar_tensor_tensor(gla_b, gla_b, 0.0, gla_e, ALU.min, ALU.subtract).then_inc(gla_ls, 1)
            dve.wait_ge(gla_ls, 1)
            for t in range(2):
                dve.tensor_tensor_scan(T(gla_b, t), cst_b[:, RESET:RESET + SEQ], T(gla_b, t), 0.0, ALU.mult, ALU.add)\
                    .then_inc(gla_cum, 1)
            dve.wait_ge(gla_cum, 2)
            chunks = gla_b.rearrange("p (n c) -> p n c", c=CHUNK)
            dve.tensor_copy(b_last[:, :], chunks[:, :, CHUNK - 1]).then_inc(gla_blast, 1)
            lo_ahead(16)
            dve.wait_ge(gla_exp, 1)
            dve.scalar_tensor_tensor(z_q[:, :], z_q[:, :], GLA_DK ** -0.5, gla_e, ALU.mult, ALU.mult)\
                .then_inc(gla_ops, 1)
            lo_ahead(17)
            dve.wait_ge(gla_exp, 2)
            dve.wait_ge(gla_blast, 1)
            last = b_last[:, :].rearrange("p (n o) -> p n o", o=1)
            dve.tensor_tensor(chunks, last.broadcast_to([P, 2 * NCH, CHUNK]), chunks, ALU.subtract)\
                .then_inc(gla_cum, 1)
            dve.tensor_tensor(gla_e, gla_e, z_k[:, :], ALU.mult).then_inc(gla_ops, 1)
            dve.wait_ge(gla_exp, 4)
            dve.tensor_tensor(gla_b, gla_b, z_k[:, :], ALU.mult).then_inc(gla_ops, 1)
            lo_ahead(18)
            unit_done(18)
            for b in range(NB):
                dve.tensor_scalar(T(z_v, b), bank[b][:, :], r_tok[:, b:b + 1], None, ALU.mult).then_inc(out_read, 1)
            lo_ahead(UNIT0["wout"])
            dve.wait_ge(p_zero, 3)
            for hd in range(GLA_H):
                dve.wait_ge(gla_scores, hd + 1)
                dve.copy_predicated(T(gla_a, hd), cst_b[:, CAUSAL:CAUSAL + SEQ].bitcast(I32), bank[hd][:, :])\
                    .then_inc(gla_masked, 1)
            dve.wait_ge(gla_tr, 1)
            dve.tensor_copy(T(gla_kdt, 0), bank[5][:, :]).then_inc(gla_tr_read, 1)
            dve.wait_ge(gla_cs, 4)
            for c in range(NCH - 1):
                for t in range(2):
                    cs = T(bank[4 + 2 * t + c % 2], c // 2, P)
                    s_new = gla_s[:, (t * NCH + c + 1) * GLA_DV:(t * NCH + c + 2) * GLA_DV]
                    if c == 0:
                        dve.tensor_copy(s_new, cs).then_inc(gla_state, 1)
                    else:
                        s_old = gla_s[:, (t * NCH + c) * GLA_DV:(t * NCH + c + 1) * GLA_DV]
                        dve.wait_ge(gla_state, 2 * (c - 1) + t + 1)
                        dve.scalar_tensor_tensor(s_new, s_old, decay[:, t * NCH + c:t * NCH + c + 1], cs,
                                                 ALU.mult, ALU.add).then_inc(gla_state, 1)
            for hd in range(GLA_H):
                dve.wait_ge(gla_rms, hd + 1)
                dve.reciprocal(gla_sq_buf(hd), gla_sq_buf(hd)).then_inc(gla_r, 1)
                dve.wait_ge(gla_r, hd + 1)
                dve.wait_ge(silu_r, hd + 1)
                dve.tensor_tensor(T(z_r, hd), T(z_r, hd), gla_sq_buf(hd), ALU.mult).then_inc(gla_gated, 1)
                dve.wait_ge(gla_gated, hd + 1)
                dve.scalar_tensor_tensor(tmp[hd][:, 0:SEQ], bank[hd][:, :], col("gla_norm"), T(z_r, hd),
                                         ALU.mult, ALU.mult).then_inc(o_done, 1)
                if hd:
                    x_lo(SPLIT0["attn"] + 3 + hd, og_lo, og_hi, hd - 1, tmp[hd - 1][:, 0:SEQ])
            x_lo(SPLIT0["attn"] + 7, og_lo, og_hi, 3, tmp[3][:, 0:SEQ])

            for k in range(8):
                n = UNIT0["wout"] + k
                if k:
                    lo_ahead(n)
                unit_done(n)
                dve.tensor_tensor(T(h, k), T(h, k), bank[k % 4][:, :], ALU.add).then_inc(out_read, 1)
                x_lo(SPLIT0["ffn"] + k, a_lo, a_hi, k, T(h, k), col("ffn_norm", k))
            lo_ahead(UNIT0["upA"])
            take_r("ffn")
            if stage < 3:
                for k in range(KD):
                    dve.memset(small[:, 24 + k:25 + k], 0.0).then_inc(out_ready, 1)
                return

            def conv_col(i, j, half, tap):
                return col_at("conv", 16 * i + (8 * j + 4 * half + tap)) if not isinstance(i, int) else \
                    col("conv", 16 * i + 8 * j + 4 * half + tap)

            def up(name, split, first_pair, pairs):
                n0, x0 = UNIT0[name], SPLIT0[split]

                def product_lo(i, j):
                    dve.wait_ge(xhi_ready, 2 * i + (x0 + j + 1))
                    dve.tensor_tensor(at(g_lo, 2 * i + j), tmp[4 + j % 2][:, 0:SEQ], f(at(g_hi, 2 * i + j)),
                                      ALU.subtract).then_inc(x_ready, 1)

                def body(i):
                    for j in range(2):
                        pr = first_pair + j
                        begun = not isinstance(i, int) or i or j
                        for half in range(2):
                            if begun or half or name == "upB":
                                lo_ahead(n0 + 2 * j + half, i)
                            unit_done(n0 + 2 * j + half, i)
                            if begun:
                                dve.wait_ge(taps_a if half == 0 else taps_b, 2 * i + pr)
                            dve.tensor_tensor(tmp[half][:, 2:2 + SEQ], bank[2 * j + half][:, :], r_pre[:, :],
                                              ALU.mult).then_inc(out_read, 1)
                        for half in range(2):
                            dve.wait_ge(tap_mid, 4 * i + (2 * pr + half + 1))
                            dve.scalar_tensor_tensor(tmp[2 + half][:, 0:SEQ], tmp[half][:, 1:1 + SEQ],
                                                     conv_col(i, first_pair + j, half, 1), tmp[2 + half][:, 0:SEQ],
                                                     ALU.mult, ALU.add).then_inc(tap_one, 1)
                        for half in range(2):
                            dve.wait_ge(tap_one, 4 * i + (2 * pr + half + 1))
                            dve.scalar_tensor_tensor(tmp[2 + half][:, 0:SEQ], tmp[half][:, 0:SEQ],
                                                     conv_col(i, first_pair + j, half, 0), tmp[2 + half][:, 0:SEQ],
                                                     ALU.mult, ALU.add).then_inc(taps_a if half == 0 else taps_b, 1)
                        if begun:
                            product_lo(i, j - 1)
                body(0)
                looped(dve, pairs // 2, body, 1)
                product_lo(pairs // 2 - 1, 1)

            def down(name, units, final):
                n0, t0 = UNIT0[name], TILE0[name]
                for n in range(n0, n0 + units // 2):
                    lo_ahead(n)
                for g in range(2):
                    if g == 1:
                        for n in range(n0 + units // 2, n0 + units):
                            lo_ahead(n)
                    unit_done(n0 + (g + 1) * units // 2 - 1)
                    for j in range(4):
                        k = 4 * g + j
                        dve.tensor_tensor(T(h, k), T(h, k), bank[4 * g + j][:, :], ALU.add)\
                            .then_inc(out_read, 1)
                        if final:
                            x_lo(SPLIT0["pre0"] + k, a_lo, a_hi, k, T(h, k), col("pre", k))

            scaled("ffn")
            dve.wait_ge(p_zero, 5)
            up("upA", "prodA", 0, PAIRS_A)
            down("downA", PAIRS_A, False)
            up("upB", "prodB", PAIRS_A, PAIRS_B)
            down("downB", PAIRS_B, True)
            lo_ahead(UNIT0["pw1"])
            take_r("pre0")
            if stage < 4:
                for k in range(KD):
                    dve.memset(small[:, 24 + k:25 + k], 0.0).then_inc(out_ready, 1)
                return
            scaled("pre0")
            dve.wait_ge(p_zero, 5 + KD + 8)

            def glu(k):
                dve.wait_ge(ug_sig, k + 1)
                b = 2 * (k % 2)
                dve.scalar_tensor_tensor(u_pad[:, k * UW + CONV_W - 1:(k + 1) * UW], tmp[b][:, 0:SEQ],
                                         col("b_pw1", k), tmp[b + 1][:, 0:SEQ], ALU.add, ALU.mult).then_inc(u_ready, 1)

            def operand_lo(k):
                dve.wait_ge(uhi_ready, k + 1)
                o = (k % 4) * UW + CONV_W - 1
                dve.tensor_tensor(u_lo[:, o:o + SEQ], u_pad[:, k * UW + CONV_W - 1:(k + 1) * UW],
                                  f(u_hi[:, o:o + SEQ]), ALU.subtract).then_inc(ulo_ready, 1)

            def taps_dve(p):
                return CONV_W - 1 - TAPS_POOL - TAPS_PE[p]

            def taps_before(p):
                return 2 * sum(taps_dve(i) for i in range(p))

            def tap_ops(p, start, count):
                for q in range(start, min(start + count, 2 * taps_dve(p))):
                    c, tap = 2 * p + q % 2, TAPS_PE[p] + q // 2
                    if q < 2:
                        dve.wait_ge(pool_tap, TAPS_POOL * (c + 1))
                    else:
                        dve.wait_ge(dw_tap, taps_before(p) + q - 1)
                    dve.scalar_tensor_tensor(T(cv, c), u_pad[:, c * UW + tap:c * UW + tap + SEQ],
                                             col("w_dw", c * CONV_W + tap), T(cv, c), ALU.mult, ALU.add)\
                        .then_inc(dw_tap, 1)

            def add_pe_taps(p):
                unit_done(conv_step(p + 1)[1].stop - 1)
                dve.wait_ge(dw_tap, taps_before(p + 1))
                for c in (2 * p, 2 * p + 1):
                    dve.tensor_tensor(T(cv, c), T(cv, c), conv_bank(c)[:, :], ALU.add).then_inc(cv_ready, 1)

            for s in range(KD // 2 + 1):
                first, taps = conv_step(s)
                units = list(first) + list(taps)
                share = -(-2 * taps_dve(s - 1) // len(units)) if s else 0
                for q, n in enumerate(units):
                    if n > UNIT0["pw1"]:
                        lo_ahead(n)
                    if n in first:
                        k, e = 2 * s + q // 2, q % 2
                        unit_done(n)
                        if k >= 2:
                            dve.wait_ge(u_ready, k - 1)
                        dve.tensor_tensor(tmp[2 * (k % 2) + e][:, 0:SEQ], bank[q][:, :], r_pre[:, :], ALU.mult)\
                            .then_inc(out_read, 1)
                    if q == 0 and s >= 2:
                        add_pe_taps(s - 2)
                    if s:
                        tap_ops(s - 1, q * share, share)
                    if n in first and q % 2:
                        glu(2 * s + q // 2)
                    if n in first and q == 2:
                        operand_lo(2 * s)
                    if n in taps and n == taps.start and s < KD // 2:
                        operand_lo(2 * s + 1)
                if s == 0:
                    operand_lo(1)
            add_pe_taps(KD // 2 - 1)
            dve.wait_ge(mean_done, 1)
            for k in range(KD):
                dve.tensor_tensor(T(cv, k), T(cv, k), bank[4][:, :], ALU.subtract).then_inc(cen_ready, 1)
            lo_ahead(UNIT0["pw2"])
            take_r("ln_var")
            dve.wait_ge(spread_done, STAT_NO["ln_var"] + 1)
            for k in range(KD):
                dve.scalar_tensor_tensor(T(cv, k), T(cv, k), col("ln_g", k), bank[4][:, :], ALU.mult, ALU.mult)\
                    .then_inc(ln_ready, 1)
            for k in range(KD):
                dve.wait_ge(ln_silu, k + 1)
                x_lo(SPLIT0["conv"] + k, a_lo, a_hi, k, T(m, k))
            for k in range(KD):
                n = UNIT0["pw2"] + k
                if k:
                    lo_ahead(n)
                unit_done(n)
                dve.tensor_scalar(T(m, k), bank[k % 4][:, :], col("b_pw2", k), None, ALU.add).then_inc(out_read, 1)

            def post_norm(stat, gain, g0, h0, split=None, next_gain=None, ng0=0):
                take_r(stat)
                dve.wait_ge(spread_done, STAT_NO[stat] + 1)
                for k in range(KD):
                    link(dve.scalar_tensor_tensor(T(m, k), T(m, k), col(gain, g0 + k), bank[4][:, :],
                                                  ALU.mult, ALU.mult))
                    dve.tensor_tensor(T(h, k), T(h, k), T(m, k), ALU.add)\
                        .then_inc(h_ready if split else out_ready, 1)
                    if split and k:
                        x_lo(SPLIT0[split] + k - 1, a_lo, a_hi, k - 1, T(h, k - 1), col(next_gain, ng0 + k - 1))
                if split:
                    x_lo(SPLIT0[split] + KD - 1, a_lo, a_hi, KD - 1, T(h, KD - 1), col(next_gain, ng0 + KD - 1))

            post_norm("post0", "post", 0, H0["post0"], "ffpre0", "ffpre", 0)
            lo_ahead(UNIT0["ff1a0"])
            take_r("ffpre0")
            if stage < 5:
                for k in range(KD):
                    dve.memset(small[:, 24 + k:25 + k], 0.0).then_inc(out_ready, 1)
                return

            def feed_forward(layer):
                scaled(f"ffpre{layer}")
                for half in range(2):
                    c = "ab"[half]
                    n0, t0, x0 = UNIT0[f"ff1{c}{layer}"], TILE0[f"ff1{c}{layer}"], SPLIT0[f"hid{layer}{c}"]

                    def body(i):
                        for j in range(4):
                            if not isinstance(i, int) or j or half:
                                lo_ahead(n0 + j, i)
                            unit_done(n0 + j, i)
                            dve.scalar_tensor_tensor(tmp[j % 2][:, 0:SEQ], bank[j][:, :], 0.0, r_pre[:, :],
                                                     ALU.max, ALU.mult).then_inc(out_read, 1)
                            dve.wait_ge(hid_sq, 4 * i + (32 * layer + 16 * half + j + 1))
                            dve.wait_ge(xhi_ready, 4 * i + (x0 + j + 1))
                            dve.tensor_tensor(at(g_lo, 4 * i + j), tmp[2 + j % 2][:, 0:SEQ], f(at(g_hi, 4 * i + j)),
                                              ALU.subtract).then_inc(x_ready, 1)
                    body(0)
                    looped(dve, 4, body, 1)
                    name = f"ff2{c}{layer}"
                    n0 = UNIT0[name]

                    def first(i):
                        for j in range(2):
                            lo_ahead(n0 + 2 * j, i)
                            lo_ahead(n0 + 2 * j + 1, i)
                            unit_done(n0 + 2 * j + 1, i)
                            dve.tensor_copy(at(m, 2 * i + j), bank[j][:, :]).then_inc(out_read, 1)

                    if half == 0:
                        looped(dve, 4, first)
                        dve.wait_ge(out_read, TILE0[name] + 8)
                    else:
                        for k in range(KD):
                            lo_ahead(n0 + 2 * k)
                            lo_ahead(n0 + 2 * k + 1)
                            unit_done(n0 + 2 * k + 1)
                            dve.tensor_tensor(T(m, k), T(m, k), bank[k % 2][:, :], ALU.add).then_inc(out_read, 1)

            feed_forward(0)
            if stage < 6:
                post_norm("ffpost0", "ffpost", 0, H0["ffpost0"])
                return
            post_norm("ffpost0", "ffpost", 0, H0["ffpost0"], "kvpre", "kv_in", 0)
            lo_ahead(UNIT0["dkv"])
            for k in range(KD):
                x_lo(SPLIT0["pre1"] + k, b_lo, b_hi, k, T(h, k), col("pre", 8 + k))
            take_r("pre1")
            scaled("pre1")
            dests = [T(c_kv, 0), T(c_kv, 1), k_rope, T(c_q, 0), T(c_q, 1), T(c_q, 2)]
            for j in range(6):
                n = UNIT0["dkv"] + j
                if j:
                    lo_ahead(n)
                unit_done(n)
                dve.tensor_tensor(dests[j], bank[j % 3][:, :], r_pre[:, :], ALU.mult).then_inc(out_read, 1)

            def rotate(x, no):
                dve.wait_ge(rope_sw, no + 1)
                if no:
                    dve.wait_ge(rope_done, no)
                dve.tensor_tensor(tmp[0][:, 0:SEQ], bank[5][:, :], cst_b[:, SIN:SIN + SEQ], ALU.mult)\
                    .then_inc(rope_t, 1)
                dve.tensor_tensor(tmp[1][:, 0:SEQ], x, cst_b[:, COS:COS + SEQ], ALU.mult).then_inc(rope_t, 1)
                dve.wait_ge(rope_t, 2 * no + 2)
                dve.tensor_tensor(x, tmp[0][:, 0:SEQ], tmp[1][:, 0:SEQ], ALU.add).then_inc(rope_done, 1)

            dve.wait_ge(cst2_landed, 16)
            rotate(k_rope, 0)
            for k in range(5):
                gain = col("ckv_norm", k) if k < 2 else col("cq_norm", k - 2)
                x_lo(SPLIT0["ckv"] + k, a_lo, a_hi, k, T(m, k), gain)
            take_r("ckv")
            take_r("cq")
            scaled("ckv")
            for u in range(2):
                n = UNIT0["uk"] + u
                lo_ahead(n)
                unit_done(n)
                for j in range(4):
                    dve.tensor_tensor(T(k_nope, 4 * u + j), bank[j][:, :], r_post[:, :], ALU.mult)\
                        .then_inc(out_read, 1)
            dve.wait_ge(r_tok_ready, STAT_NO["ckv"] + 1)
            for u in range(2):
                n = UNIT0["uv"] + u
                lo_ahead(n)
                unit_done(n)
                for b in range(NB):
                    c = 4 * STAT_NO["ckv"] + b
                    dve.tensor_scalar(T(v_tok, b, MLA_H * V_DIM)[:, u * SEQ:(u + 1) * SEQ], bank[b][:, :],
                                      r_tok[:, c:c + 1], None, ALU.mult).then_inc(out_read, 1)
            scaled("cq")
            for u in range(6):
                n = UNIT0["uq"] + u
                lo_ahead(n)
                unit_done(n)
                for e in range(2):
                    j = 2 * u + e
                    dst = T(q_nope, j) if j < 8 else T(q_rope, j - 8)
                    dve.tensor_tensor(dst, bank[j % 4][:, :], r_pre[:, :], ALU.mult).then_inc(out_read, 1)
            for t in range(4):
                rotate(T(q_rope, t), 1 + t)

            def mla_max(i):
                nm = small[:, 32:36] if i % 2 == 0 else small[:, 40:44]
                for b in range(NB):
                    dve.wait_ge(mla_sc, NB * i + b + 1)
                    dve.tensor_reduce(nm[:, b:b + 1], bank[b][:, 0:(b + 1) * P], AX_X, ALU.max).then_inc(mla_mx, 1)
                dve.wait_ge(mla_mx, 5 * i + 4)
                dve.tensor_scalar(nm, nm, -MLA_SCALE, None, ALU.mult).then_inc(mla_mx, 1)

            lo_ahead(UNIT0["wo"])
            mla_max(0)
            for i in range(MLA_H):
                den = small[:, 36:40] if i % 2 == 0 else small[:, 44:48]
                dve.wait_ge(mla_exp, NB * (i + 1))
                link(dve.reciprocal(den, den))
                for b in range(NB):
                    o = P * b * (b + 1) // 2
                    x = prob[:, o:o + (b + 1) * P]
                    dve.tensor_scalar(x, x, den[:, b:b + 1], None, ALU.mult).then_inc(mla_pn, 1)
                if i + 1 < MLA_H:
                    mla_max(i + 1)
                dve.wait_ge(mla_tr, 3 * i + 1)
                if i:
                    dve.wait_ge(mla_pv, i)
                dve.tensor_copy(probT[:, 0:SEQ], bank[5][:, :]).then_inc(mla_ev, 1)
                dve.wait_ge(mla_tr, 3 * i + 3)
                dve.tensor_copy(probT[:, 2 * SEQ:2 * SEQ + 2 * P], bank[7][:, 0:2 * P]).then_inc(mla_ev, 1)
                x_lo(SPLIT0["mla"] + i, a_lo, a_hi, i, bank[4][:, :])
            for k in range(KD):
                n = UNIT0["wo"] + k
                if k:
                    lo_ahead(n)
                unit_done(n)
                dve.tensor_copy(T(m, k), bank[k % 4][:, :]).then_inc(out_read, 1)
            post_norm("post1", "post", 8, H0["post1"], "ffpre1", "ffpre", 8)
            lo_ahead(UNIT0["ff1a1"])
            take_r("ffpre1")
            feed_forward(1)
            post_norm("ffpost1", "ffpost", 8, None)


def _tiles(w):
    k, n = w.shape
    return w.reshape(k // P, P, n // P, P).transpose(2, 1, 0, 3).reshape(n // P, P, (k // P) * P)


def _pairs(w, kt, width):
    k, n = w.shape
    u = w.reshape(k // (kt * P), kt, P, n // width, width).transpose(3, 0, 2, 1, 4)
    return u.reshape(-1, P, kt * width)


def _stream(a):
    def pad(u):
        out = np.zeros((u.shape[0], P, UNIT), np.float32)
        out[:, :, :u.shape[2]] = u
        return out

    w_in = a["w_in"][0]
    qk = GLA_H * GLA_DK
    vw = GLA_H * GLA_DV
    o = np.cumsum([0, qk, qk, vw, vw, GLA_RANK, SWA_H * SWA_HD, SWA_KV * SWA_HD, SWA_KV * SWA_HD])
    gq, gk, gv, gr, glr, sq, sk, sv = (w_in[:, o[i]:o[i + 1]] for i in range(8))
    low = np.zeros((D, P), np.float32)
    low[:, :GLA_RANK] = glr
    sqp = sq.reshape(D, 2, 4, SWA_HD).transpose(0, 2, 1, 3).reshape(D, SWA_H * SWA_HD)
    units = [_tiles(sqp), _tiles(sk), _tiles(sv), _tiles(gq), _tiles(gk), _tiles(low), _tiles(gr), _pairs(gv, 2, 512)]
    w_out = a["w_out"][0]
    swa_rows = w_out[vw:].reshape(2, 4, SWA_HD, D).transpose(1, 0, 2, 3).reshape(SWA_H * SWA_HD, D)
    units.append(_tiles(np.concatenate([swa_rows, w_out[:vw]])))
    up = _tiles(a["w_up"][0])
    down = a["w_down"][0]
    both = np.stack([up[:UP_PAIRS], up[UP_PAIRS:]], 1)
    units += [both[:PAIRS_A].reshape(-1, P, UNIT), _pairs(down[:PAIRS_A * P], 2, 512)]
    units += [both[PAIRS_A:].reshape(-1, P, UNIT), _pairs(down[PAIRS_A * P:], 2, 512)]
    pw1 = _tiles(a["conv_w_pw1_2"][0])
    pw1 = np.stack([pw1[:KD], pw1[KD:]], 1).reshape(KD // 2, 4, P, UNIT)
    taps = a["conv_w_dw_2"][0].reshape(CONV_W, KD, P).transpose(1, 0, 2)
    diag = np.zeros((KD, CONV_W, P, P), np.float32)
    diag[:, :, np.arange(P), np.arange(P)] = taps
    for s in range(KD // 2 + 1):
        if s < KD // 2:
            units.append(pw1[s])
        if s:
            t = diag[2 * s - 2:2 * s, :TAPS_PE[s - 1]].reshape(-1, 8, P, P)
            units.append(t.transpose(0, 2, 1, 3).reshape(-1, P, UNIT))
    units.append(_tiles(a["conv_w_pw2_2"][0]))

    def ff(layer):
        w1 = _tiles(a["w_ff1_2"][layer])
        w2 = a["w_ff2_2"][layer]
        out = []
        for half in range(2):
            w = w2[half * 2048:(half + 1) * 2048].reshape(2, 1024, D)
            out += [w1[half * 16:(half + 1) * 16],
                    np.stack([_tiles(w[0]), _tiles(w[1])], 1).reshape(-1, P, UNIT)]
        return out
    units += ff(0)
    kr = a["kv_w_kr_2"]
    uq = a["mla_w_uq_2"][0].reshape(Q_RANK, MLA_H, NOPE + ROPE)
    units += [_tiles(a["kv_w_dkv_2"]), _tiles(np.concatenate([kr, kr], 1)), _tiles(a["mla_w_dq_2"][0])]
    units += [_pairs(a["kv_w_uk_2"], 2, 512), _pairs(a["kv_w_uv_2"], 2, 512)]
    uq2 = np.concatenate([uq[:, :, :NOPE].reshape(Q_RANK, -1), uq[:, :, NOPE:].reshape(Q_RANK, -1)], 1)
    units.append(pad(_pairs(uq2, 3, 256)))
    units.append(_tiles(a["mla_w_o_2"][0]))
    units += ff(1)
    out = np.concatenate(units)
    assert out.shape == (N_UNITS, P, UNIT)
    return out.reshape(N_UNITS * P, UNIT)


def _vectors(a):
    def c(v):
        return v.reshape(-1, P).T

    conv = np.concatenate([a["conv_w"][0], a["conv_b"]], 0)
    conv = conv.reshape(4, 2, UP_PAIRS, P).transpose(3, 2, 1, 0).reshape(P, -1)
    dw = a["conv_w_dw_2"][0].reshape(CONV_W, KD, P).transpose(2, 1, 0).reshape(P, -1)
    return np.concatenate([
        c(a["mix_norm"][0]), c(a["b_alpha"][0]), c(a["gla_norm"][0]), c(np.tile(a["q_norm"][0], 2)),
        c(np.tile(a["k_norm"][0], 2)), np.broadcast_to(a["sinks"], (P, SWA_H)), c(a["ffn_norm"][0]), conv,
        c(a["mix_pre_g_2"]), c(a["mix_post_g_2"]), c(a["ffn_pre_g_2"]), c(a["ffn_post_g_2"]), c(a["conv_b_pw1_2"][0]),
        dw, c(a["conv_b_dw_2"][0]), c(a["conv_ln_g_2"][0]), c(a["conv_ln_b_2"][0]), c(a["conv_b_pw2_2"][0]),
        c(a["kv_in_g_2"]), c(a["kv_norm_g_2"]), c(a["mla_q_norm_g_2"][0])], 1)


def _consts():
    i = np.arange(P)
    both = np.concatenate([np.eye(P), np.ones((P, P)), np.full((P, P), 1.0 / D), i[:, None] == (i[None, :] ^ 32),
                           (i[:, None] // 64) == np.arange(2)[None, :]], 1).astype(np.float32)
    one = np.zeros((P, N_CONST), np.float32)
    causal = (i[:, None] <= i[None, :]) & (i[:, None] // CHUNK == i[None, :] // CHUNK)
    one[:, CAUSAL:CAUSAL + SEQ] = np.tile(causal, (1, NB))
    one[:, RESET:RESET + SEQ] = (np.arange(SEQ) % CHUNK != 0)
    dist = WINDOW + i[:, None] - np.arange(2 * WINDOW)[None, :]
    seen = (dist >= 0) & (dist < WINDOW)
    d = np.where(seen, -dist, NEG).astype(np.float32)
    first = np.where(np.arange(2 * WINDOW)[None, :] >= WINDOW, d, np.float32(NEG))
    one[:, DIST:DIST + 768] = np.concatenate([first, d, d], 1)
    two = np.zeros((P, N_CONST), np.float32)
    half = ROPE // 2
    inv = (1.0 / (np.float32(10000.0) ** (np.arange(0, ROPE, 2, dtype=np.float32) / np.float32(ROPE)))).astype(np.float32)
    ang = np.arange(SEQ, dtype=np.float32)[:, None] * inv[None, :]
    cos, sin = np.cos(ang).T, np.sin(ang).T
    two[:, COS:COS + SEQ] = np.tile(cos, (P // half, 1))
    two[:, SIN:SIN + SEQ] = np.tile(np.concatenate([-sin, sin]), (2, 1))
    two[:, MASK_Q:MASK_Q + P] = i[None, :] < CHUNK
    two[:, MASK_K:MASK_K + P] = np.where(i[None, :] >= CHUNK, NEG, 0.0)
    return both, one, two


def kernel(**inputs):
    import concourse.bacc as _bacc
    from concourse import mybir as _mybir
    from concourse.bass_utils import run_bass_kernel_spmd as _run

    a = {k: np.asarray(v) for k, v in inputs.items()}
    both, one, two = _consts()
    w_alpha = np.zeros((P, 256), np.float32)
    w_alpha[:GLA_RANK] = a["w_alpha2"][0]
    arrays = {
        "in_xT": np.ascontiguousarray(a["x"][0].T), "in_stream": _stream(a), "in_vectors": _vectors(a),
        "in_w_alpha": w_alpha, "in_consts": both, "in_consts1": one, "in_consts2": two,
    }
    arrays = {k: np.ascontiguousarray(v) for k, v in arrays.items()}
    nc = _bacc.Bacc("TRN2", target_bir_lowering=False, num_devices=1)
    args = [nc.dram_tensor(k, v.shape, _mybir.dt.float32, kind="ExternalInput").ap() for k, v in arrays.items()]
    out = nc.dram_tensor("out_0", (D, SEQ), _mybir.dt.float32, kind="ExternalOutput").ap()
    program(nc, *args, out)
    r = _run(nc, [arrays], core_ids=[0])
    got = r.results[0]["out_0"]
    return np.ascontiguousarray(got.T)[None]
```

```python
from contextlib import ExitStack

import numpy as np

import concourse.bass as bass
from concourse import mybir

F32 = mybir.dt.float32
F32R = mybir.dt.float32r
I32 = mybir.dt.int32
ALU = mybir.AluOpType
ACT = mybir.ActivationFunctionType
AX_X = mybir.AxisListType.X

P = 128
SEQ = 512
D = 1024
KD = D // P
UNIT = 1024
RING = 4
AHEAD = 3
EPS = 1e-6
LN_EPS = 1e-5
NEG = -1e30

GLA_H, GLA_DK, GLA_DV, GLA_RANK, CHUNK = 4, 64, 128, 16, 64
SWA_H, SWA_KV, SWA_HD, WINDOW = 8, 2, 64, 128
D_FF = 2816
UP_PAIRS = D_FF // P
PAIRS_A = 12
PAIRS_B = UP_PAIRS - PAIRS_A
D_FF_2 = 4096
CONV_W = 31
TAPS_PE = [12, 12, 16, 16]
TAPS_POOL = [2, 2, 3, 4]
MLA_H, NOPE, ROPE, V_DIM, Q_RANK, KV_RANK = 8, 128, 64, 128, 384, 256
MLA_SCALE = float(NOPE + ROPE) ** -0.5
NB = SEQ // P
NCH = SEQ // CHUNK
N_PROB = P * NB * (NB + 1) // 2
DQ_BANK = (3, 0, 1)

PRODUCTS = [
    ("z", 19, 19), ("wout", 8, 8),
    ("upA", 2 * PAIRS_A, 2 * PAIRS_A), ("downA", PAIRS_A, 8),
    ("upB", 2 * PAIRS_B, 2 * PAIRS_B), ("downB", PAIRS_B, 8),
    ("pw1", 16 + sum(TAPS_PE) // 4, 16), ("pw2", 8, 8),
    ("ff1a0", 16, 16), ("ff2a0", 16, 8), ("ff1b0", 16, 16), ("ff2b0", 16, 8),
    ("dkv", 3, 3), ("dq", 3, 3), ("uk", 2, 8), ("uq", 6, 12), ("uv", 2, 8), ("wo", 8, 8),
    ("ff1a1", 16, 16), ("ff2a1", 16, 8), ("ff1b1", 16, 16), ("ff2b1", 16, 8),
]
UNIT0, TILE0 = {}, {}
_u = _t = 0
for _name, _units, _tiles in PRODUCTS:
    UNIT0[_name], TILE0[_name] = _u, _t
    _u, _t = _u + _units, _t + _tiles
N_UNITS = _u

SPLITS = [
    ("mix", 8), ("attn", 8), ("ffn", 8), ("prodA", PAIRS_A), ("prodB", PAIRS_B), ("pre0", 8), ("conv", 8),
    ("ffpre0", 8), ("hid0a", 16), ("hid0b", 16), ("kvpre", 8), ("pre1", 8), ("ckv", 2), ("cq", 3), ("mla", 8),
    ("ffpre1", 8), ("hid1a", 16), ("hid1b", 16),
]
SPLIT0 = {}
_x = 0
for _name, _n in SPLITS:
    SPLIT0[_name] = _x
    _x += _n

STATS = [
    ("mix", 8), ("ffn", 8), ("pre0", 8), ("ln_var", 8), ("post0", 8), ("ffpre0", 8), ("ffpost0", 8),
    ("pre1", 8), ("ckv", 2), ("cq", 3), ("post1", 8), ("ffpre1", 8), ("ffpost1", 8),
]
STAT_NO, SQ0, ADD0, STAT_TILES = {}, {}, {}, {}
_s = _a = 0
for _i, (_name, _n) in enumerate(STATS):
    STAT_NO[_name], SQ0[_name], ADD0[_name], STAT_TILES[_name] = _i, _s, _a, _n
    _s, _a = _s + _n, _a + (max(_n - 2, 0) if _name != "ln_var" else KD // 2)

R_NO = {name: i for i, name in enumerate(n for n, _ in STATS if "post" not in n and n != "ln_var")}

RC_SWA = 4 * len(STATS)
RC_GLA = RC_SWA + 40
N_RC = RC_GLA + 16

VECTORS = [
    ("mix_norm", 8), ("b_alpha", 2), ("gla_norm", 1), ("q_norm", 1), ("k_norm", 1), ("sinks", 8), ("ffn_norm", 8),
    ("conv", 4 * 2 * UP_PAIRS), ("pre", 16), ("post", 16), ("ffpre", 16), ("ffpost", 16), ("b_pw1", 16),
    ("w_dw", 8 * CONV_W), ("b_dw", 8), ("ln_g", 8), ("ln_b", 8), ("b_pw2", 8), ("kv_in", 8), ("ckv_norm", 2),
    ("cq_norm", 3),
]
COL0 = {}
_c = 0
for _name, _n in VECTORS:
    COL0[_name] = _c
    _c += _n
N_COLS = _c

IDENT, ONES, MEAN, SWAP, HALVES = 0, P, 2 * P, 3 * P, 4 * P
N_CST = 4 * P + 2
CAUSAL, RESET, DIST = 0, SEQ, 2 * SEQ
COS, SIN, MASK_Q, MASK_K = 0, SEQ, 2 * SEQ, 2 * SEQ + P
N_CONST = 2 * SEQ + 3 * 256


def program(nc, xT, stream, vectors, w_alpha, consts, consts1, consts2, outT):
    ctx = ExitStack()
    with ctx:
        def sb(name, shape, dtype=F32, where=ctx):
            return where.enter_context(nc.sbuf_tensor(name, shape, dtype))

        def sem(name):
            return ctx.enter_context(nc.semaphore(name))

        h = sb("h", [P, KD * SEQ])
        at_m = ExitStack()
        prob = sb("prob", [P, N_PROB], where=at_m)
        pt_hi = sb("pt_hi", [P, N_PROB], F32R, at_m)
        pt_lo = sb("pt_lo", [P, N_PROB], F32R, at_m)
        at_m.close()
        m = sb("m", [P, KD * SEQ])
        w_raw = [sb(f"w_raw{i}", [P, UNIT]) for i in range(RING)]
        w_hi = [sb(f"w_hi{i}", [P, UNIT], F32R) for i in range(RING)]
        w_lo = [sb(f"w_lo{i}", [P, UNIT], F32R) for i in range(RING)]
        cst = sb("cst", [P, N_CST])
        cst_b = sb("cst_b", [P, N_CONST])
        cols = sb("cols", [P, N_COLS])
        TW = SEQ + 8
        tmp = [sb(f"tmp{i}", [P, TW]) for i in range(6)]
        ssum = sb("ssum", [P, SEQ])
        r_pre = sb("r_pre", [P, SEQ])
        r_post = sb("r_post", [P, SEQ])
        small = sb("small", [P, 64 + len(STATS) + 2])
        rms = sb("rms", [P, N_RC])
        r_tok = sb("r_tok", [P, N_RC])
        b_last = sb("b_last", [P, 2 * NCH])
        decay = sb("decay", [P, 2 * NCH])
        sq_buf = [tmp[4][:, 0:SEQ], tmp[5][:, 0:SEQ]]

        at_a = ExitStack()
        a_hi = sb("a_hi", [P, KD * SEQ], F32R, at_a)
        a_lo = sb("a_lo", [P, KD * SEQ], F32R, at_a)
        at_a.close()
        at_a = ExitStack()
        gla_kdt = sb("gla_kdt", [P, 2 * SEQ], where=at_a)
        gla_s = sb("gla_s", [P, 2 * NCH * GLA_DV], where=at_a)
        gla_a = sb("gla_a", [P, GLA_H * SEQ], where=at_a)
        at_a.close()
        sb("a_region", [P, 2 * KD * SEQ])

        big = ExitStack()
        os_hi = sb("os_hi", [P, 4 * SEQ], F32R, big)
        os_lo = sb("os_lo", [P, 4 * SEQ], F32R, big)
        at_o = ExitStack()
        og_hi = sb("og_hi", [P, 4 * SEQ], F32R, at_o)
        og_lo = sb("og_lo", [P, 4 * SEQ], F32R, at_o)
        at_o.close()
        swa_p = [sb(f"swa_p{i}", [P, NB * 256], where=big) for i in range(2)]
        swa_pt = [sb(f"swa_pt{i}", [P, NB * 256], where=big) for i in range(2)]
        z_q = sb("z_q", [P, 2 * SEQ], where=big)
        z_k = sb("z_k", [P, 2 * SEQ], where=big)
        z_sq = sb("z_sq", [P, 4 * SEQ], where=big)
        z_v = sb("z_v", [P, NB * SEQ], where=big)
        z_sk = sb("z_sk", [P, P + SEQ], where=big)
        z_vs = sb("z_vs", [P, NB * P], where=big)
        z_lr = sb("z_lr", [P, SEQ], where=big)
        w_al = sb("w_al", [P, 256], where=big)
        big.close()
        z_r = m[:, 0:4 * SEQ]
        gla_b, gla_e = m[:, 4 * SEQ:6 * SEQ], m[:, 6 * SEQ:8 * SEQ]
        big = ExitStack()
        g_hi = sb("g_hi", [P, 16 * SEQ], F32R, big)
        g_lo = sb("g_lo", [P, 16 * SEQ], F32R, big)
        big.close()
        big = ExitStack()
        UW = SEQ + CONV_W - 1
        u_pad = sb("u_pad", [P, KD * UW], where=big)
        cv = sb("cv", [P, KD * SEQ], where=big)
        u_hi = sb("u_hi", [P, 4 * UW], F32R, big)
        u_lo = sb("u_lo", [P, 4 * UW], F32R, big)
        big.close()
        big = ExitStack()
        at_k = ExitStack()
        k_nope = sb("k_nope", [P, MLA_H * SEQ], where=at_k)
        at_k.close()
        mo_hi = sb("mo_hi", [P, MLA_H * SEQ], F32R, big)
        v_hi = sb("v_hi", [P, NB * MLA_H * V_DIM], F32R, big)
        small_mla = ExitStack()
        b_hi = sb("b_hi", [P, KD * SEQ], F32R, small_mla)
        b_lo = sb("b_lo", [P, KD * SEQ], F32R, small_mla)
        small_mla.close()
        small_mla = ExitStack()
        q_nope = sb("q_nope", [P, MLA_H * SEQ], where=small_mla)
        small_mla.close()
        small_mla = ExitStack()
        mo_lo = sb("mo_lo", [P, MLA_H * SEQ], F32R, small_mla)
        qr_hi = sb("qr_hi", [P, 4 * SEQ], F32R, small_mla)
        qr_lo = sb("qr_lo", [P, 4 * SEQ], F32R, small_mla)
        small_mla.close()
        big.close()
        sb("big_region", [P, 32 * SEQ])
        c_kv, c_q = m[:, 0:2 * SEQ], m[:, 2 * SEQ:5 * SEQ]
        k_rope = tmp[2][:, 0:SEQ]
        q_rope = m[:, 0:4 * SEQ]
        kr_hi, kr_lo = a_lo[:, 5 * SEQ:6 * SEQ], a_lo[:, 6 * SEQ:7 * SEQ]

        def v_lo(b):
            return a_hi[:, (2 + 2 * b) * SEQ:(4 + 2 * b) * SEQ] if b < 3 else a_lo[:, 2 * SEQ:4 * SEQ]

        bank = [ctx.enter_context(nc.psum_tensor(f"bank{i}", [P, SEQ], F32)) for i in range(8)]

        h_landed = [sem(f"h_landed{k}") for k in range(KD)]
        vec_landed = sem("vec_landed")
        cst_landed = sem("cst_landed")
        cst2_landed = sem("cst2_landed")
        w_landed = [sem(f"w_landed{i}") for i in range(RING)]
        whi_ready = sem("whi_ready")
        wlo_ready = sem("wlo_ready")
        unit_used = sem("unit_used")
        out_read = sem("out_read")
        xhi_ready = sem("xhi_ready")
        x_ready = sem("x_ready")
        sq_ready = sem("sq_ready")
        sum_added = sem("sum_added")
        stat_done = sem("stat_done")
        r_ready = sem("r_ready")
        out_stored = sem("out_stored")
        out_ready = sem("out_ready")
        out_scaled = sem("out_scaled")
        out_added = sem("out_added")
        rms_ready = sem("rms_ready")
        r_tok_ready = sem("r_tok_ready")
        spread_done = sem("spread_done")
        mean_done = sem("mean_done")
        swa_sq = sem("swa_sq")
        swa_sums = sem("swa_sums")
        swa_rms = sem("swa_rms")
        swa_r = sem("swa_r")
        sv_turned = sem("sv_turned")
        sv_copied = sem("sv_copied")
        sk_spread = sem("sk_spread")
        swa_dist = sem("swa_dist")
        gla_sq = sem("gla_sq")
        gla_sums = sem("gla_sums")
        gla_r = sem("gla_r")
        gla_spread = sem("gla_spread")
        v_chain = sem("v_chain")
        a_chain = sem("a_chain")
        p_zero = sem("p_zero")
        gla_y = sem("gla_y")
        gla_l = sem("gla_l")
        gla_ls = sem("gla_ls")
        gla_cum = sem("gla_cum")
        gla_exp = sem("gla_exp")
        gla_ops = sem("gla_ops")
        gla_blast = sem("gla_blast")
        gla_logit = sem("gla_logit")
        gla_scores = sem("gla_scores")
        gla_masked = sem("gla_masked")
        gla_tr = sem("gla_tr")
        gla_tr_read = sem("gla_tr_read")
        gla_cs = sem("gla_cs")
        gla_state = sem("gla_state")
        gla_o = sem("gla_o")
        gla_rms = sem("gla_rms")
        gla_gated = sem("gla_gated")
        silu_r = sem("silu_r")
        o_done = sem("o_done")
        k_normed = sem("k_normed")
        swa_sc = sem("swa_sc")
        swa_bias = sem("swa_bias")
        swa_mx = sem("swa_mx")
        swa_exp = sem("swa_exp")
        swa_se = sem("swa_se")
        swa_pn = sem("swa_pn")
        swa_tr = sem("swa_tr")
        swa_ev = sem("swa_ev")
        swa_ea = sem("swa_ea")
        swa_pv = sem("swa_pv")
        taps_a = sem("taps_a")
        taps_b = sem("taps_b")
        tap_mid = sem("tap_mid")
        tap_one = sem("tap_one")
        gated = sem("gated")
        prod = sem("prod")
        ug_sig = sem("ug_sig")
        u_ready = sem("u_ready")
        uhi_ready = sem("uhi_ready")
        ulo_ready = sem("ulo_ready")
        last_tap = sem("last_tap")
        tap_product = sem("tap_product")
        pool_tap = sem("pool_tap")
        dw_tap = sem("dw_tap")
        cv_ready = sem("cv_ready")
        mean_add = sem("mean_add")
        cen_ready = sem("cen_ready")
        ln_ready = sem("ln_ready")
        ln_silu = sem("ln_silu")
        h_ready = sem("h_ready")
        hid_sq = sem("hid_sq")
        rope_sw = sem("rope_sw")
        rope_t = sem("rope_t")
        rope_done = sem("rope_done")
        rope_hi = sem("rope_hi")
        rope_split = sem("rope_split")
        v_hi_ready = sem("v_hi_ready")
        mla_sc = sem("mla_sc")
        mla_mx = sem("mla_mx")
        mla_exp = sem("mla_exp")
        mla_pn = sem("mla_pn")
        mla_tr = sem("mla_tr")
        mla_ev = sem("mla_ev")
        mla_ea = sem("mla_ea")
        mla_pv = sem("mla_pv")

        def T(t, k, w=SEQ):
            return t[:, k * w:(k + 1) * w]

        def col(name, k=0):
            c = COL0[name] + k
            return cols[:, c:c + 1]

        def col_at(name, k):
            return cols[:, bass.ds(COL0[name] + k, 1)]

        def f(x):
            return x.bitcast(F32)

        def at(t, i, w=SEQ):
            return t[:, bass.ds(i * w, w)] if not isinstance(i, int) else t[:, i * w:(i + 1) * w]

        def swa_head(i):
            return i // 2 + 4 * (i % 2)

        def swa_sq_buf(n):
            return ssum[:, :] if n % 3 == 0 else sq_buf[n % 3 - 1]

        def rope_bank(no):
            return bank[(5, 5, 6, 7, 4)[no]]

        def ln_sq_buf(k):
            return (ssum[:, :], sq_buf[0], sq_buf[1], r_post[:, :])[k] if k < 4 else tmp[k - 4][:, 0:SEQ]

        def gla_sq_buf(hd):
            return (ssum[:, :], sq_buf[0], sq_buf[1], r_post[:, :])[hd]

        def r_cols(c, width=P):
            return r_tok[:, c:c + 1].broadcast_to([P, width])

        def swa_bias_t(i):
            return tmp[4 + i % 2][:, 0:SEQ]

        def looped(eng, n, body, first=0):
            with eng.Fori(first, n) as i:
                body(i)

        H0 = {"post0": 0, "ffpost0": 8, "post1": 16}

        mla_cols = {0: (5, 0, 0), 1: (6, 0, SEQ), 3: (6, 3 * P, SEQ + 3 * P), 2: (7, 0, 2 * SEQ)}
        mla_parts = ((5, 0, SEQ), (6, SEQ, 2 * SEQ), (7, 2 * SEQ, N_PROB))

        def conv_step(s):
            n = UNIT0["pw1"] + 4 * s + sum(TAPS_PE[:max(s - 1, 0)]) // 4
            first = range(n, n + 4) if s < KD // 2 else range(n, n)
            taps = range(first.stop, first.stop + TAPS_PE[s - 1] // 4) if s else range(n, n)
            return first, taps

        def pool_taps(c):
            return sum(TAPS_POOL[k // 2] for k in range(c))

        def conv_bank(c):
            return bank[4 + c % 4]

        def o_tiles(k):
            return (T(os_hi, k), T(os_lo, k)) if k < 4 else (T(og_hi, k - 4), T(og_lo, k - 4))

        block = ctx.enter_context(nc.Block())

        @block.sync
        def _(sp):
            def load(n, slot):
                if not isinstance(n, int) or n >= RING:
                    sp.wait_ge(wlo_ready, n - RING + 1)
                src = stream[bass.ds(n * P, P), :] if not isinstance(n, int) else stream[n * P:(n + 1) * P, :]
                sp.dma_start(w_raw[slot][:, :], src).then_inc(w_landed[slot], 16)

            sp.dma_start(cols[:, :], vectors).then_inc(vec_landed, 16)
            sp.dma_start(h[:, 0:SEQ], xT[0:P, :]).then_inc(h_landed[0], 16)
            load(0, 0)
            for k in range(1, KD):
                sp.dma_start(T(h, k), xT[k * P:(k + 1) * P, :]).then_inc(h_landed[k], 16)
                if k in (2, 4):
                    load(k // 2, k // 2)
            load(3, 3)
            sp.dma_start(cst[:, :], consts).then_inc(cst_landed, 16)
            sp.dma_start(cst_b[:, :], consts1).then_inc(cst_landed, 16)
            sp.dma_start(w_al[:, :], w_alpha).then_inc(cst_landed, 16)

            def four(i):
                for j in range(RING):
                    load(4 * i + (RING + j), j)
            rounds = (N_UNITS - RING) // RING
            looped(sp, rounds, four)
            for n in range(RING + RING * rounds, N_UNITS):
                load(n, n % RING)
            for k in range(KD):
                sp.wait_ge(out_added if k % 2 else out_ready, k // 2 + 1)
                sp.dma_start(outT[k * P:(k + 1) * P, :], T(h, k)).then_inc(out_stored, 16)
            sp.wait_ge(out_stored, 16 * KD)
            sp.wait_ge(cst2_landed, 16)

        @block.gpsimd
        def _(pool):
            def add_squares(name):
                for k in range(1, STAT_TILES[name] - 1):
                    pool.wait_ge(sq_ready, SQ0[name] + k + 1)
                    if k >= 2:
                        pool.wait_ge(sum_added, ADD0[name] + k - 1)
                    pool.tensor_tensor(ssum[:, :], ssum[:, :], sq_buf[(k - 1) % 2], ALU.add).then_inc(sum_added, 1)

            def gate_products(name, pairs):
                base = 0 if name == "prodA" else PAIRS_A

                def body(i):
                    for j in range(2):
                        pool.wait_ge(gated, 2 * i + (base + j + 1))
                        pool.wait_ge(taps_b, 2 * i + (base + j + 1))
                        pool.tensor_tensor(tmp[4 + j][:, 0:SEQ], tmp[4 + j][:, 0:SEQ], tmp[3][:, 0:SEQ], ALU.mult)\
                            .then_inc(prod, 1)
                looped(pool, pairs // 2, body)

            def hidden_squares(half):
                def body(i):
                    for j in range(4):
                        pool.wait_ge(out_read, 4 * i + (TILE0[f"ff1{half[1]}{half[0]}"] + j + 1))
                        pool.wait_ge(x_ready, 4 * i + (SPLIT0[f"hid{half}"] + j - 1))
                        pool.tensor_tensor(tmp[2 + j % 2][:, 0:SEQ], tmp[j % 2][:, 0:SEQ], tmp[j % 2][:, 0:SEQ],
                                           ALU.mult).then_inc(hid_sq, 1)
                looped(pool, 4, body)

            pool.memset(z_sk[:, 0:P], 0.0).then_inc(p_zero, 1)
            add_squares("mix")
            pool.wait_ge(swa_sums, 5)
            for i in range(SWA_H):
                if i >= 2:
                    pool.wait_ge(swa_bias, NB * (i - 1))
                slope = 2.0 ** (-8.0 * (swa_head(i) + 1) / SWA_H) * SWA_HD ** 0.5
                pool.tensor_scalar(swa_bias_t(i), cst_b[:, DIST:DIST + SEQ], slope, None, ALU.mult)\
                    .then_inc(swa_dist, 1)
            pool.wait_ge(unit_used, UNIT0["wout"])
            for t in range(2):
                pool.memset(gla_a[:, 2 * t * SEQ:2 * (t + 1) * SEQ], 0.0).then_inc(p_zero, 1)
            add_squares("ffn")
            for i in range(2):
                pool.memset(tmp[i][:, 0:2], 0.0).then_inc(p_zero, 1)
            gate_products("prodA", PAIRS_A)
            gate_products("prodB", PAIRS_B)
            add_squares("pre0")
            pool.wait_ge(unit_used, UNIT0["pw1"])
            for k in range(KD):
                pool.memset(u_pad[:, k * UW:k * UW + CONV_W - 1], 0.0).then_inc(p_zero, 1)
            for t in (u_hi, u_lo):
                for k in range(4):
                    pool.memset(t[:, k * UW:k * UW + CONV_W - 1].bitcast(F32), 0.0).then_inc(p_zero, 1)

            def add_taps(k):
                pool.wait_ge(last_tap, k + 1)
                for j in range(TAPS_POOL[k // 2]):
                    no = pool_taps(k) + j
                    pool.wait_ge(tap_product, no + 1)
                    if j:
                        pool.wait_ge(pool_tap, no)
                    pool.tensor_tensor(T(cv, k), T(cv, k), sq_buf[no % 2], ALU.add).then_inc(pool_tap, 1)

            def add_tile(k):
                pool.wait_ge(cv_ready, k + 1)
                if k == 0:
                    pool.wait_ge(stat_done, STAT_NO["ln_var"])
                    pool.tensor_copy(ssum[:, :], T(cv, 0)).then_inc(mean_add, 1)
                else:
                    pool.wait_ge(mean_add, k)
                    pool.tensor_tensor(ssum[:, :], ssum[:, :], T(cv, k), ALU.add).then_inc(mean_add, 1)

            for p in range(KD // 2):
                if p >= 2:
                    add_tile(2 * p - 4)
                    add_tile(2 * p - 3)
                add_taps(2 * p)
                add_taps(2 * p + 1)
            add_tile(KD - 4)
            add_tile(KD - 3)
            for p in range(KD // 2):
                pool.wait_ge(sq_ready, SQ0["ln_var"] + 2 * p + 2)
                pool.tensor_tensor(ln_sq_buf(2 * p), ln_sq_buf(2 * p), ln_sq_buf(2 * p + 1), ALU.add)\
                    .then_inc(sum_added, 1)
            add_squares("post0")
            add_squares("ffpre0")
            for layer in range(2):
                if layer == 1:
                    add_squares("pre1")
                    add_squares("ckv")
                    add_squares("cq")
                    add_squares("post1")
                    add_squares("ffpre1")
                hidden_squares(f"{layer}a")
                hidden_squares(f"{layer}b")
                add_squares(f"ffpost{layer}")
            for k in range(1, KD, 2):
                pool.wait_ge(out_scaled, (k + 1) // 2)
                pool.tensor_tensor(T(h, k), T(h, k), T(m, k), ALU.add).then_inc(out_added, 1)

        @block.scalar
        def _(act):
            def w_hi_of(n, slot):
                if n >= N_UNITS:
                    return
                act.wait_ge(w_landed[slot], 16 * (n // RING + 1))
                if n >= RING:
                    act.wait_ge(unit_used, n - RING + 1)
                act.activation(w_hi[slot][:, :], w_raw[slot][:, :], ACT.Copy).then_inc(whi_ready, 1)

            def w_hi_loop(n0, i, j):
                n = n0 + j + AHEAD
                slot = n % RING
                if isinstance(i, int):
                    return w_hi_of(n + 4 * i, slot)
                act.wait_ge(w_landed[slot], 16 * i + 16 * (n // RING + 1))
                act.wait_ge(unit_used, 4 * i + (n - RING + 1))
                act.activation(w_hi[slot][:, :], w_raw[slot][:, :], ACT.Copy).then_inc(whi_ready, 1)

            def square(name, k, src, n=D):
                if k == 0:
                    if STAT_NO[name]:
                        act.wait_ge(stat_done, STAT_NO[name])
                    dst = ssum[:, :]
                else:
                    if k >= 3:
                        act.wait_ge(sum_added, ADD0[name] + k - 2)
                    dst = sq_buf[(k - 1) % 2]
                act.activation(dst, src, ACT.Square, scale=float(n) ** -0.5).then_inc(sq_ready, 1)

            def load_sqrt(no):
                act.activation(small[:, 64 + no:65 + no], small[:, 60:61], ACT.Sqrt)

            def take_root(name, dst, eps=EPS, sums=4):
                c = 4 * STAT_NO[name]
                act.wait_ge(stat_done, STAT_NO[name] + 1)
                act.activation(rms[:, c:c + NB], bank[sums][:, 0:NB], ACT.Sqrt,
                               bias=small[:, 60:61] if eps == EPS else small[:, 61:62]).then_inc(rms_ready, 1)
                if dst is not None:
                    act.wait_ge(spread_done, STAT_NO[name] + 1)
                    act.activation(dst[:, :], bank[4][:, :], ACT.Copy).then_inc(r_ready, 1)

            def x_hi(dst, k, src, gain):
                act.activation(T(dst, k), src, ACT.Identity, scale=gain).then_inc(xhi_ready, 1)

            act.wait_ge(vec_landed, 16)
            for k in range(KD):
                act.wait_ge(h_landed[k], 16)
                x_hi(a_hi, k, T(h, k), col("mix_norm", k))
                if k in (0, 2, 4):
                    w_hi_of(k // 2, k // 2)
                square("mix", k, T(h, k))
            w_hi_of(AHEAD, AHEAD)
            act.wait_ge(v_chain, 2)
            take_root("mix", r_pre)
            z0 = UNIT0["z"]
            for n in range(z0, z0 + 6):
                if n > z0:
                    w_hi_of(n + AHEAD, (n + AHEAD) % RING)
                if n < z0 + 5:
                    src = T(z_sq, n) if n < 4 else z_sk[:, P:]
                    act.wait_ge(out_read, n + 1)
                    if n == z0:
                        act.wait_ge(stat_done, 1)
                    if n >= 3:
                        act.wait_ge(swa_sums, n - 2)
                    act.activation(swa_sq_buf(n), src, ACT.Square, scale=SWA_HD ** -0.5).then_inc(swa_sq, 1)
            load_sqrt(len(STATS))
            act.wait_ge(swa_sums, 5)
            act.activation(rms[:, RC_SWA:RC_SWA + 40], bank[4][:, 0:40], ACT.Sqrt, bias=small[:, 60:61])\
                .then_inc(swa_rms, 1)
            act.wait_ge(sv_turned, 1)
            act.activation(z_vs[:, :], bank[6][:, :], ACT.Copy).then_inc(sv_copied, 1)

            def swa_exp_of(i):
                p = swa_p[i % 2]
                act.wait_ge(swa_mx, 2 * (i + 1))
                nm = small[:, 32:36] if i % 2 == 0 else small[:, 40:44]
                den = small[:, 36:40] if i % 2 == 0 else small[:, 44:48]
                se = small[:, 48:52] if i % 2 == 0 else small[:, 52:56]
                act.activation(se, nm, ACT.Exp, bias=col("sinks", swa_head(i))).then_inc(swa_se, 1)
                for b in range(NB):
                    act.activation(T(p, b, 256), T(p, b, 256), ACT.Exp, scale=SWA_HD ** -0.5, bias=nm[:, b:b + 1],
                                   accum_out=den[:, b:b + 1]).then_inc(swa_exp, 1)

            def swa_out_of(i):
                if i % 2:
                    act.wait_ge(swa_pv, i + 1)
                    act.activation(T(os_hi, i // 2), bank[7][:, :], ACT.Copy).then_inc(xhi_ready, 1)

            for i in range(-1, SWA_H):
                n = z0 + 6 + i + 1
                w_hi_of(n + AHEAD, (n + AHEAD) % RING)
                if i + 1 < SWA_H:
                    swa_exp_of(i + 1)
                if i > 0:
                    swa_out_of(i - 1)
                if i >= 0:
                    act.wait_ge(swa_tr, 2 * (i + 1))
                    if i >= 2:
                        act.wait_ge(swa_pv, i - 1)
                    act.activation(swa_pt[i % 2][:, SEQ:], bank[6][:, :], ACT.Copy).then_inc(swa_ea, 1)
                if i in (4, 5):
                    act.wait_ge(gla_logit, i - 3)
                    act.activation(T(gla_b, i - 4), bank[4][:, :], ACT.Identity, bias=col("b_alpha", i - 4))\
                        .then_inc(gla_y, 1)
            w_hi_of(z0 + 15 + AHEAD, (z0 + 15 + AHEAD) % RING)
            swa_out_of(SWA_H - 1)
            act.wait_ge(gla_y, 2)
            act.activation(gla_e, gla_b, ACT.Abs).then_inc(a_chain, 1)
            act.wait_ge(a_chain, 1)
            act.activation(gla_e, gla_e, ACT.Exp, scale=-1.0).then_inc(a_chain, 1)
            act.wait_ge(a_chain, 2)
            act.activation(gla_e, gla_e, ACT.Ln, bias=1.0).then_inc(gla_l, 1)
            w_hi_of(z0 + 16 + AHEAD, (z0 + 16 + AHEAD) % RING)
            act.wait_ge(gla_cum, 2)
            act.activation(gla_e, gla_b, ACT.Exp, scale=1.0 / 16).then_inc(gla_exp, 1)
            w_hi_of(z0 + 17 + AHEAD, (z0 + 17 + AHEAD) % RING)
            act.wait_ge(gla_ops, 1)
            act.activation(gla_e, gla_b, ACT.Exp, scale=-1.0 / 16).then_inc(gla_exp, 1)
            act.wait_ge(gla_blast, 1)
            act.activation(decay[:, :], b_last[:, :], ACT.Exp, scale=1.0 / 16).then_inc(gla_exp, 1)
            act.wait_ge(gla_cum, 3)
            act.activation(gla_b, gla_b, ACT.Exp, scale=1.0 / 16).then_inc(gla_exp, 1)
            w_hi_of(z0 + 18 + AHEAD, (z0 + 18 + AHEAD) % RING)
            w_hi_of(z0 + 19 + AHEAD, (z0 + 19 + AHEAD) % RING)
            for t in range(4):
                act.activation(T(z_r, t), T(z_r, t), ACT.Silu).then_inc(silu_r, 1)
            act.wait_ge(gla_tr, 2)
            act.activation(T(gla_kdt, 1), bank[6][:, :], ACT.Copy).then_inc(gla_tr_read, 1)
            load_sqrt(len(STATS) + 1)
            for hd in range(GLA_H + 2):
                if hd < GLA_H:
                    act.wait_ge(gla_o, hd + 1)
                    act.activation(gla_sq_buf(hd), bank[hd][:, :], ACT.Square, scale=GLA_DV ** -0.5).then_inc(gla_sq, 1)
                if 0 < hd <= GLA_H:
                    c = RC_GLA + NB * (hd - 1)
                    act.wait_ge(gla_sums, hd)
                    act.activation(rms[:, c:c + NB], bank[3 + hd][:, 0:NB], ACT.Sqrt, bias=small[:, 60:61])\
                        .then_inc(gla_rms, 1)
                if hd >= 2:
                    act.wait_ge(o_done, hd - 1)
                    act.activation(T(og_hi, hd - 2), tmp[hd - 2][:, 0:SEQ], ACT.Copy).then_inc(xhi_ready, 1)
            for k in range(8):
                if k:
                    w_hi_of(UNIT0["wout"] + k + AHEAD, (UNIT0["wout"] + k + AHEAD) % RING)
                act.wait_ge(out_read, TILE0["wout"] + k + 1)
                x_hi(a_hi, k, T(h, k), col("ffn_norm", k))
                if k == 7:
                    load_sqrt(STAT_NO["ffn"])
                square("ffn", k, T(h, k))
            w_hi_of(UNIT0["upA"] + AHEAD, (UNIT0["upA"] + AHEAD) % RING)
            take_root("ffn", r_pre)
            act.dma_start(cst_b[:, :], consts2).then_inc(cst2_landed, 16)

            def up(name, split, first_pair, pairs):
                n0, x0 = UNIT0[name], SPLIT0[split]

                def product_hi(i, j):
                    act.wait_ge(prod, 2 * i + (first_pair + j + 1))
                    act.activation(at(g_hi, 2 * i + j), tmp[4 + j % 2][:, 0:SEQ], ACT.Copy).then_inc(xhi_ready, 1)

                def body(i):
                    for j in range(2):
                        pr = first_pair + j
                        begun = not isinstance(i, int) or i or j
                        if begun or name == "upB":
                            w_hi_loop(n0, i, 2 * j)
                        act.wait_ge(out_read, 4 * i + (TILE0[name] + 2 * j + 1))
                        if begun:
                            act.wait_ge(gated, 2 * i + pr)
                        act.activation(tmp[2][:, 0:SEQ], tmp[0][:, 2:2 + SEQ], ACT.Identity,
                                       scale=conv_col(i, first_pair + j, 0, 2), bias=conv_col(i, first_pair + j, 0, 3))\
                            .then_inc(tap_mid, 1)
                        if begun:
                            product_hi(i, j - 1)
                        w_hi_loop(n0, i, 2 * j + 1)
                        act.wait_ge(out_read, 4 * i + (TILE0[name] + 2 * j + 2))
                        act.activation(tmp[3][:, 0:SEQ], tmp[1][:, 2:2 + SEQ], ACT.Identity,
                                       scale=conv_col(i, first_pair + j, 1, 2), bias=conv_col(i, first_pair + j, 1, 3))\
                            .then_inc(tap_mid, 1)
                        act.wait_ge(taps_a, 2 * i + (pr + 1))
                        act.wait_ge(x_ready, 2 * i + (x0 + j - 1))
                        act.activation(tmp[4 + j][:, 0:SEQ], tmp[2][:, 0:SEQ], ACT.Silu).then_inc(gated, 1)
                body(0)
                looped(act, pairs // 2, body, 1)
                product_hi(pairs // 2 - 1, 1)

            def conv_col(i, j, half, tap):
                return col_at("conv", 16 * i + (8 * j + 4 * half + tap)) if not isinstance(i, int) else \
                    col("conv", 16 * i + 8 * j + 4 * half + tap)

            act.wait_ge(p_zero, 5)
            act.wait_ge(r_ready, R_NO["ffn"] + 1)
            up("upA", "prodA", 0, PAIRS_A)
            for n in range(UNIT0["downA"], UNIT0["upB"]):
                w_hi_of(n + AHEAD, (n + AHEAD) % RING)
            up("upB", "prodB", PAIRS_A, PAIRS_B)
            for k in range(KD):
                if k % 4 == 0:
                    first = UNIT0["downB"] + k // 4 * (PAIRS_B // 2)
                    for n in range(first, first + PAIRS_B // 2):
                        w_hi_of(n + AHEAD, (n + AHEAD) % RING)
                act.wait_ge(out_read, TILE0["downB"] + k + 1)
                x_hi(a_hi, k, T(h, k), col("pre", k))
                if k == 7:
                    load_sqrt(STAT_NO["pre0"])
                square("pre0", k, T(h, k))
            w_hi_of(UNIT0["pw1"] + AHEAD, (UNIT0["pw1"] + AHEAD) % RING)
            take_root("pre0", r_pre)

            def conv_operand(k):
                act.wait_ge(u_ready, k + 1)
                if k >= 4:
                    act.wait_ge(unit_used, conv_step(k // 2 - 1)[1].stop)
                src = u_pad[:, k * UW + CONV_W - 1:(k + 1) * UW]
                act.activation(u_hi[:, (k % 4) * UW + CONV_W - 1:(k % 4 + 1) * UW], src, ACT.Copy)\
                    .then_inc(uhi_ready, 1)
                act.activation(T(cv, k), src, ACT.Identity, scale=col("w_dw", k * CONV_W + CONV_W - 1),
                               bias=col("b_dw", k)).then_inc(last_tap, 1)
                for j in range(TAPS_POOL[k // 2]):
                    tap = CONV_W - 2 - j
                    no = pool_taps(k) + j
                    if no >= 2:
                        act.wait_ge(pool_tap, no - 1)
                    act.activation(sq_buf[no % 2], u_pad[:, k * UW + tap:k * UW + tap + SEQ], ACT.Copy,
                                   scale=col("w_dw", k * CONV_W + tap)).then_inc(tap_product, 1)

            for s in range(KD // 2 + 1):
                first, taps = conv_step(s)
                for n in first:
                    if n > UNIT0["pw1"]:
                        w_hi_of(n + AHEAD, (n + AHEAD) % RING)
                    q = n - first.start
                    k = 2 * s + q // 2
                    if q % 2:
                        act.wait_ge(out_read, TILE0["pw1"] + 2 * k + 2)
                        gate = tmp[2 * (k % 2) + 1][:, 0:SEQ]
                        act.activation(gate, gate, ACT.Sigmoid, bias=col("b_pw1", 8 + k)).then_inc(ug_sig, 1)
                    elif q:
                        conv_operand(k - 1)
                for n in taps:
                    w_hi_of(n + AHEAD, (n + AHEAD) % RING)
                    if n == taps.start and s < KD // 2:
                        conv_operand(2 * s + 1)
                if s == 0:
                    conv_operand(1)
            load_sqrt(STAT_NO["ln_var"])
            act.wait_ge(mean_done, 1)
            for k in range(KD):
                act.wait_ge(cen_ready, k + 1)
                act.activation(ln_sq_buf(k), T(cv, k), ACT.Square, scale=float(D) ** -0.5).then_inc(sq_ready, 1)
            w_hi_of(UNIT0["pw2"] + AHEAD, (UNIT0["pw2"] + AHEAD) % RING)
            take_root("ln_var", None, LN_EPS, 5)
            act.activation(small[:, 63:64], small[:, 60:61], ACT.Silu)
            for k in range(KD):
                act.wait_ge(ln_ready, k + 1)
                act.activation(T(a_hi, k), T(cv, k), ACT.Silu, bias=col("ln_b", k)).then_inc(xhi_ready, 1)
                act.activation(T(m, k), T(cv, k), ACT.Silu, bias=col("ln_b", k)).then_inc(ln_silu, 1)

            def after(product, stat, per_tile_units, done=0):
                for k in range(KD):
                    for u in range(done if k == 0 else 0, per_tile_units):
                        n = UNIT0[product] + per_tile_units * k + u + AHEAD
                        w_hi_of(n, n % RING)
                    act.wait_ge(out_read, TILE0[product] + k + 1)
                    if k == 7:
                        load_sqrt(STAT_NO[stat])
                    square(stat, k, T(m, k))
                take_root(stat, None)

            def next_operand(h0, gain, g0, stat, product):
                for k in range(KD):
                    act.wait_ge(h_ready, h0 + k + 1)
                    x_hi(a_hi, k, T(h, k), col(gain, g0 + k))
                    square(stat, k, T(h, k))
                w_hi_of(UNIT0[product] + AHEAD, (UNIT0[product] + AHEAD) % RING)
                take_root(stat, r_pre)

            after("pw2", "post0", 1, 1)
            next_operand(H0["post0"], "ffpre", 0, "ffpre0", "ff1a0")

            def feed_forward(layer):
                for half in range(2):
                    c = "ab"[half]
                    n0 = UNIT0[f"ff1{c}{layer}"]
                    t0 = TILE0[f"ff1{c}{layer}"]

                    def body(i):
                        for j in range(4):
                            if not isinstance(i, int) or j or half:
                                w_hi_loop(n0, i, j)
                            act.wait_ge(out_read, 4 * i + (t0 + j + 1))
                            act.activation(at(g_hi, 4 * i + j), tmp[j % 2][:, 0:SEQ], ACT.Square)\
                                .then_inc(xhi_ready, 1)
                    body(0)
                    looped(act, 4, body, 1)
                    if half == 0:
                        looped(act, 4, lambda i: [w_hi_loop(UNIT0[f"ff2a{layer}"], i, j) for j in range(4)])
                after(f"ff2b{layer}", f"ffpost{layer}", 2)

            feed_forward(0)
            for k in range(KD):
                act.wait_ge(h_ready, H0["ffpost0"] + k + 1)
                x_hi(a_hi, k, T(h, k), col("kv_in", k))
                square("pre1", k, T(h, k))
            w_hi_of(UNIT0["dkv"] + AHEAD, (UNIT0["dkv"] + AHEAD) % RING)
            for k in range(KD):
                x_hi(b_hi, k, T(h, k), col("pre", 8 + k))
            take_root("pre1", r_pre)
            for n in range(UNIT0["dkv"] + 1, UNIT0["dq"]):
                w_hi_of(n + AHEAD, (n + AHEAD) % RING)
            for k in range(2):
                act.wait_ge(out_read, TILE0["dkv"] + k + 1)
                square("ckv", k, T(c_kv, k), KV_RANK)
            act.wait_ge(unit_used, UNIT0["dq"])
            for k in range(2):
                x_hi(a_hi, k, T(c_kv, k), col("ckv_norm", k))
            for n in range(UNIT0["dq"], UNIT0["dq"] + 2):
                w_hi_of(n + AHEAD, (n + AHEAD) % RING)
            take_root("ckv", r_post)
            w_hi_of(UNIT0["dq"] + 2 + AHEAD, (UNIT0["dq"] + 2 + AHEAD) % RING)
            for k in range(3):
                act.wait_ge(out_read, TILE0["dq"] + k + 1)
                square("cq", k, T(c_q, k), Q_RANK)
                x_hi(a_hi, 2 + k, T(c_q, k), col("cq_norm", k))
            w_hi_of(UNIT0["uk"] + AHEAD, (UNIT0["uk"] + AHEAD) % RING)
            w_hi_of(UNIT0["uk"] + 1 + AHEAD, (UNIT0["uk"] + 1 + AHEAD) % RING)
            take_root("cq", r_pre)
            for n in range(UNIT0["uk"] + 2, UNIT0["uv"] + 1):
                w_hi_of(n + AHEAD, (n + AHEAD) % RING)
            for t in range(5):
                act.wait_ge(rope_done, t + 1)
                act.activation(kr_hi if t == 0 else T(qr_hi, t - 1), k_rope if t == 0 else T(q_rope, t - 1), ACT.Copy)\
                    .then_inc(rope_hi, 1)
            for u in range(2):
                n = UNIT0["uv"] + u
                act.wait_ge(unit_used, n + 1)
                for b in range(NB):
                    c = 4 * STAT_NO["ckv"] + b
                    act.activation(T(v_hi, b, MLA_H * V_DIM)[:, u * SEQ:(u + 1) * SEQ], bank[4 * u + b][:, :], ACT.Copy,
                                   scale=r_tok[:, c:c + 1]).then_inc(v_hi_ready, 1)
                w_hi_of(n + 1 + AHEAD, (n + 1 + AHEAD) % RING)

            def mla_exp_of(i):
                nm = small[:, 32:36] if i % 2 == 0 else small[:, 40:44]
                den = small[:, 36:40] if i % 2 == 0 else small[:, 44:48]
                act.wait_ge(mla_mx, 5 * (i + 1))
                if i:
                    act.wait_ge(mla_tr, 3 * i)
                for b in range(NB):
                    w = (b + 1) * P
                    o = P * b * (b + 1) // 2
                    act.activation(prob[:, o:o + w], bank[b][:, 0:w], ACT.Exp, scale=MLA_SCALE, bias=nm[:, b:b + 1],
                                   accum_out=den[:, b:b + 1]).then_inc(mla_exp, 1)

            mla_exp_of(0)
            for i in range(MLA_H):
                if i:
                    act.wait_ge(mla_pv, i)
                for q, (bk, c0, c1) in enumerate(mla_parts):
                    act.wait_ge(mla_tr, 3 * i + q + 1)
                    act.activation(pt_hi[:, c0:c1], bank[bk][:, 0:c1 - c0], ACT.Copy).then_inc(mla_ea, 1)
                if i + 1 < MLA_H:
                    mla_exp_of(i + 1)
                act.wait_ge(mla_pv, i + 1)
                act.activation(T(mo_hi, i), bank[4][:, :], ACT.Copy).then_inc(xhi_ready, 1)
            after("wo", "post1", 1, 1)
            next_operand(H0["post1"], "ffpre", 8, "ffpre1", "ff1a1")
            feed_forward(1)

        @block.tensor
        def _(pe):
            def three(out, w0, w1, x0, x1, start, stop, loose=False):
                pe.matmul(out, w0, x0, start=start, stop=False, skip_group_check=loose)
                pe.matmul(out, w0, x1, start=False, stop=False, skip_group_check=loose)
                return pe.matmul(out, w1, x0, start=False, stop=stop, skip_group_check=loose)

            def x_tile(hi, lo, k):
                return hi(k) if lo is None else (T(hi, k), T(lo, k))

            def bank_free(name, j):
                if name == "pw1" and j < 4:
                    pe.wait_ge(out_read, TILE0["downB"] + 5 + j)
                else:
                    pe.wait_ge(out_read, TILE0[name] + max(j - 3, 0))

            def k_ready(split, k):
                pe.wait_ge(x_ready, SPLIT0[split] + k + 1)

            def unit_ready(n, i=0):
                pe.wait_ge(wlo_ready, n + 1 + 4 * i if isinstance(i, int) else 4 * i + (n + 1))

            def tile_of_eight(n, slot, out, hi, lo, k0=0, start=True, stop=True, split=None):
                for k in range(8):
                    if split:
                        k_ready(split, k0 + k)
                    last = three(out, T(w_hi[slot], k, P), T(w_lo[slot], k, P), *x_tile(hi, lo, k0 + k),
                                 start and k == 0, stop and k == 7)
                last.then_inc(unit_used, 1)

            def token_sums(dst, sq, rhs=None, start=True, stop=True):
                rhs = cst[:, ONES:ONES + 1] if rhs is None else rhs
                w = rhs.shape[-1]
                for b in range(NB):
                    last = pe.matmul(dst[:, w * b:w * (b + 1)], T(sq, b, P), rhs, start=start, stop=stop)
                return last

            def stat(name):
                s, n = STAT_NO[name], STAT_TILES[name]
                if s == 0:
                    pe.wait_ge(cst_landed, 48)
                pe.wait_ge(sq_ready, SQ0[name] + n - 1)
                if n > 2:
                    pe.wait_ge(sum_added, ADD0[name] + n - 2)
                before = STATS[s - 1][0]
                if before in H0:
                    pe.wait_ge(h_ready, H0[before] + KD)
                elif before == "ln_var":
                    pe.wait_ge(ln_ready, KD)
                elif s:
                    pe.wait_ge(r_ready, R_NO[before] + 1)
                for b in range(NB):
                    pe.matmul(bank[4][:, b:b + 1], T(ssum, b, P), cst[:, ONES:ONES + 1], start=(b == 0), stop=False,
                              skip_group_check=True)
                pe.wait_ge(sq_ready, SQ0[name] + n)
                for b in range(NB):
                    last = pe.matmul(bank[4][:, b:b + 1], T(sq_buf[(n - 2) % 2], b, P), cst[:, ONES:ONES + 1],
                                     start=False, stop=(b == NB - 1), skip_group_check=True)
                last.then_inc(stat_done, 1)

            def spread(name):
                pe.wait_ge(r_tok_ready, STAT_NO[name] + 1)
                for b in range(NB):
                    last = pe.matmul(T(bank[4], b, P), r_cols(4 * STAT_NO[name] + b), cst[:, IDENT:IDENT + P],
                                     start=True, stop=True)
                last.then_inc(spread_done, 1)

            def three_tiles(name, hi, lo, split, stat_name=None):
                n0 = UNIT0[name]
                for k in range(8):
                    k_ready(split, k)
                    for j in range(3):
                        if k == 0:
                            unit_ready(n0 + j)
                            bank_free(name, j)
                        slot = (n0 + j) % RING
                        last = three(bank[j][:, :], T(w_hi[slot], k, P), T(w_lo[slot], k, P), *x_tile(hi, lo, k),
                                     k == 0, k == 7)
                        if k == 7:
                            last.then_inc(unit_used, 1)
                            if j == 0 and stat_name:
                                stat(stat_name)
                if stat_name and stat_name != "pre1":
                    spread(stat_name)

            def tiles(name, count, hi, lo, split=None, stat_name=None):
                n0 = UNIT0[name]
                if split:
                    three_tiles(name, hi, lo, split, stat_name)
                for j in range(3 if split else 0, count):
                    n = n0 + j
                    unit_ready(n)
                    bank_free(name, j)
                    tile_of_eight(n, n % RING, bank[j % 4][:, :], hi, lo)

            n0 = UNIT0["z"]
            three_tiles("z", a_hi, a_lo, "mix", "mix")

            def z_tile(j):
                unit_ready(n0 + j)
                if j < 6:
                    bk = j % 4
                    if j >= 4:
                        pe.wait_ge(out_read, j - 3)
                else:
                    bk = j % 2
                    pe.wait_ge(out_read, j - 1)
                tile_of_eight(n0 + j, (n0 + j) % RING, bank[bk][:, :], a_hi, a_lo)

            for j in range(3, 5):
                z_tile(j)
            halves = cst[:, HALVES:HALVES + 2]
            pe.wait_ge(r_ready, 1)
            for t in range(5):
                pe.wait_ge(swa_sq, t + 1)
                token_sums(bank[4][:, 8 * t:8 * t + 8], swa_sq_buf(t), halves).then_inc(swa_sums, 1)
            z_tile(5)
            pe.wait_ge(swa_r, 1)
            for b in range(NB):
                for e in range(2):
                    last = pe.matmul(T(bank[5], b, P)[64 * e:64 * e + 64, :], r_cols(RC_SWA + 32 + 2 * b + e, 64),
                                     cst[:, IDENT:IDENT + P], start=True, stop=True)
            last.then_inc(sk_spread, 1)
            pe.wait_ge(out_read, 6)
            for b in range(NB):
                last = pe.transpose(T(bank[6], b, P), z_lr[:, b * P:(b + 1) * P], cst[:, IDENT:IDENT + P])
            last.then_inc(sv_turned, 1)
            def swa_scores(i):
                hd = swa_head(i)
                r = slice(64 * (hd // 4), 64 * (hd // 4) + 64)
                t = hd % 4
                if i == 0:
                    pe.wait_ge(k_normed, 1)
                    pe.wait_ge(p_zero, 1)
                else:
                    pe.wait_ge(swa_bias, NB * i)
                for b in range(NB):
                    pe.matmul(bank[2 + b // 2][:, 256 * (b % 2):256 * (b % 2) + 256], T(z_sq, t)[r, b * P:(b + 1) * P],
                              z_sk[r, b * P:b * P + 256], start=True, stop=True).then_inc(swa_sc, 1)

            def swa_transpose(i):
                p = swa_p[i % 2]
                pe.wait_ge(swa_pn, NB * (i + 1))
                if i == 0:
                    pe.wait_ge(sv_copied, 1)
                if i:
                    pe.wait_ge(swa_ev, i)
                    pe.wait_ge(swa_ea, i)
                for b in range(NB):
                    for e in range(2):
                        if b == 0 and e == 0:
                            continue
                        last = pe.transpose(bank[5 + b // 2][:, (2 * (b % 2) + e) * P:(2 * (b % 2) + e + 1) * P],
                                            p[:, b * 256 + e * P:b * 256 + (e + 1) * P], cst[:, IDENT:IDENT + P])
                    if b % 2:
                        last.then_inc(swa_tr, 1)

            def swa_values(i):
                t, g = swa_pt[i % 2], i % 2
                pe.wait_ge(swa_ev, i + 1)
                pe.wait_ge(swa_ea, i + 1)
                if g == 0 and i:
                    pe.wait_ge(x_ready, SPLIT0["attn"] + i // 2)
                for b in range(NB):
                    es = [e for e in range(2) if b + e > 0]
                    for e in es:
                        last = pe.matmul(bank[7][64 * g:64 * g + 64, b * P:(b + 1) * P],
                                         z_vs[:, (b - 1 + e) * P + 64 * g:(b - 1 + e) * P + 64 * g + 64],
                                         t[:, (2 * b + e) * P:(2 * b + e + 1) * P], start=(e == es[0]), stop=(e == 1))
                last.then_inc(swa_pv, 1)

            for i in range(-1, SWA_H):
                if i + 1 < SWA_H:
                    swa_scores(i + 1)
                if i in (4, 5):
                    pe.wait_ge(out_read, 11)
                    if i == 5:
                        pe.wait_ge(gla_y, 1)
                    pe.matmul(bank[4][:, :], T(w_al, i - 4, P), z_lr[:, :], start=True, stop=True)\
                        .then_inc(gla_logit, 1)
                z_tile(6 + i + 1)
                if i > 0:
                    swa_values(i - 1)
                if i >= 0:
                    swa_transpose(i)
            for u in range(4):
                n = n0 + 15 + u
                unit_ready(n)
                for kk in range(2):
                    k = 2 * u + kk
                    for b in range(NB):
                        if k == 0:
                            pe.wait_ge(out_read, 15)
                            pe.wait_ge(swa_bias, NB * SWA_H)
                        xh, xl = T(a_hi, k)[:, b * P:(b + 1) * P], T(a_lo, k)[:, b * P:(b + 1) * P]
                        last = three(bank[b][:, :], xh, xl, T(w_hi[n % RING], kk), T(w_lo[n % RING], kk),
                                     k == 0, k == KD - 1)
                last.then_inc(unit_used, 1)
                if u == 0:
                    swa_values(SWA_H - 1)
            pe.wait_ge(out_read, TILE0["wout"])
            pe.wait_ge(gla_ops, 3)
            for hd in range(GLA_H):
                r = slice(64 * (hd % 2), 64 * (hd % 2) + 64)
                for b in range(NB):
                    last = pe.matmul(T(bank[hd], b, P), T(gla_e, hd // 2)[r, b * P:(b + 1) * P],
                                     T(z_q, hd // 2)[r, b * P:(b + 1) * P], start=True, stop=True)
                last.then_inc(gla_scores, 1)
            for t in range(2):
                for b in range(NB):
                    last = pe.transpose(T(bank[5 + t], b, P), T(gla_b, t)[:, b * P:(b + 1) * P],
                                        cst[:, IDENT:IDENT + P])
                last.then_inc(gla_tr, 1)
            pe.wait_ge(gla_tr_read, 2)
            for t in range(2):
                for par in range(2):
                    for q in range(NB):
                        for e in range(2):
                            hd = 2 * t + e
                            last = pe.matmul(T(bank[4 + 2 * t + par], q, P)[64 * e:64 * e + 64, :],
                                             T(gla_kdt, t)[64 * par:64 * par + 64, q * P + 64 * e:q * P + 64 * e + 64],
                                             T(z_v, q)[64 * par:64 * par + 64, hd * P:(hd + 1) * P],
                                             start=True, stop=True, skip_group_check=True)
                    last.then_inc(gla_cs, 1)
            for hd in range(GLA_H):
                pe.wait_ge(gla_masked, hd + 1)
                for b in range(NB):
                    pe.matmul(T(bank[hd], b, P), T(z_v, b)[:, hd * P:(hd + 1) * P],
                              T(gla_a, hd)[:, b * P:(b + 1) * P], start=(b == 0), stop=False, skip_group_check=True)

            def gla_mean_square(hd):
                pe.wait_ge(gla_sq, hd + 1)
                token_sums(bank[4 + hd], gla_sq_buf(hd)).then_inc(gla_sums, 1)

            def gla_factors(hd):
                pe.wait_ge(gla_r, hd + 1)
                for b in range(NB):
                    last = pe.matmul(T(bank[4 + hd], b, P), r_cols(RC_GLA + NB * hd + b), cst[:, IDENT:IDENT + P],
                                     start=True, stop=True)
                last.then_inc(gla_spread, 1)

            pe.wait_ge(gla_state, 2 * (NCH - 1))
            for hd in range(GLA_H):
                r = slice(64 * (hd % 2), 64 * (hd % 2) + 64)
                for c in range(1, NCH):
                    s = gla_s[r, ((hd // 2) * NCH + c) * GLA_DV:((hd // 2) * NCH + c + 1) * GLA_DV]
                    last = pe.matmul(bank[hd][:, c * CHUNK:(c + 1) * CHUNK], s,
                                     T(z_q, hd // 2)[r, c * CHUNK:(c + 1) * CHUNK], start=False, stop=(c == NCH - 1),
                                     skip_group_check=True)
                last.then_inc(gla_o, 1)
                if hd:
                    gla_mean_square(hd - 1)
                if hd >= 2:
                    gla_factors(hd - 2)
            gla_mean_square(GLA_H - 1)
            gla_factors(GLA_H - 2)
            gla_factors(GLA_H - 1)
            pe.wait_ge(o_done, GLA_H - 1)
            tiles("wout", 8, o_tiles, None, "attn")

            def up(name, split, pairs):
                n0 = UNIT0[name]

                def body(i):
                    for j in range(4):
                        unit_ready(n0 + j, i)
                        pe.wait_ge(out_read, 4 * i + (TILE0[name] + j - 3))
                        tile_of_eight(n0 + j, (n0 + j) % RING, bank[j % 4][:, :], a_hi, a_lo)
                if split:
                    three_tiles(name, a_hi, a_lo, split, split)
                    unit_ready(n0 + 3)
                    bank_free(name, 3)
                    tile_of_eight(n0 + 3, (n0 + 3) % RING, bank[3][:, :], a_hi, a_lo)

                    def rest(i):
                        for j in range(4):
                            unit_ready(n0 + 4 + j, i)
                            pe.wait_ge(out_read, 4 * i + (TILE0[name] + j + 1))
                            tile_of_eight(n0 + j, (n0 + j) % RING, bank[j % 4][:, :], a_hi, a_lo)
                    looped(pe, pairs // 2 - 1, rest)
                else:
                    looped(pe, pairs // 2, body)

            def down(name, split, kts):
                n = UNIT0[name]
                for g in range(2):
                    for u in range(kts // 2):
                        unit_ready(n)
                        for kk in range(2):
                            k = 2 * u + kk
                            k_ready(split, k)
                            for j in range(4):
                                if g == 1 and k == 0:
                                    pe.wait_ge(out_read, TILE0[name])
                                w = slice((4 * kk + j) * P, (4 * kk + j + 1) * P)
                                last = three(bank[4 * (1 - g) + j][:, :], w_hi[n % RING][:, w], w_lo[n % RING][:, w],
                                             T(g_hi, k), T(g_lo, k), k == 0, k == kts - 1)
                        last.then_inc(unit_used, 1)
                        n += 1

            up("upA", "ffn", PAIRS_A)
            down("downA", "prodA", PAIRS_A)
            up("upB", None, PAIRS_B)
            down("downB", "prodB", PAIRS_B)
            for s in range(KD // 2 + 1):
                first, taps = conv_step(s)
                if s == 0:
                    three_tiles("pw1", a_hi, a_lo, "pre0", "pre0")
                for n in first:
                    q = n - first.start
                    if s or q == 3:
                        unit_ready(n)
                        bank_free("pw1", 4 * s + q)
                        tile_of_eight(n, n % RING, bank[q][:, :], a_hi, a_lo)
                for n in taps:
                    unit_ready(n)
                    for i in range(8):
                        e, tap = divmod(8 * (n - taps.start) + i, TAPS_PE[s - 1])
                        c = 2 * (s - 1) + e
                        if tap == 0:
                            pe.wait_ge(ulo_ready, c + 1)
                            if c >= 4:
                                pe.wait_ge(cv_ready, c - 3)
                        o = (c % 4) * UW + tap
                        last = three(conv_bank(c)[:, :], T(w_hi[n % RING], i, P), T(w_lo[n % RING], i, P),
                                     u_hi[:, o:o + SEQ], u_lo[:, o:o + SEQ], tap == 0, tap == TAPS_PE[s - 1] - 1)
                    last.then_inc(unit_used, 1)
            pe.wait_ge(mean_add, KD - 2)
            pe.matmul(bank[4][:, :], cst[:, MEAN:MEAN + P], ssum[:, :], start=True, stop=False)
            pe.wait_ge(cv_ready, KD)
            pe.matmul(bank[4][:, :], cst[:, MEAN:MEAN + P], T(cv, KD - 2), start=False, stop=False)
            pe.matmul(bank[4][:, :], cst[:, MEAN:MEAN + P], T(cv, KD - 1), start=False, stop=True)\
                .then_inc(mean_done, 1)
            for p in range(KD // 2):
                pe.wait_ge(sum_added, ADD0["ln_var"] + p + 1)
                for b in range(NB):
                    last = pe.matmul(bank[5][:, b:b + 1], T(ln_sq_buf(2 * p), b, P), cst[:, ONES:ONES + 1],
                                     start=(p == 0 and b == 0), stop=(p == KD // 2 - 1 and b == NB - 1),
                                     skip_group_check=True)
            last.then_inc(stat_done, 1)
            spread("ln_var")
            tiles("pw2", 8, a_hi, a_lo, "conv")
            stat("post0")
            spread("post0")

            def feed_forward(layer):
                up(f"ff1a{layer}", f"ffpre{layer}", 8)
                for half in range(2):
                    c = "ab"[half]
                    if half:
                        pe.wait_ge(out_read, TILE0[f"ff1b{layer}"])
                        up(f"ff1b{layer}", None, 8)
                    name = f"ff2{c}{layer}"
                    n0, t0 = UNIT0[name], TILE0[name]

                    def body(i):
                        for j in range(2):
                            pe.wait_ge(out_read, 2 * i + (t0 + j - 1))
                            if isinstance(i, int) and j == 0:
                                pe.wait_ge(out_read, t0)
                            for u in range(2):
                                n = n0 + 2 * j + u
                                unit_ready(n, i)
                                tile_of_eight(n, n % RING, bank[j][:, :], g_hi, g_lo, 8 * u, u == 0, u == 1,
                                              f"hid{layer}{c}" if isinstance(i, int) and j == 0 else None)
                    body(0)
                    looped(pe, 4, body, 1)
                stat(f"ffpost{layer}")
                spread(f"ffpost{layer}")

            feed_forward(0)
            tiles("dkv", 3, a_hi, a_lo, "kvpre", "pre1")
            for j in range(3):
                n = UNIT0["dq"] + j
                unit_ready(n)
                pe.wait_ge(out_read, TILE0["dkv"] + j)
                tile_of_eight(n, n % RING, bank[DQ_BANK[j]][:, :], b_hi, b_lo, split="pre1" if j == 0 else None)
                if j == 0:
                    spread("pre1")
                if j == 1:
                    stat("ckv")
            spread("ckv")
            swap = cst[:, SWAP:SWAP + P]
            pe.wait_ge(out_read, TILE0["dkv"] + 3)
            pe.matmul(bank[5][:, :], swap, k_rope, start=True, stop=True).then_inc(rope_sw, 1)
            for u in range(2):
                n = UNIT0["uk"] + u
                unit_ready(n)
                for j in range(4):
                    bank_free("uk", 4 * u + j)
                    for k in range(2):
                        if u == 0 and j == 0:
                            k_ready("ckv", k)
                        w = slice((4 * k + j) * P, (4 * k + j + 1) * P)
                        last = three(bank[j][:, :], w_hi[n % RING][:, w], w_lo[n % RING][:, w], T(a_hi, k), T(a_lo, k),
                                     k == 0, k == 1)
                last.then_inc(unit_used, 1)
                if u == 0:
                    stat("cq")
                else:
                    spread("cq")
            for u in range(6):
                n = UNIT0["uq"] + u
                unit_ready(n)
                for e in range(2):
                    j = 2 * u + e
                    bank_free("uq", j)
                    for k in range(3):
                        if j == 0:
                            k_ready("cq", k)
                        w = slice(k * 256 + e * P, k * 256 + (e + 1) * P)
                        last = three(bank[j % 4][:, :], w_hi[n % RING][:, w], w_lo[n % RING][:, w],
                                     T(a_hi, 2 + k), T(a_lo, 2 + k), k == 0, k == 2)
                last.then_inc(unit_used, 1)
            for t in range(4):
                pe.wait_ge(out_read, TILE0["uq"] + 8 + t + 1)
                if t == 3:
                    pe.wait_ge(r_ready, R_NO["cq"] + 1)
                pe.matmul(rope_bank(t + 1)[:, :], swap, T(q_rope, t), start=True, stop=True).then_inc(rope_sw, 1)
            for u in range(2):
                n = UNIT0["uv"] + u
                unit_ready(n)
                if u:
                    pe.wait_ge(rope_t, 10)
                for b in range(NB):
                    if u == 0:
                        bank_free("uv", b)
                    for k in range(2):
                        last = three(bank[4 * u + b][:, :], T(a_hi, k)[:, b * P:(b + 1) * P],
                                     T(a_lo, k)[:, b * P:(b + 1) * P], T(w_hi[n % RING], k), T(w_lo[n % RING], k),
                                     k == 0, k == 1)
                last.then_inc(unit_used, 1)
            pe.wait_ge(rope_split, 5)
            pe.wait_ge(out_read, TILE0["uv"] + 4)
            pe.wait_ge(cst2_landed, 16)

            def mla_scores(i):
                r = slice(64 * (i % 2), 64 * (i % 2) + 64)
                for b in range(NB):
                    w = (b + 1) * P
                    if i:
                        pe.wait_ge(mla_exp, NB * (i - 1) + b + 1)
                    pe.matmul(bank[b][:, 0:w], T(q_nope, i)[:, b * P:(b + 1) * P], T(k_nope, i)[:, 0:w],
                              start=True, stop=False)
                    pe.matmul(bank[b][:, w - P:w], cst_b[0:1, MASK_Q:MASK_Q + P], cst_b[0:1, MASK_K:MASK_K + P],
                              start=False, stop=False)
                    three(bank[b][:, 0:w], T(qr_hi, i // 2)[r, b * P:(b + 1) * P],
                          T(qr_lo, i // 2)[r, b * P:(b + 1) * P], kr_hi[r, 0:w], kr_lo[r, 0:w], False, True)\
                        .then_inc(mla_sc, 1)

            mla_scores(0)
            for i in range(MLA_H):
                if i + 1 < MLA_H:
                    mla_scores(i + 1)
                pe.wait_ge(mla_pn, NB * (i + 1))
                if i:
                    pe.wait_ge(mla_ev, 3 * i)
                else:
                    pe.wait_ge(out_read, TILE0["wo"])
                for kt in (0, 1, 3, 2):
                    bk, c0, _ = mla_cols[kt]
                    for b in range(kt, NB):
                        o = P * b * (b + 1) // 2 + kt * P
                        c = c0 + (b - kt) * P
                        last = pe.transpose(bank[bk][:, c:c + P], prob[:, o:o + P], cst[:, IDENT:IDENT + P])
                    if kt != 1:
                        last.then_inc(mla_tr, 1)
                pe.wait_ge(x_ready, SPLIT0["mla"] + i)
                for kt in (0, 1, 3, 2):
                    pe.wait_ge(mla_ev, 3 * i + mla_cols[kt][0] - 4)
                    c = mla_cols[kt][2]
                    w = slice(i * P, (i + 1) * P)
                    last = three(bank[4][:, kt * P:], T(v_hi, kt, MLA_H * V_DIM)[:, w], v_lo(kt)[:, w],
                                 pt_hi[:, c:c + SEQ - kt * P], pt_lo[:, c:c + SEQ - kt * P], kt == 0, kt == 2, True)
                last.then_inc(mla_pv, 1)
            tiles("wo", 8, mo_hi, mo_lo, "mla")
            stat("post1")
            spread("post1")
            feed_forward(1)

        @block.vector
        def _(dve):
            def lo(n, slot, i=None):
                if i is None:
                    if n >= N_UNITS:
                        return
                    dve.wait_ge(whi_ready, n + 1)
                else:
                    dve.wait_ge(whi_ready, 4 * i + (n + 1))
                dve.tensor_tensor(w_lo[slot][:, :], w_raw[slot][:, :], f(w_hi[slot][:, :]), ALU.subtract)\
                    .then_inc(wlo_ready, 1)

            def lo_ahead(n, i=None):
                n += AHEAD
                if isinstance(i, int):
                    n, i = n + 4 * i, None
                lo(n, n % RING, i)

            def unit_done(n, i=None):
                dve.wait_ge(unit_used, n + 1 if i is None else 4 * i + (n + 1))

            def x_lo(no, dst_lo, dst_hi, k, src, gain=None):
                dve.wait_ge(xhi_ready, no + 1)
                if gain is None:
                    ins = dve.tensor_tensor(T(dst_lo, k), src, f(T(dst_hi, k)), ALU.subtract)
                else:
                    ins = dve.scalar_tensor_tensor(T(dst_lo, k), src, gain, f(T(dst_hi, k)), ALU.mult, ALU.subtract)
                ins.then_inc(x_ready, 1)

            def take_r(name):
                c = 4 * STAT_NO[name]
                dve.wait_ge(rms_ready, STAT_NO[name] + 1)
                dve.reciprocal(r_tok[:, c:c + NB], rms[:, c:c + NB]).then_inc(r_tok_ready, 1)

            def scaled(name):
                dve.wait_ge(r_ready, R_NO[name] + 1)

            links = [0]

            def link(ins):
                links[0] += 1
                ins.then_inc(v_chain, 1)
                dve.wait_ge(v_chain, links[0])

            link(dve.memset(small[:, 60:61], EPS))
            link(dve.memset(small[:, 61:62], LN_EPS))
            dve.wait_ge(vec_landed, 16)
            for k in range(KD):
                x_lo(SPLIT0["mix"] + k, a_lo, a_hi, k, T(h, k), col("mix_norm", k))
                if k in (0, 2, 4):
                    lo(k // 2, k // 2)
            lo_ahead(0)
            take_r("mix")
            scaled("mix")
            for j in range(5):
                if j:
                    lo_ahead(j)
                unit_done(j)
                dst = T(z_sq, j) if j < 4 else z_sk[:, P:]
                dve.tensor_tensor(dst, bank[j % 4][:, :], r_pre[:, :], ALU.mult).then_inc(out_read, 1)
            lo_ahead(5)
            link(dve.tensor_tensor(small[:, 62:63], col("q_norm"), col("k_norm"), ALU.mult))
            dve.wait_ge(swa_rms, 1)
            dve.reciprocal(r_tok[:, RC_SWA:RC_SWA + 40], rms[:, RC_SWA:RC_SWA + 40]).then_inc(swa_r, 1)
            unit_done(5)
            dve.tensor_tensor(z_lr[:, :], bank[1][:, :], r_pre[:, :], ALU.mult).then_inc(out_read, 1)
            dve.wait_ge(sk_spread, 1)
            dve.wait_ge(out_read, 5)
            dve.scalar_tensor_tensor(z_sk[:, P:], z_sk[:, P:], small[:, 62:63], bank[5][:, :], ALU.mult, ALU.mult)\
                .then_inc(k_normed, 1)

            def swa_softmax_in(i):
                p, t, e = swa_p[i % 2], swa_head(i) % 4, swa_head(i) // 4
                nm = small[:, 32:36] if i % 2 == 0 else small[:, 40:44]
                dve.wait_ge(swa_dist, i + 1)
                if i == 0:
                    dve.wait_ge(swa_r, 1)
                for b in range(NB):
                    dve.wait_ge(swa_sc, NB * i + b // 2 * 2 + 2)
                    c = RC_SWA + 8 * t + 2 * b + e
                    d0 = 0 if b == 0 else 256
                    dve.scalar_tensor_tensor(T(p, b, 256), bank[2 + b // 2][:, 256 * (b % 2):256 * (b % 2) + 256],
                                             r_tok[:, c:c + 1], swa_bias_t(i)[:, d0:d0 + 256], ALU.mult, ALU.add)\
                        .then_inc(swa_bias, 1)
                dve.wait_ge(swa_bias, NB * (i + 1))
                link(dve.tensor_reduce(nm, p[:, :].rearrange("p (b k) -> p b k", b=NB), AX_X, ALU.max))
                dve.tensor_scalar(nm, nm, SWA_HD ** -0.5, col("sinks", swa_head(i)), ALU.mult, ALU.max)\
                    .then_inc(swa_mx, 1)
                dve.wait_ge(swa_mx, 2 * i + 1)
                dve.tensor_scalar(nm, nm, -1.0, None, ALU.mult).then_inc(swa_mx, 1)

            def swa_normalise(i):
                p = swa_p[i % 2]
                den = small[:, 36:40] if i % 2 == 0 else small[:, 44:48]
                se = small[:, 48:52] if i % 2 == 0 else small[:, 52:56]
                dve.wait_ge(swa_se, i + 1)
                dve.wait_ge(swa_exp, NB * (i + 1))
                link(dve.tensor_tensor(den, den, se, ALU.add))
                link(dve.reciprocal(den, den))
                for b in range(NB):
                    dve.tensor_scalar(T(p, b, 256), T(p, b, 256), den[:, b:b + 1], None, ALU.mult).then_inc(swa_pn, 1)

            def swa_out_lo(i):
                if i % 2:
                    x_lo(SPLIT0["attn"] + i // 2, os_lo, os_hi, i // 2, bank[7][:, :])

            dests = [T(z_q, 0), T(z_q, 1), T(z_k, 0), T(z_k, 1), z_lr[:, :]] + [T(z_r, t) for t in range(4)]
            for i in range(-1, SWA_H):
                n = 6 + i + 1
                lo_ahead(n)
                if i + 1 < SWA_H:
                    if i >= 1:
                        dve.wait_ge(swa_tr, 2 * i)
                    swa_softmax_in(i + 1)
                if i >= 0:
                    swa_normalise(i)
                unit_done(n)
                dve.tensor_tensor(dests[i + 1], bank[n % 2][:, :], r_pre[:, :], ALU.mult).then_inc(out_read, 1)
                if i > 0:
                    swa_out_lo(i - 1)
                if i >= 0:
                    dve.wait_ge(swa_tr, 2 * i + 1)
                    if i >= 2:
                        dve.wait_ge(swa_pv, i - 1)
                    dve.tensor_copy(swa_pt[i % 2][:, P:SEQ], bank[5][:, P:SEQ]).then_inc(swa_ev, 1)
            lo_ahead(15)
            swa_out_lo(SWA_H - 1)
            dve.wait_ge(gla_l, 1)
            dve.scalar_tensor_tensor(gla_b, gla_b, 0.0, gla_e, ALU.min, ALU.subtract).then_inc(gla_ls, 1)
            dve.wait_ge(gla_ls, 1)
            for t in range(2):
                dve.tensor_tensor_scan(T(gla_b, t), cst_b[:, RESET:RESET + SEQ], T(gla_b, t), 0.0, ALU.mult, ALU.add)\
                    .then_inc(gla_cum, 1)
            dve.wait_ge(gla_cum, 2)
            chunks = gla_b.rearrange("p (n c) -> p n c", c=CHUNK)
            dve.tensor_copy(b_last[:, :], chunks[:, :, CHUNK - 1]).then_inc(gla_blast, 1)
            lo_ahead(16)
            dve.wait_ge(gla_exp, 1)
            dve.scalar_tensor_tensor(z_q[:, :], z_q[:, :], GLA_DK ** -0.5, gla_e, ALU.mult, ALU.mult)\
                .then_inc(gla_ops, 1)
            lo_ahead(17)
            dve.wait_ge(gla_exp, 2)
            dve.wait_ge(gla_blast, 1)
            last = b_last[:, :].rearrange("p (n o) -> p n o", o=1)
            dve.tensor_tensor(chunks, last.broadcast_to([P, 2 * NCH, CHUNK]), chunks, ALU.subtract)\
                .then_inc(gla_cum, 1)
            dve.tensor_tensor(gla_e, gla_e, z_k[:, :], ALU.mult).then_inc(gla_ops, 1)
            dve.wait_ge(gla_exp, 4)
            dve.tensor_tensor(gla_b, gla_b, z_k[:, :], ALU.mult).then_inc(gla_ops, 1)
            lo_ahead(18)
            unit_done(18)
            for b in range(NB):
                dve.tensor_scalar(T(z_v, b), bank[b][:, :], r_tok[:, b:b + 1], None, ALU.mult).then_inc(out_read, 1)
            lo_ahead(UNIT0["wout"])
            dve.wait_ge(p_zero, 3)
            for hd in range(GLA_H):
                dve.wait_ge(gla_scores, hd + 1)
                dve.copy_predicated(T(gla_a, hd), cst_b[:, CAUSAL:CAUSAL + SEQ].bitcast(I32), bank[hd][:, :])\
                    .then_inc(gla_masked, 1)
            dve.wait_ge(gla_tr, 1)
            dve.tensor_copy(T(gla_kdt, 0), bank[5][:, :]).then_inc(gla_tr_read, 1)
            dve.wait_ge(gla_cs, 4)
            for c in range(NCH - 1):
                for t in range(2):
                    cs = T(bank[4 + 2 * t + c % 2], c // 2, P)
                    s_new = gla_s[:, (t * NCH + c + 1) * GLA_DV:(t * NCH + c + 2) * GLA_DV]
                    if c == 0:
                        dve.tensor_copy(s_new, cs).then_inc(gla_state, 1)
                    else:
                        s_old = gla_s[:, (t * NCH + c) * GLA_DV:(t * NCH + c + 1) * GLA_DV]
                        dve.wait_ge(gla_state, 2 * (c - 1) + t + 1)
                        dve.scalar_tensor_tensor(s_new, s_old, decay[:, t * NCH + c:t * NCH + c + 1], cs,
                                                 ALU.mult, ALU.add).then_inc(gla_state, 1)
            def gla_factor(hd):
                c = RC_GLA + NB * hd
                dve.wait_ge(gla_rms, hd + 1)
                dve.reciprocal(r_tok[:, c:c + NB], rms[:, c:c + NB]).then_inc(gla_r, 1)

            gla_factor(0)
            for hd in range(GLA_H):
                if hd + 1 < GLA_H:
                    gla_factor(hd + 1)
                dve.wait_ge(gla_spread, hd + 1)
                dve.wait_ge(silu_r, hd + 1)
                dve.tensor_tensor(T(z_r, hd), T(z_r, hd), bank[4 + hd][:, :], ALU.mult).then_inc(gla_gated, 1)
                dve.wait_ge(gla_gated, hd + 1)
                dve.scalar_tensor_tensor(tmp[hd][:, 0:SEQ], bank[hd][:, :], col("gla_norm"), T(z_r, hd),
                                         ALU.mult, ALU.mult).then_inc(o_done, 1)
                if hd:
                    x_lo(SPLIT0["attn"] + 3 + hd, og_lo, og_hi, hd - 1, tmp[hd - 1][:, 0:SEQ])
            x_lo(SPLIT0["attn"] + 7, og_lo, og_hi, 3, tmp[3][:, 0:SEQ])

            for k in range(8):
                n = UNIT0["wout"] + k
                if k:
                    lo_ahead(n)
                unit_done(n)
                dve.tensor_tensor(T(h, k), T(h, k), bank[k % 4][:, :], ALU.add).then_inc(out_read, 1)
                x_lo(SPLIT0["ffn"] + k, a_lo, a_hi, k, T(h, k), col("ffn_norm", k))
            lo_ahead(UNIT0["upA"])
            take_r("ffn")

            def conv_col(i, j, half, tap):
                return col_at("conv", 16 * i + (8 * j + 4 * half + tap)) if not isinstance(i, int) else \
                    col("conv", 16 * i + 8 * j + 4 * half + tap)

            def up(name, split, first_pair, pairs):
                n0, x0 = UNIT0[name], SPLIT0[split]

                def product_lo(i, j):
                    dve.wait_ge(xhi_ready, 2 * i + (x0 + j + 1))
                    dve.tensor_tensor(at(g_lo, 2 * i + j), tmp[4 + j % 2][:, 0:SEQ], f(at(g_hi, 2 * i + j)),
                                      ALU.subtract).then_inc(x_ready, 1)

                def body(i):
                    for j in range(2):
                        pr = first_pair + j
                        begun = not isinstance(i, int) or i or j
                        for half in range(2):
                            if begun or half or name == "upB":
                                lo_ahead(n0 + 2 * j + half, i)
                            unit_done(n0 + 2 * j + half, i)
                            if begun:
                                dve.wait_ge(taps_a if half == 0 else taps_b, 2 * i + pr)
                            dve.tensor_tensor(tmp[half][:, 2:2 + SEQ], bank[2 * j + half][:, :], r_pre[:, :],
                                              ALU.mult).then_inc(out_read, 1)
                        for half in range(2):
                            dve.wait_ge(tap_mid, 4 * i + (2 * pr + half + 1))
                            dve.scalar_tensor_tensor(tmp[2 + half][:, 0:SEQ], tmp[half][:, 1:1 + SEQ],
                                                     conv_col(i, first_pair + j, half, 1), tmp[2 + half][:, 0:SEQ],
                                                     ALU.mult, ALU.add).then_inc(tap_one, 1)
                        for half in range(2):
                            dve.wait_ge(tap_one, 4 * i + (2 * pr + half + 1))
                            dve.scalar_tensor_tensor(tmp[2 + half][:, 0:SEQ], tmp[half][:, 0:SEQ],
                                                     conv_col(i, first_pair + j, half, 0), tmp[2 + half][:, 0:SEQ],
                                                     ALU.mult, ALU.add).then_inc(taps_a if half == 0 else taps_b, 1)
                        if begun:
                            product_lo(i, j - 1)
                body(0)
                looped(dve, pairs // 2, body, 1)
                product_lo(pairs // 2 - 1, 1)

            def down(name, units, final):
                n0, t0 = UNIT0[name], TILE0[name]
                for n in range(n0, n0 + units // 2):
                    lo_ahead(n)
                for g in range(2):
                    if g == 1:
                        for n in range(n0 + units // 2, n0 + units):
                            lo_ahead(n)
                    unit_done(n0 + (g + 1) * units // 2 - 1)
                    for j in range(4):
                        k = 4 * g + j
                        dve.tensor_tensor(T(h, k), T(h, k), bank[4 * (1 - g) + j][:, :], ALU.add)\
                            .then_inc(out_read, 1)
                        if final:
                            x_lo(SPLIT0["pre0"] + k, a_lo, a_hi, k, T(h, k), col("pre", k))

            scaled("ffn")
            dve.wait_ge(p_zero, 5)
            up("upA", "prodA", 0, PAIRS_A)
            down("downA", PAIRS_A, False)
            up("upB", "prodB", PAIRS_A, PAIRS_B)
            down("downB", PAIRS_B, True)
            lo_ahead(UNIT0["pw1"])
            take_r("pre0")
            scaled("pre0")
            dve.wait_ge(p_zero, 5 + KD + 8)

            def glu(k):
                dve.wait_ge(ug_sig, k + 1)
                b = 2 * (k % 2)
                dve.scalar_tensor_tensor(u_pad[:, k * UW + CONV_W - 1:(k + 1) * UW], tmp[b][:, 0:SEQ],
                                         col("b_pw1", k), tmp[b + 1][:, 0:SEQ], ALU.add, ALU.mult).then_inc(u_ready, 1)

            def operand_lo(k):
                dve.wait_ge(uhi_ready, k + 1)
                o = (k % 4) * UW + CONV_W - 1
                dve.tensor_tensor(u_lo[:, o:o + SEQ], u_pad[:, k * UW + CONV_W - 1:(k + 1) * UW],
                                  f(u_hi[:, o:o + SEQ]), ALU.subtract).then_inc(ulo_ready, 1)

            def taps_dve(p):
                return CONV_W - 1 - TAPS_POOL[p] - TAPS_PE[p]

            def taps_before(p):
                return 2 * sum(taps_dve(i) for i in range(p))

            def tap_ops(p, start, count):
                for q in range(start, min(start + count, 2 * taps_dve(p))):
                    c, tap = 2 * p + q % 2, TAPS_PE[p] + q // 2
                    if q < 2:
                        dve.wait_ge(pool_tap, pool_taps(c + 1))
                    else:
                        dve.wait_ge(dw_tap, taps_before(p) + q - 1)
                    dve.scalar_tensor_tensor(T(cv, c), u_pad[:, c * UW + tap:c * UW + tap + SEQ],
                                             col("w_dw", c * CONV_W + tap), T(cv, c), ALU.mult, ALU.add)\
                        .then_inc(dw_tap, 1)

            def add_pe_taps(p):
                unit_done(conv_step(p + 1)[1].stop - 1)
                dve.wait_ge(dw_tap, taps_before(p + 1))
                for c in (2 * p, 2 * p + 1):
                    dve.tensor_tensor(T(cv, c), T(cv, c), conv_bank(c)[:, :], ALU.add).then_inc(cv_ready, 1)

            for s in range(KD // 2 + 1):
                first, taps = conv_step(s)
                units = list(first) + list(taps)
                share = -(-2 * taps_dve(s - 1) // len(units)) if s else 0
                for q, n in enumerate(units):
                    if n > UNIT0["pw1"]:
                        lo_ahead(n)
                    if n in first:
                        k, e = 2 * s + q // 2, q % 2
                        unit_done(n)
                        if k >= 2:
                            dve.wait_ge(u_ready, k - 1)
                        dve.tensor_tensor(tmp[2 * (k % 2) + e][:, 0:SEQ], bank[q][:, :], r_pre[:, :], ALU.mult)\
                            .then_inc(out_read, 1)
                    if q == 0 and s >= 2:
                        add_pe_taps(s - 2)
                    if s:
                        tap_ops(s - 1, q * share, share)
                    if n in first and q % 2:
                        glu(2 * s + q // 2)
                    if n in first and q == 2:
                        operand_lo(2 * s)
                    if n in taps and n == taps.start and s < KD // 2:
                        operand_lo(2 * s + 1)
                if s == 0:
                    operand_lo(1)
            add_pe_taps(KD // 2 - 1)
            dve.wait_ge(mean_done, 1)
            for k in range(KD):
                dve.tensor_tensor(T(cv, k), T(cv, k), bank[4][:, :], ALU.subtract).then_inc(cen_ready, 1)
            lo_ahead(UNIT0["pw2"])
            take_r("ln_var")
            dve.wait_ge(spread_done, STAT_NO["ln_var"] + 1)
            for k in range(KD):
                dve.scalar_tensor_tensor(T(cv, k), T(cv, k), col("ln_g", k), bank[4][:, :], ALU.mult, ALU.mult)\
                    .then_inc(ln_ready, 1)
            for k in range(KD):
                dve.wait_ge(ln_silu, k + 1)
                x_lo(SPLIT0["conv"] + k, a_lo, a_hi, k, T(m, k))
            for k in range(KD):
                n = UNIT0["pw2"] + k
                if k:
                    lo_ahead(n)
                unit_done(n)
                dve.tensor_scalar(T(m, k), bank[k % 4][:, :], col("b_pw2", k), None, ALU.add).then_inc(out_read, 1)

            def post_norm(stat, gain, g0, h0, split=None, next_gain=None, ng0=0):
                take_r(stat)
                dve.wait_ge(spread_done, STAT_NO[stat] + 1)
                for k in range(KD):
                    scale = dve.scalar_tensor_tensor(T(m, k), T(m, k), col(gain, g0 + k), bank[4][:, :],
                                                     ALU.mult, ALU.mult)
                    if not split and k % 2:
                        scale.then_inc(out_scaled, 1)
                        continue
                    link(scale)
                    dve.tensor_tensor(T(h, k), T(h, k), T(m, k), ALU.add)\
                        .then_inc(h_ready if split else out_ready, 1)
                    if split and k:
                        x_lo(SPLIT0[split] + k - 1, a_lo, a_hi, k - 1, T(h, k - 1), col(next_gain, ng0 + k - 1))
                if split:
                    x_lo(SPLIT0[split] + KD - 1, a_lo, a_hi, KD - 1, T(h, KD - 1), col(next_gain, ng0 + KD - 1))

            post_norm("post0", "post", 0, H0["post0"], "ffpre0", "ffpre", 0)
            lo_ahead(UNIT0["ff1a0"])
            take_r("ffpre0")

            def feed_forward(layer):
                scaled(f"ffpre{layer}")
                for half in range(2):
                    c = "ab"[half]
                    n0, t0, x0 = UNIT0[f"ff1{c}{layer}"], TILE0[f"ff1{c}{layer}"], SPLIT0[f"hid{layer}{c}"]

                    def body(i):
                        for j in range(4):
                            if not isinstance(i, int) or j or half:
                                lo_ahead(n0 + j, i)
                            unit_done(n0 + j, i)
                            dve.scalar_tensor_tensor(tmp[j % 2][:, 0:SEQ], bank[j][:, :], 0.0, r_pre[:, :],
                                                     ALU.max, ALU.mult).then_inc(out_read, 1)
                            dve.wait_ge(hid_sq, 4 * i + (32 * layer + 16 * half + j + 1))
                            dve.wait_ge(xhi_ready, 4 * i + (x0 + j + 1))
                            dve.tensor_tensor(at(g_lo, 4 * i + j), tmp[2 + j % 2][:, 0:SEQ], f(at(g_hi, 4 * i + j)),
                                              ALU.subtract).then_inc(x_ready, 1)
                    body(0)
                    looped(dve, 4, body, 1)
                    name = f"ff2{c}{layer}"
                    n0 = UNIT0[name]

                    def first(i):
                        for j in range(2):
                            lo_ahead(n0 + 2 * j, i)
                            lo_ahead(n0 + 2 * j + 1, i)
                            unit_done(n0 + 2 * j + 1, i)
                            dve.tensor_copy(at(m, 2 * i + j), bank[j][:, :]).then_inc(out_read, 1)

                    if half == 0:
                        looped(dve, 4, first)
                        dve.wait_ge(out_read, TILE0[name] + 8)
                    else:
                        for k in range(KD):
                            lo_ahead(n0 + 2 * k)
                            lo_ahead(n0 + 2 * k + 1)
                            unit_done(n0 + 2 * k + 1)
                            dve.tensor_tensor(T(m, k), T(m, k), bank[k % 2][:, :], ALU.add).then_inc(out_read, 1)

            feed_forward(0)
            post_norm("ffpost0", "ffpost", 0, H0["ffpost0"], "kvpre", "kv_in", 0)
            lo_ahead(UNIT0["dkv"])
            for k in range(KD):
                x_lo(SPLIT0["pre1"] + k, b_lo, b_hi, k, T(h, k), col("pre", 8 + k))
            take_r("pre1")
            scaled("pre1")
            dests = [T(c_kv, 0), T(c_kv, 1), k_rope, T(c_q, 0), T(c_q, 1), T(c_q, 2)]
            for j in range(6):
                n = UNIT0["dkv"] + j
                if j:
                    lo_ahead(n)
                if j == 3:
                    for k in range(2):
                        x_lo(SPLIT0["ckv"] + k, a_lo, a_hi, k, T(c_kv, k), col("ckv_norm", k))
                unit_done(n)
                src = bank[j] if j < 3 else bank[DQ_BANK[j - 3]]
                dve.tensor_tensor(dests[j], src[:, :], r_pre[:, :], ALU.mult).then_inc(out_read, 1)
                if j == 4:
                    take_r("ckv")

            def rotate(x, no):
                dve.wait_ge(rope_sw, no + 1)
                if no:
                    dve.wait_ge(rope_done, no)
                dve.tensor_tensor(tmp[0][:, 0:SEQ], rope_bank(no)[:, :], cst_b[:, SIN:SIN + SEQ], ALU.mult)\
                    .then_inc(rope_t, 1)
                dve.tensor_tensor(tmp[1][:, 0:SEQ], x, cst_b[:, COS:COS + SEQ], ALU.mult).then_inc(rope_t, 1)
                dve.wait_ge(rope_t, 2 * no + 2)
                dve.tensor_tensor(x, tmp[0][:, 0:SEQ], tmp[1][:, 0:SEQ], ALU.add).then_inc(rope_done, 1)

            dve.wait_ge(cst2_landed, 16)
            rotate(k_rope, 0)
            for k in range(3):
                x_lo(SPLIT0["cq"] + k, a_lo, a_hi, 2 + k, T(c_q, k), col("cq_norm", k))
            scaled("ckv")
            for u in range(2):
                n = UNIT0["uk"] + u
                if u == 1:
                    take_r("cq")
                lo_ahead(n)
                unit_done(n)
                for j in range(4):
                    dve.tensor_tensor(T(k_nope, 4 * u + j), bank[j][:, :], r_post[:, :], ALU.mult)\
                        .then_inc(out_read, 1)
            scaled("cq")
            for u in range(6):
                n = UNIT0["uq"] + u
                lo_ahead(n)
                unit_done(n)
                for e in range(2):
                    j = 2 * u + e
                    dst = T(q_nope, j) if j < 8 else T(q_rope, j - 8)
                    dve.tensor_tensor(dst, bank[j % 4][:, :], r_pre[:, :], ALU.mult).then_inc(out_read, 1)
            lo_ahead(UNIT0["uv"])
            for t in range(4):
                rotate(T(q_rope, t), 1 + t)
            for u in range(2):
                n = UNIT0["uv"] + u
                if u:
                    for t in range(5):
                        dve.wait_ge(rope_hi, t + 1)
                        x, hi, lo_ = (k_rope, kr_hi, kr_lo) if t == 0 else \
                            (T(q_rope, t - 1), T(qr_hi, t - 1), T(qr_lo, t - 1))
                        dve.tensor_tensor(lo_, x, f(hi), ALU.subtract).then_inc(rope_split, 1)
                    lo_ahead(n)
                for b in range(NB):
                    c = 4 * STAT_NO["ckv"] + b
                    dve.wait_ge(v_hi_ready, NB * u + b + 1)
                    dve.scalar_tensor_tensor(v_lo(b)[:, u * SEQ:(u + 1) * SEQ], bank[4 * u + b][:, :],
                                             r_tok[:, c:c + 1],
                                             f(T(v_hi, b, MLA_H * V_DIM)[:, u * SEQ:(u + 1) * SEQ]),
                                             ALU.mult, ALU.subtract).then_inc(out_read, 1)

            def mla_max(i):
                nm = small[:, 32:36] if i % 2 == 0 else small[:, 40:44]
                for b in range(NB):
                    dve.wait_ge(mla_sc, NB * i + b + 1)
                    dve.tensor_reduce(nm[:, b:b + 1], bank[b][:, 0:(b + 1) * P], AX_X, ALU.max).then_inc(mla_mx, 1)
                dve.wait_ge(mla_mx, 5 * i + 4)
                dve.tensor_scalar(nm, nm, -MLA_SCALE, None, ALU.mult).then_inc(mla_mx, 1)

            lo_ahead(UNIT0["wo"])
            mla_max(0)
            for i in range(MLA_H):
                den = small[:, 36:40] if i % 2 == 0 else small[:, 44:48]
                dve.wait_ge(mla_exp, NB * (i + 1))
                link(dve.reciprocal(den, den))
                for b in range(NB):
                    o = P * b * (b + 1) // 2
                    x = prob[:, o:o + (b + 1) * P]
                    dve.tensor_scalar(x, x, den[:, b:b + 1], None, ALU.mult).then_inc(mla_pn, 1)
                if i + 1 < MLA_H:
                    mla_max(i + 1)
                for q, (bk, c0, c1) in enumerate(mla_parts):
                    dve.wait_ge(mla_ea, 3 * i + q + 1)
                    dve.tensor_tensor(pt_lo[:, c0:c1], bank[bk][:, 0:c1 - c0], f(pt_hi[:, c0:c1]), ALU.subtract)\
                        .then_inc(mla_ev, 1)
                x_lo(SPLIT0["mla"] + i, mo_lo, mo_hi, i, bank[4][:, :])
            for k in range(KD):
                n = UNIT0["wo"] + k
                if k:
                    lo_ahead(n)
                unit_done(n)
                dve.tensor_copy(T(m, k), bank[k % 4][:, :]).then_inc(out_read, 1)
            post_norm("post1", "post", 8, H0["post1"], "ffpre1", "ffpre", 8)
            lo_ahead(UNIT0["ff1a1"])
            take_r("ffpre1")
            feed_forward(1)
            post_norm("ffpost1", "ffpost", 8, None)


def _tiles(w):
    k, n = w.shape
    return w.reshape(k // P, P, n // P, P).transpose(2, 1, 0, 3).reshape(n // P, P, (k // P) * P)


def _pairs(w, kt, width):
    k, n = w.shape
    u = w.reshape(k // (kt * P), kt, P, n // width, width).transpose(3, 0, 2, 1, 4)
    return u.reshape(-1, P, kt * width)


def _stream(a):
    def pad(u):
        out = np.zeros((u.shape[0], P, UNIT), np.float32)
        out[:, :, :u.shape[2]] = u
        return out

    w_in = a["w_in"][0]
    qk = GLA_H * GLA_DK
    vw = GLA_H * GLA_DV
    o = np.cumsum([0, qk, qk, vw, vw, GLA_RANK, SWA_H * SWA_HD, SWA_KV * SWA_HD, SWA_KV * SWA_HD])
    gq, gk, gv, gr, glr, sq, sk, sv = (w_in[:, o[i]:o[i + 1]] for i in range(8))
    low = np.zeros((D, P), np.float32)
    low[:, :GLA_RANK] = glr
    sqp = sq.reshape(D, 2, 4, SWA_HD).transpose(0, 2, 1, 3).reshape(D, SWA_H * SWA_HD)
    units = [_tiles(sqp), _tiles(sk), _tiles(sv), _tiles(gq), _tiles(gk), _tiles(low), _tiles(gr), _pairs(gv, 2, 512)]
    w_out = a["w_out"][0]
    swa_rows = w_out[vw:].reshape(2, 4, SWA_HD, D).transpose(1, 0, 2, 3).reshape(SWA_H * SWA_HD, D)
    units.append(_tiles(np.concatenate([swa_rows, w_out[:vw]])))
    up = _tiles(a["w_up"][0])
    down = a["w_down"][0]
    both = np.stack([up[:UP_PAIRS], up[UP_PAIRS:]], 1)
    units += [both[:PAIRS_A].reshape(-1, P, UNIT), _pairs(down[:PAIRS_A * P], 2, 512)]
    units += [both[PAIRS_A:].reshape(-1, P, UNIT), _pairs(down[PAIRS_A * P:], 2, 512)]
    pw1 = _tiles(a["conv_w_pw1_2"][0])
    pw1 = np.stack([pw1[:KD], pw1[KD:]], 1).reshape(KD // 2, 4, P, UNIT)
    taps = a["conv_w_dw_2"][0].reshape(CONV_W, KD, P).transpose(1, 0, 2)
    diag = np.zeros((KD, CONV_W, P, P), np.float32)
    diag[:, :, np.arange(P), np.arange(P)] = taps
    for s in range(KD // 2 + 1):
        if s < KD // 2:
            units.append(pw1[s])
        if s:
            t = diag[2 * s - 2:2 * s, :TAPS_PE[s - 1]].reshape(-1, 8, P, P)
            units.append(t.transpose(0, 2, 1, 3).reshape(-1, P, UNIT))
    units.append(_tiles(a["conv_w_pw2_2"][0]))

    def ff(layer):
        w1 = _tiles(a["w_ff1_2"][layer])
        w2 = a["w_ff2_2"][layer]
        out = []
        for half in range(2):
            w = w2[half * 2048:(half + 1) * 2048].reshape(2, 1024, D)
            out += [w1[half * 16:(half + 1) * 16],
                    np.stack([_tiles(w[0]), _tiles(w[1])], 1).reshape(-1, P, UNIT)]
        return out
    units += ff(0)
    kr = a["kv_w_kr_2"]
    uq = a["mla_w_uq_2"][0].reshape(Q_RANK, MLA_H, NOPE + ROPE)
    units += [_tiles(a["kv_w_dkv_2"]), _tiles(np.concatenate([kr, kr], 1)), _tiles(a["mla_w_dq_2"][0])]
    units.append(_pairs(a["kv_w_uk_2"], 2, 512))
    uq2 = np.concatenate([uq[:, :, :NOPE].reshape(Q_RANK, -1), uq[:, :, NOPE:].reshape(Q_RANK, -1)], 1)
    units += [pad(_pairs(uq2, 3, 256)), _pairs(a["kv_w_uv_2"], 2, 512)]
    units.append(_tiles(a["mla_w_o_2"][0]))
    units += ff(1)
    out = np.concatenate(units)
    assert out.shape == (N_UNITS, P, UNIT)
    return out.reshape(N_UNITS * P, UNIT)


def _vectors(a):
    def c(v):
        return v.reshape(-1, P).T

    conv = np.concatenate([a["conv_w"][0], a["conv_b"]], 0)
    conv = conv.reshape(4, 2, UP_PAIRS, P).transpose(3, 2, 1, 0).reshape(P, -1)
    dw = a["conv_w_dw_2"][0].reshape(CONV_W, KD, P).transpose(2, 1, 0).reshape(P, -1)
    return np.concatenate([
        c(a["mix_norm"][0]), c(a["b_alpha"][0]), c(a["gla_norm"][0]), c(np.tile(a["q_norm"][0], 2)),
        c(np.tile(a["k_norm"][0], 2)), np.broadcast_to(a["sinks"], (P, SWA_H)), c(a["ffn_norm"][0]), conv,
        c(a["mix_pre_g_2"]), c(a["mix_post_g_2"]), c(a["ffn_pre_g_2"]), c(a["ffn_post_g_2"]), c(a["conv_b_pw1_2"][0]),
        dw, c(a["conv_b_dw_2"][0]), c(a["conv_ln_g_2"][0]), c(a["conv_ln_b_2"][0]), c(a["conv_b_pw2_2"][0]),
        c(a["kv_in_g_2"]), c(a["kv_norm_g_2"]), c(a["mla_q_norm_g_2"][0])], 1)


def _consts():
    i = np.arange(P)
    both = np.concatenate([np.eye(P), np.ones((P, P)), np.full((P, P), 1.0 / D), i[:, None] == (i[None, :] ^ 32),
                           (i[:, None] // 64) == np.arange(2)[None, :]], 1).astype(np.float32)
    one = np.zeros((P, N_CONST), np.float32)
    causal = (i[:, None] <= i[None, :]) & (i[:, None] // CHUNK == i[None, :] // CHUNK)
    one[:, CAUSAL:CAUSAL + SEQ] = np.tile(causal, (1, NB))
    one[:, RESET:RESET + SEQ] = (np.arange(SEQ) % CHUNK != 0)
    dist = WINDOW + i[:, None] - np.arange(2 * WINDOW)[None, :]
    seen = (dist >= 0) & (dist < WINDOW)
    d = np.where(seen, -dist, NEG).astype(np.float32)
    first = np.where(np.arange(2 * WINDOW)[None, :] >= WINDOW, d, np.float32(NEG))
    one[:, DIST:DIST + 768] = np.concatenate([first, d, d], 1)
    two = np.zeros((P, N_CONST), np.float32)
    half = ROPE // 2
    powers = np.arange(0, ROPE, 2, dtype=np.float32) / np.float32(ROPE)
    inv = (1.0 / (np.float32(10000.0) ** powers)).astype(np.float32)
    ang = np.arange(SEQ, dtype=np.float32)[:, None] * inv[None, :]
    cos, sin = np.cos(ang).T, np.sin(ang).T
    two[:, COS:COS + SEQ] = np.tile(cos, (P // half, 1))
    two[:, SIN:SIN + SEQ] = np.tile(np.concatenate([-sin, sin]), (2, 1))
    two[:, MASK_Q:MASK_Q + P] = i[None, :] < CHUNK
    two[:, MASK_K:MASK_K + P] = np.where(i[None, :] >= CHUNK, NEG, 0.0)
    return both, one, two


def kernel(**inputs):
    import concourse.bacc as _bacc
    from concourse import mybir as _mybir
    from concourse.bass_utils import run_bass_kernel_spmd as _run

    a = {k: np.asarray(v) for k, v in inputs.items()}
    both, one, two = _consts()
    w_alpha = np.zeros((P, 256), np.float32)
    w_alpha[:GLA_RANK] = a["w_alpha2"][0]
    arrays = {
        "in_xT": np.ascontiguousarray(a["x"][0].T), "in_stream": _stream(a), "in_vectors": _vectors(a),
        "in_w_alpha": w_alpha, "in_consts": both, "in_consts1": one, "in_consts2": two,
    }
    arrays = {k: np.ascontiguousarray(v) for k, v in arrays.items()}
    nc = _bacc.Bacc("TRN2", target_bir_lowering=False, num_devices=1)
    args = [nc.dram_tensor(k, v.shape, _mybir.dt.float32, kind="ExternalInput").ap() for k, v in arrays.items()]
    out = nc.dram_tensor("out_0", (D, SEQ), _mybir.dt.float32, kind="ExternalOutput").ap()
    program(nc, *args, out)
    r = _run(nc, [arrays], core_ids=[0])
    got = r.results[0]["out_0"]
    return np.ascontiguousarray(got.T)[None]
```
